# Optimizing a Trainium2 kernel written in Bass

```python
import math
import jax, jax.numpy as jnp
from jax import lax
import numpy as np

D_MODEL = 1024
BATCH = 1
SEQ = 512
DEPTH = 1
DEC_BATCH = 8
DEC_SEQ = 4
PAST_LEN = 2048
PAGE_SIZE = 128

HEAD_DIM = 64
EPS = 1e-6
ROPE_THETA = 10000.0
SSM_WIDTH = 512
SSM_GROUP = 16
SSM_GROUPS = SSM_WIDTH // SSM_GROUP
SSM_STATE = 64
DT_MIN = 1e-3
DT_MAX = 1e-1
SWA_Q_HEADS = 4
SWA_KV_HEADS = 2
SWA_REP = SWA_Q_HEADS // SWA_KV_HEADS
SWA_WIDTH = SWA_Q_HEADS * HEAD_DIM
SWA_KV_WIDTH = SWA_KV_HEADS * HEAD_DIM
WINDOW = 128
MEM_TOKENS = 256
MEM_HEADS = 4
MEM_WIDTH = MEM_HEADS * HEAD_DIM
MIX_WIDTH = SSM_WIDTH + SWA_WIDTH + MEM_WIDTH
IN_WIDTH = SSM_WIDTH + SWA_WIDTH + 2 * SWA_KV_WIDTH + MEM_WIDTH
SPLITS = (SSM_WIDTH, SSM_WIDTH + SWA_WIDTH, SSM_WIDTH + SWA_WIDTH + SWA_KV_WIDTH,
          SSM_WIDTH + SWA_WIDTH + 2 * SWA_KV_WIDTH)
PEER_HEADS = 8
PEER_KEYS = 128
PEER_EXPERTS = PEER_KEYS * PEER_KEYS
PEER_TOPK = 16
PEER_QDIM = 256
PEER_HALF = PEER_QDIM // 2
PEER_CHUNK = 256

kernel_name = 'hymba_s5_swa_sink_memx_peer_step'

def rms_norm(x, g):
    xf = x.astype(jnp.float32)
    y = xf * lax.rsqrt(jnp.mean(xf * xf, axis=-1, keepdims=True) + EPS)
    return (y * g.astype(jnp.float32)).astype(x.dtype)

def rope(x, pos):
    half = x.shape[-1] // 2
    inv = ROPE_THETA ** (-jnp.arange(half, dtype=jnp.float32) / half)
    ang = pos.astype(jnp.float32)[:, None] * inv[None, :]
    cos = jnp.cos(ang)[:, None, :]
    sin = jnp.sin(ang)[:, None, :]
    xf = x.astype(jnp.float32)
    x1, x2 = xf[..., :half], xf[..., half:]
    return jnp.concatenate([x1 * cos - x2 * sin, x2 * cos + x1 * sin], axis=-1).astype(x.dtype)

def _complex_affine_combine(left, right):
    ar1, ai1, br1, bi1 = left
    ar2, ai2, br2, bi2 = right
    return (ar2 * ar1 - ai2 * ai1, ar2 * ai1 + ai2 * ar1,
            ar2 * br1 - ai2 * bi1 + br2, ar2 * bi1 + ai2 * br1 + bi2)

def s5_mixer(u, s0_re, s0_im, log_dt, a_re, a_im, b_re, b_im, c_re, c_im, d_skip, w_glu, b_glu):
    f32 = jnp.float32
    B, T, _ = u.shape
    uf = u.astype(f32).reshape(B, T, SSM_GROUPS, SSM_GROUP)
    dt = jnp.exp(log_dt.astype(f32))
    ar, ai = a_re.astype(f32), a_im.astype(f32)
    mag = jnp.exp(ar * dt)
    lam_re = mag * jnp.cos(ai * dt)
    lam_im = mag * jnp.sin(ai * dt)
    den = ar * ar + ai * ai
    z_re = ((lam_re - 1.0) * ar + lam_im * ai) / den
    z_im = (lam_im * ar - (lam_re - 1.0) * ai) / den
    br, bi = b_re.astype(f32), b_im.astype(f32)
    bb_re = z_re[..., None] * br - z_im[..., None] * bi
    bb_im = z_re[..., None] * bi + z_im[..., None] * br
    bu_re = jnp.einsum('gnc,btgc->btgn', bb_re, uf)
    bu_im = jnp.einsum('gnc,btgc->btgn', bb_im, uf)
    s0r, s0i = s0_re.astype(f32), s0_im.astype(f32)
    bu_re = bu_re.at[:, 0].add(lam_re * s0r - lam_im * s0i)
    bu_im = bu_im.at[:, 0].add(lam_re * s0i + lam_im * s0r)
    lr = jnp.broadcast_to(lam_re, bu_re.shape)
    li = jnp.broadcast_to(lam_im, bu_im.shape)
    _, _, s_re, s_im = lax.associative_scan(_complex_affine_combine, (lr, li, bu_re, bu_im), axis=1)
    y = (jnp.einsum('gcn,btgn->btgc', c_re.astype(f32), s_re)
         - jnp.einsum('gcn,btgn->btgc', c_im.astype(f32), s_im)
         + d_skip.astype(f32) * uf)
    y = jax.nn.gelu(y.reshape(B, T, SSM_WIDTH), approximate=False)
    y = y * jax.nn.sigmoid(y @ w_glu.astype(f32) + b_glu.astype(f32))
    return y.astype(u.dtype), s_re[:, -1], s_im[:, -1]

def sink_attention(q, k, v, qpos, kpos, sinks):
    s = jnp.einsum('...qkrd,...skd->...krqs', q, k, preferred_element_type=jnp.float32) * HEAD_DIM ** -0.5
    diff = qpos[..., :, None] - kpos[..., None, :]
    valid = (diff >= 0) & (diff < WINDOW) & (kpos[..., None, :] >= 0)
    s = jnp.where(valid[..., None, None, :, :], s, -jnp.inf)
    sk = sinks.astype(jnp.float32).reshape(SWA_KV_HEADS, SWA_REP)[:, :, None, None]
    m = jnp.maximum(jnp.max(s, axis=-1, keepdims=True), sk)
    p = jnp.exp(s - m)
    p = p / (jnp.sum(p, axis=-1, keepdims=True) + jnp.exp(sk - m))
    return jnp.einsum('...krqs,...skd->...qkrd', p.astype(v.dtype), v)

def swa_prompt(q, k, v, sinks):
    B, T = q.shape[0], q.shape[1]
    nb = T // WINDOW
    qb = q.reshape(B, nb, WINDOW, SWA_KV_HEADS, SWA_REP, HEAD_DIM)
    kb = k.reshape(B, nb, WINDOW, SWA_KV_HEADS, HEAD_DIM)
    vb = v.reshape(B, nb, WINDOW, SWA_KV_HEADS, HEAD_DIM)
    padw = ((0, 0), (1, 0), (0, 0), (0, 0), (0, 0))
    kk = jnp.concatenate([jnp.pad(kb, padw)[:, :-1], kb], axis=2)
    vv = jnp.concatenate([jnp.pad(vb, padw)[:, :-1], vb], axis=2)
    pos = jnp.arange(T, dtype=jnp.int32).reshape(nb, WINDOW)
    kpos = jnp.concatenate([pos - WINDOW, pos], axis=1)
    o = sink_attention(qb, kk, vv, pos, kpos, sinks)
    return o.reshape(B, T, SWA_WIDTH)

def memory_kv(mem, mem_norm_g, w_mem_kv, mem_k_norm):
    B, M, _ = mem.shape
    kv = (rms_norm(mem, mem_norm_g) @ w_mem_kv).reshape(B, M, 2, MEM_HEADS, HEAD_DIM)
    return rms_norm(kv[:, :, 0], mem_k_norm), kv[:, :, 1]

def memory_attention(q, k, v):
    s = jnp.einsum('bthd,bmhd->bhtm', q, k, preferred_element_type=jnp.float32) * HEAD_DIM ** -0.5
    p = jax.nn.softmax(s, axis=-1).astype(v.dtype)
    o = jnp.einsum('bhtm,bmhd->bthd', p, v)
    return o.reshape(o.shape[0], o.shape[1], MEM_WIDTH)

def peer_ffn(xn, wq, k1, k2, u_tab, v_tab):
    shp = xn.shape
    x2 = xn.reshape(-1, D_MODEL)
    n = x2.shape[0]
    c = PEER_CHUNK
    pad = (-n) % c
    xp = jnp.pad(x2, ((0, pad), (0, 0))).reshape(-1, c, D_MODEL)

    def block(xc):
        q = (xc @ wq).reshape(c, PEER_HEADS, 2, PEER_HALF)
        s1 = jnp.einsum('chd,kd->chk', q[:, :, 0], k1, preferred_element_type=jnp.float32)
        s2 = jnp.einsum('chd,kd->chk', q[:, :, 1], k2, preferred_element_type=jnp.float32)
        v1, i1 = lax.top_k(s1, PEER_TOPK)
        v2, i2 = lax.top_k(s2, PEER_TOPK)
        cand = (v1[..., :, None] + v2[..., None, :]).reshape(c, PEER_HEADS, PEER_TOPK * PEER_TOPK)
        sc, ci = lax.top_k(cand, PEER_TOPK)
        ia = jnp.take_along_axis(i1, ci // PEER_TOPK, axis=-1)
        ib = jnp.take_along_axis(i2, ci % PEER_TOPK, axis=-1)
        expert = ia * PEER_KEYS + ib
        gate = jax.nn.softmax(sc, axis=-1)
        a = jnp.einsum('chkd,cd->chk', u_tab[expert], xc, preferred_element_type=jnp.float32)
        wgt = (gate * jax.nn.gelu(a, approximate=False)).astype(xc.dtype)
        return jnp.einsum('chk,chkd->cd', wgt, v_tab[expert])

    y = lax.map(block, xp).reshape(-1, D_MODEL)[:n]
    return y.reshape(shp)

def hybrid_layer(x, s0_re, s0_im, win_k, win_v, mem_k, mem_v, start,
                 norm1_g, w_in, log_dt, a_re, a_im, b_re, b_im, c_re, c_im, d_skip, w_glu, b_glu,
                 swa_q_norm, swa_k_norm, swa_sinks, mem_q_norm, w_out, norm2_g,
                 peer_wq, peer_k1, peer_k2, peer_u, peer_v):
    B, T, _ = x.shape
    pos = start + jnp.arange(T, dtype=jnp.int32)
    xn = rms_norm(x, norm1_g)
    u, q, k, v, qm = jnp.split(xn @ w_in, SPLITS, axis=-1)
    o_ssm, s_re, s_im = s5_mixer(u, s0_re, s0_im, log_dt, a_re, a_im, b_re, b_im,
                                 c_re, c_im, d_skip, w_glu, b_glu)
    q = rope(rms_norm(q.reshape(B, T, SWA_Q_HEADS, HEAD_DIM), swa_q_norm), pos)
    k = rope(rms_norm(k.reshape(B, T, SWA_KV_HEADS, HEAD_DIM), swa_k_norm), pos)
    v = v.reshape(B, T, SWA_KV_HEADS, HEAD_DIM)
    q = q.reshape(B, T, SWA_KV_HEADS, SWA_REP, HEAD_DIM)
    w = min(WINDOW, PAST_LEN)
    if win_k is None:
        o_swa = swa_prompt(q, k, v, swa_sinks)
        new_k, new_v = k[:, T - w:], v[:, T - w:]
    else:
        k_all = jnp.concatenate([win_k.astype(k.dtype), k], axis=1)
        v_all = jnp.concatenate([win_v.astype(v.dtype), v], axis=1)
        kpos = jnp.concatenate([start - w + jnp.arange(w, dtype=jnp.int32), pos])
        o_swa = sink_attention(q, k_all, v_all, pos, kpos, swa_sinks).reshape(B, T, SWA_WIDTH)
        new_k, new_v = k_all[:, -w:], v_all[:, -w:]
    qm = rms_norm(qm.reshape(B, T, MEM_HEADS, HEAD_DIM), mem_q_norm)
    o_mem = memory_attention(qm, mem_k.astype(qm.dtype), mem_v.astype(qm.dtype))
    mixed = jnp.concatenate([o_ssm, o_swa.astype(x.dtype), o_mem.astype(x.dtype)], axis=-1)
    x = x + mixed @ w_out
    x = x + peer_ffn(rms_norm(x, norm2_g), peer_wq, peer_k1, peer_k2, peer_u, peer_v)
    return x, s_re, s_im, new_k, new_v

def setup_inputs(seed: int = 0) -> dict:
    key = jax.random.key(seed)
    ks = iter(jax.random.split(key, 48))
    f32 = jnp.float32

    def nrm(shape, scale):
        return scale * jax.random.normal(next(ks), shape, f32)

    def gain(shape):
        return 1.0 + 0.05 * jax.random.normal(next(ks), shape, f32)

    L = DEPTH
    w = min(WINDOW, PAST_LEN)
    G, N, C = SSM_GROUPS, SSM_STATE, SSM_GROUP
    n_idx = jnp.arange(N, dtype=f32)
    return {
        'x_prompt': nrm((BATCH, SEQ, D_MODEL), 1.0),
        'x_sample': nrm((DEC_BATCH, DEC_SEQ, D_MODEL), 1.0),
        'state_ssm_re': nrm((L, DEC_BATCH, G, N), 0.1),
        'state_ssm_im': nrm((L, DEC_BATCH, G, N), 0.1),
        'cache_win_k': nrm((L, DEC_BATCH, w, SWA_KV_HEADS, HEAD_DIM), 1.0),
        'cache_win_v': nrm((L, DEC_BATCH, w, SWA_KV_HEADS, HEAD_DIM), 1.0),
        'cache_mem_k': nrm((L, DEC_BATCH, MEM_TOKENS, MEM_HEADS, HEAD_DIM), 1.0),
        'cache_mem_v': nrm((L, DEC_BATCH, MEM_TOKENS, MEM_HEADS, HEAD_DIM), 1.0),
        'mem_prompt': nrm((BATCH, MEM_TOKENS, D_MODEL), 1.0),
        'norm1_g': gain((L, D_MODEL)),
        'w_in': nrm((L, D_MODEL, IN_WIDTH), D_MODEL ** -0.5),
        'ssm_log_dt': jax.random.uniform(next(ks), (L, G, N), f32, math.log(DT_MIN), math.log(DT_MAX)),
        'ssm_a_re': -0.5 * jnp.exp(0.02 * jax.random.normal(next(ks), (L, G, N), f32)),
        'ssm_a_im': math.pi * n_idx + 0.01 * jax.random.normal(next(ks), (L, G, N), f32),
        'ssm_b_re': nrm((L, G, N, C), C ** -0.5),
        'ssm_b_im': nrm((L, G, N, C), C ** -0.5),
        'ssm_c_re': nrm((L, G, C, N), 0.5),
        'ssm_c_im': nrm((L, G, C, N), 0.5),
        'ssm_d': nrm((L, G, C), 1.0),
        'w_glu': nrm((L, SSM_WIDTH, SSM_WIDTH), SSM_WIDTH ** -0.5),
        'b_glu': nrm((L, SSM_WIDTH), 0.02),
        'swa_q_norm': gain((L, HEAD_DIM)),
        'swa_k_norm': gain((L, HEAD_DIM)),
        'swa_sinks': nrm((L, SWA_Q_HEADS), 0.5),
        'mem_norm_g': gain((L, D_MODEL)),
        'w_mem_kv': nrm((L, D_MODEL, 2 * MEM_WIDTH), D_MODEL ** -0.5),
        'mem_q_norm': gain((L, HEAD_DIM)),
        'mem_k_norm': gain((L, HEAD_DIM)),
        'w_out': nrm((L, MIX_WIDTH, D_MODEL), MIX_WIDTH ** -0.5),
        'norm2_g': gain((L, D_MODEL)),
        'peer_wq': nrm((L, D_MODEL, PEER_HEADS * PEER_QDIM), D_MODEL ** -0.5),
        'peer_k1': nrm((L, PEER_KEYS, PEER_HALF), PEER_HALF ** -0.5),
        'peer_k2': nrm((L, PEER_KEYS, PEER_HALF), PEER_HALF ** -0.5),
        'peer_u': nrm((L, PEER_EXPERTS, D_MODEL), D_MODEL ** -0.5),
        'peer_v': nrm((L, PEER_EXPERTS, D_MODEL), PEER_HEADS ** -0.5),
    }

def reference(x_prompt, x_sample, state_ssm_re, state_ssm_im, cache_win_k, cache_win_v,
              cache_mem_k, cache_mem_v, mem_prompt, norm1_g, w_in, ssm_log_dt, ssm_a_re, ssm_a_im,
              ssm_b_re, ssm_b_im, ssm_c_re, ssm_c_im, ssm_d, w_glu, b_glu, swa_q_norm, swa_k_norm,
              swa_sinks, mem_norm_g, w_mem_kv, mem_q_norm, mem_k_norm, w_out, norm2_g,
              peer_wq, peer_k1, peer_k2, peer_u, peer_v):
    y_p, y_s = x_prompt, x_sample
    p_sr, p_si, p_wk, p_wv, p_mk, p_mv = [], [], [], [], [], []
    s_sr, s_si, s_wk, s_wv = [], [], [], []
    for l in range(DEPTH):
        shared = (norm1_g[l], w_in[l], ssm_log_dt[l], ssm_a_re[l], ssm_a_im[l], ssm_b_re[l],
                  ssm_b_im[l], ssm_c_re[l], ssm_c_im[l], ssm_d[l], w_glu[l], b_glu[l],
                  swa_q_norm[l], swa_k_norm[l], swa_sinks[l], mem_q_norm[l], w_out[l], norm2_g[l],
                  peer_wq[l], peer_k1[l], peer_k2[l], peer_u[l], peer_v[l])
        mk, mv = memory_kv(mem_prompt, mem_norm_g[l], w_mem_kv[l], mem_k_norm[l])
        zeros = jnp.zeros((y_p.shape[0], SSM_GROUPS, SSM_STATE), jnp.float32)
        y_p, sr, si, wk, wv = hybrid_layer(y_p, zeros, zeros, None, None, mk, mv, 0, *shared)
        p_sr.append(sr); p_si.append(si); p_wk.append(wk); p_wv.append(wv)
        p_mk.append(mk); p_mv.append(mv)
        y_s, sr, si, wk, wv = hybrid_layer(y_s, state_ssm_re[l], state_ssm_im[l], cache_win_k[l],
                                           cache_win_v[l], cache_mem_k[l], cache_mem_v[l],
                                           PAST_LEN, *shared)
        s_sr.append(sr); s_si.append(si); s_wk.append(wk); s_wv.append(wv)
    return (y_p, y_s,
            jnp.stack(p_sr), jnp.stack(p_si), jnp.stack(p_wk), jnp.stack(p_wv),
            jnp.stack(p_mk), jnp.stack(p_mv),
            jnp.stack(s_sr), jnp.stack(s_si), jnp.stack(s_wk), jnp.stack(s_wv))


_drawn_inputs = setup_inputs


def setup_inputs(seed=0):
    import zlib

    import numpy as np

    out = dict(_drawn_inputs(seed))
    spreads = {}
    factors = {'ssm_a_re': 18.47,
     'b_glu': 16.62,
     'swa_q_norm': 5.37,
     'swa_sinks': 29.991,
     'mem_q_norm': 6.211}
    for name, (base, spread) in spreads.items():
        noise = np.random.default_rng([zlib.crc32(name.encode()), seed]).standard_normal(out[name].shape)
        drawn = base * np.exp(spread * noise) if base else spread * noise
        out[name] = __import__('jax').numpy.asarray(drawn.astype(out[name].dtype))
    for name, factor in factors.items():
        out[name] = (out[name] * factor).astype(out[name].dtype)
    return out
```

```python
from contextlib import ExitStack

import numpy as np

import concourse.bass as bass
from concourse import mybir
from concourse.alu_op_type import AluOpType as ALU

ACT = mybir.ActivationFunctionType
AX = mybir.AxisListType
F32 = mybir.dt.float32
BF16 = mybir.dt.bfloat16
U32 = mybir.dt.uint32

P = 128
D = 1024
KD = D // P
SEQ, NSEQ, DSEQ = 512, 8, 4
NSMP = NSEQ * DSEQ
T = SEQ + NSMP
NT = 5
ROWS = [P, P, P, P, NSMP]
HD = 64
EPS = 1e-6
WIN = 128
MEM = 256
G, N, C = 32, 64, 16
GP = G // 2
CH = 8
NJ = SEQ // CH
COLS = NJ + NSEQ
ROWH, ROWK = 6, 10
ZW = 768
UW = 512
PH, PK, TOPK = 8, 128, 16
CAND = 80
BIG = 3.0e38
SLOTS = PH * TOPK


class Chain:

    def __init__(self, eng, sem):
        self.eng, self.sem, self.n = eng, sem, 0

    def __call__(self, ins):
        self.n += 1
        ins.then_inc(self.sem, 1)
        self.eng.wait_ge(self.sem, self.n)


def widen(ap, axis, n):
    v = ap.unsqueeze(axis)
    shape = list(v.shape)
    shape[axis] = n
    return v.broadcast_to(shape)


class Stage:

    def __init__(self, nc, name, side="left"):
        self.nc, self.name, self.side, self.ctx = nc, name, side, ExitStack()

    def __enter__(self):
        self.ctx.__enter__()
        return self

    def __exit__(self, *a):
        return self.ctx.__exit__(*a)

    def sb(self, name, shape, dt=F32):
        return self.ctx.enter_context(self.nc.sbuf_tensor(f"sb_{self.name}_{name}", shape, dt, side=self.side))

    def ps(self, name, shape, dt=F32):
        return self.ctx.enter_context(self.nc.psum_tensor(f"sb_{self.name}_{name}", shape, dt))

    def sem(self, name):
        return self.ctx.enter_context(self.nc.semaphore(f"sb_{self.name}_{name}"))

    def block(self):
        return self.nc.Block()


def project(nc, d, K):
    with Stage(nc, "proj") as S:
        xT = S.sb("xT", [P, KD, T])
        w_in = S.sb("w_in", [P, KD, UW + ZW])
        memT = S.sb("memT", [P, KD, MEM])
        w_mem = S.sb("w_mem", [P, KD, 512])
        mem_tok = S.sb("mem_tok", [P, 2, D])
        g1 = S.sb("g1", [P, 2, KD])
        gains = S.sb("gains", [P, ROWK + 4, HD])
        rope = S.sb("rope", [P, NT, 2, HD])
        square = S.sb("square", [P, 2, D])
        NJOB = NT + 2
        ss = S.sb("ss", [P, NJOB])
        rstd = S.sb("rstd", [P, NJOB])
        z = S.sb("z", [P, 2, ZW])
        u = S.sb("u", [P, 2, UW])
        sq = S.sb("sq", [P, ROWK, HD])
        hs = S.sb("hs", [P, ROWK])
        hr = S.sb("hr", [P, ROWK])
        rc = S.sb("rc", [P, ROWH, HD])
        rs = S.sb("rs", [P, ROWH, HD])
        zn = S.sb("zn", [P, NJOB, ROWK * HD])
        pz = [S.ps(f"pz{i}", [P, 3 * 512]) for i in range(2)]
        pt = S.ps("pt", [P, 2 * 512])

        s_small = S.sem("small_landed")
        s_xtok = S.sem("xtok_landed")
        s_k = [S.sem(f"k{k}_landed") for k in range(KD)]
        s_m = [S.sem(f"m{k}_landed") for k in range(2)]
        s_gain = S.sem("gained")
        s_ss = S.sem("squares")
        s_std = S.sem("std")
        s_rstd = S.sem("rstd")
        s_mm = S.sem("projected")
        s_z = S.sem("evacuated")
        s_u = [S.sem(f"u_stored{i}") for i in range(2)]
        s_hs = S.sem("head_squares")
        s_hq = S.sem("head_std")
        s_zn = S.sem("normed")
        s_t = S.sem("transposed")
        s_te = S.sem("transposes_out")
        s_out = S.sem("stored")
        s_v = S.sem("dve_chain")
        s_init = S.sem("init")

        rows = ROWS + [P, P]

        with S.block() as block:
            @block.sync
            def _(sp):
                sp.dma_start(g1[:, :, :], d["g1T"]).then_inc(s_small, 16)
                for k in range(KD):
                    sp.dma_start(xT[:, k, :], d["xT"][:, k, :]).then_inc(s_k[k], 16)
                    sp.dma_start(w_in[:, k, :], d["w_in"][:, k, :]).then_inc(s_k[k], 16)
                sp.dma_start(gains[:, :, :], d["gains"]).then_inc(s_small, 16)
                sp.dma_start(rope[:, :, :, :], d["rope"]).then_inc(s_small, 16)
                sp.dma_start(memT[:, :, :], d["memT"]).then_inc(s_m[0], 16)
                sp.dma_start(w_mem[:, :, :], d["w_mem"]).then_inc(s_m[1], 16)
                for j in range(NT):
                    sp.wait_ge(s_z, j + 1)
                    r = rows[j]
                    sp.dma_start(d["u_scratch"][j * P:j * P + r, :], u[:r, j % 2, :]).then_inc(s_u[j % 2], 16)
                sp.wait_ge(s_zn, NT)
                sp.dma_start(d["p_win_k"], zn[:, 3, 256:384]).then_inc(s_out, 16)
                sp.dma_start(d["p_win_v"], K.v[:, 3, :]).then_inc(s_out, 16)
                for b in range(NSEQ):
                    q = slice(b * DSEQ, (b + 1) * DSEQ)
                    sp.dma_start(d["s_win_k"][b, WIN - DSEQ:, :], zn[q, 4, 256:384]).then_inc(s_out, 16)
                    sp.dma_start(d["s_win_v"][b, WIN - DSEQ:, :], K.v[q, 4, :]).then_inc(s_out, 16)
                sp.dma_start(d["s_win_k"][:, 0:WIN - DSEQ, :], d["cache_k"][:, DSEQ:, :]).then_inc(s_out, 16)
                sp.dma_start(d["s_win_v"][:, 0:WIN - DSEQ, :], d["cache_v"][:, DSEQ:, :]).then_inc(s_out, 16)
                sp.wait_ge(s_zn, NJOB)
                for m in range(2):
                    sp.dma_start(d["p_mem_k"][m * P:(m + 1) * P, :], zn[:, NT + m, 0:256]).then_inc(s_out, 16)
                    sp.dma_start(d["p_mem_v"][m * P:(m + 1) * P, :], K.mv[:, m, :]).then_inc(s_out, 16)
                for i in range(2):
                    sp.wait_ge(s_u[i], 16 * (3 - i))
                sp.wait_ge(s_out, 16 * (2 + 2 * NSEQ + 2 + 4))

            @block.gpsimd
            def _(pool):
                pool.dma_start(K.x[:, 0:4, :], d["x_tok"][0:SEQ, :].rearrange("(i p) n -> p i n", p=P)).then_inc(s_xtok, 16)
                pool.dma_start(K.x[0:NSMP, 4, :], d["x_tok"][SEQ:T, :]).then_inc(s_xtok, 16)
                pool.dma_start(mem_tok[:, :, :], d["mem_tok"]).then_inc(s_xtok, 16)
                pool.dma_start(K.ident[:, :], d["ident"]).then_inc(s_xtok, 16)

            @block.scalar
            def _(act):
                act.wait_ge(s_xtok, 64)
                act.wait_ge(s_init, 1)
                for j in range(NJOB):
                    r = rows[j]
                    src = K.x[:r, j, :] if j < NT else mem_tok[:, j - NT, :]
                    if j >= 2:
                        act.wait_ge(s_ss, j - 1)
                    act.activation(square[:r, j % 2, :], src, ACT.Square, accum_out=ss[:r, j:j + 1]).then_inc(s_ss, 1)
                act.wait_ge(s_ss, NJOB)
                act.activation(rstd[:, :], ss[:, :], ACT.Sqrt, bias=K.eps[:, 0:1], scale=1.0 / D).then_inc(s_std, 1)
                act.wait_ge(s_rstd, 1)

                def out_of_transposes(j):
                    act.wait_ge(s_t, j + 1)
                    r = rows[j]
                    if j < NT:
                        act.activation(K.qkT[:, :, j * P:j * P + r], pt[:, 0:5 * P].rearrange("p (c t) -> p c t", t=P)[:, :, :r],
                                       ACT.Copy).then_inc(s_te, 1)
                    else:
                        m = j - NT
                        act.activation(K.mkT[:, :, m * P:(m + 1) * P], pt[:, 0:2 * P].rearrange("p (c t) -> p c t", t=P),
                                       ACT.Copy).then_inc(s_te, 1)

                for j in range(NJOB):
                    r = rows[j]
                    act.wait_ge(s_mm, j + 1)
                    if j >= 2:
                        act.wait_ge(s_zn, j - 1)
                        if j < NT:
                            act.wait_ge(s_u[j % 2], 16 * (j // 2))
                    if j < NT:
                        act.activation(u[:r, j % 2, :], pz[j % 2][:r, 0:UW], ACT.Copy, scale=rstd[:r, j:j + 1])
                        act.activation(K.v[:r, j, :], pz[j % 2][:r, UW + 640:UW + ZW], ACT.Copy, scale=rstd[:r, j:j + 1])
                        act.activation(z[:r, j % 2, 0:640], pz[j % 2][:r, UW:UW + 640], ACT.Copy,
                                       scale=rstd[:r, j:j + 1]).then_inc(s_z, 1)
                    else:
                        act.activation(K.mv[:, j - NT, :], pz[j % 2][:, 256:512], ACT.Copy, scale=rstd[:, j:j + 1])
                        act.activation(z[:, j % 2, 0:256], pz[j % 2][:, 0:256], ACT.Copy,
                                       scale=rstd[:, j:j + 1]).then_inc(s_z, 1)
                    nh = ROWK if j < NT else 4
                    act.wait_ge(s_hs, j + 1)
                    act.activation(hr[:r, :nh], hs[:r, :nh], ACT.Sqrt, bias=K.eps[:r, 0:1], scale=1.0 / HD).then_inc(s_hq, 1)
                    if j >= 1:
                        out_of_transposes(j - 1)
                out_of_transposes(NJOB - 1)

            @block.vector
            def _(dve):
                step = Chain(dve, s_v)
                dve.memset(ss[:, :], 1.0)
                dve.memset(K.eps[:, :], EPS).then_inc(s_init, 1)
                dve.wait_ge(s_small, 48)
                for k in range(KD):
                    dve.wait_ge(s_k[k], 32)
                    dve.tensor_scalar(xT[:, k, :], xT[:, k, :], g1[:, 0, k:k + 1], None, ALU.mult).then_inc(s_gain, 1)
                dve.wait_ge(s_std, 1)
                dve.reciprocal(rstd[:, :], rstd[:, :]).then_inc(s_rstd, 1)
                dve.wait_ge(s_m[0], 16)
                for k in range(KD):
                    dve.tensor_scalar(memT[:, k, :], memT[:, k, :], g1[:, 1, k:k + 1], None, ALU.mult).then_inc(s_gain, 1)
                for j in range(NJOB):
                    r = rows[j]
                    nh = ROWK if j < NT else 4
                    g0 = 0 if j < NT else ROWK
                    zj = z[:r, j % 2, 0:nh * HD].rearrange("p (h c) -> p h c", c=HD)
                    out = zn[:r, j, 0:nh * HD].rearrange("p (h c) -> p h c", c=HD)
                    dve.wait_ge(s_z, j + 1)
                    step(dve.tensor_tensor(sq[:r, :nh, :], zj, zj, ALU.mult))
                    dve.tensor_reduce(hs[:r, :nh], sq[:r, :nh, :], AX.X, ALU.add).then_inc(s_hs, 1)
                    dve.wait_ge(s_hq, j + 1)
                    step(dve.reciprocal(hr[:r, :nh], hr[:r, :nh]))
                    step(dve.tensor_tensor(out, zj, widen(hr[:r, :nh], 2, HD), ALU.mult))
                    last = dve.tensor_tensor(out, out, gains[:r, g0:g0 + nh, :], ALU.mult)
                    if j < NT:
                        step(last)
                        rot = out[:, 0:ROWH, :]
                        dve.tensor_tensor(rc[:r, :, :], rot, widen(rope[:r, j, 0, :], 1, ROWH), ALU.mult)
                        step(dve.tensor_tensor(rs[:r, :, :], rot, widen(rope[:r, j, 1, :], 1, ROWH), ALU.mult))
                        h = HD // 2
                        dve.tensor_tensor(rot[:, :, 0:h], rc[:r, :, 0:h], rs[:r, :, h:HD], ALU.subtract)
                        last = dve.tensor_tensor(rot[:, :, h:HD], rc[:r, :, h:HD], rs[:r, :, 0:h], ALU.add)
                    last.then_inc(s_zn, 1)

            @block.tensor
            def _(pe):
                def transposes(j):
                    r = rows[j]
                    pe.wait_ge(s_zn, j + 1)
                    if j >= 1:
                        pe.wait_ge(s_te, j)
                    for c in range(5 if j < NT else 2):
                        mm = pe.transpose(pt[:, c * P:c * P + r], zn[:r, j, c * P:(c + 1) * P], K.ident[:r, :r])
                    mm.then_inc(s_t, 1)

                pe.wait_ge(s_xtok, 64)
                for j in range(NJOB):
                    r = rows[j]
                    if j >= 2:
                        pe.wait_ge(s_z, j - 1)
                    if j >= NT:
                        pe.wait_ge(s_m[1], 16)
                        pe.wait_ge(s_gain, 2 * KD)
                    for k in range(KD):
                        if j == 0:
                            pe.wait_ge(s_k[k], 32)
                            pe.wait_ge(s_gain, k + 1)
                        if j < NT:
                            for c in range(0, UW + ZW, 512):
                                w = min(512, UW + ZW - c)
                                mm = pe.matmul(pz[j % 2][:r, c:c + w], xT[:, k, j * P:j * P + r], w_in[:, k, c:c + w],
                                               start=(k == 0), stop=(k == KD - 1))
                        else:
                            m = j - NT
                            mm = pe.matmul(pz[j % 2][:, 0:512], memT[:, k, m * P:(m + 1) * P], w_mem[:, k, :],
                                           start=(k == 0), stop=(k == KD - 1))
                    mm.then_inc(s_mm, 1)
                    if j >= 1:
                        transposes(j - 1)
                transposes(NJOB - 1)


def attend(nc, d, K):
    with Stage(nc, "att") as S:
        kcT = S.sb("kcT", [P, NSEQ, WIN])
        vc = S.sb("vc", [P, NSEQ, 128])
        mcT = S.sb("mcT", [P, 2, NSEQ, MEM])
        mcv = S.sb("mcv", [P, 2, NSEQ, 256])
        mask = S.sb("mask", [P, 256])
        smask = S.sb("smask", [P, NSEQ * WIN + NSMP])
        bmask = S.sb("bmask", [P, NSEQ])
        sinks = S.sb("sinks", [P, 5])
        sm = S.sb("sm", [P, 2, 1024])
        big = S.sb("big", [P, NSEQ * MEM])
        pr = S.sb("pr", [P, 2, 1024])
        prT = S.sb("prT", [P, 2, 1024])
        mx = S.sb("mx", [P, 2, 4])
        nm = S.sb("nm", [P, 2, 4])
        den = S.sb("den", [P, 2, 4])
        es = S.sb("es", [P, 2, 4])
        sc = S.ps("sc", [P, 2048])
        tp = S.ps("tp", [P, 1024])
        ov = S.ps("ov", [P, 2, 512])

        s_in = S.sem("masks_landed")
        s_cache = S.sem("caches_landed")
        s_sc = S.sem("scores")
        s_sm = S.sem("scores_read")
        s_mx = S.sem("maxima")
        s_ex = S.sem("exps")
        s_pr = S.sem("probs")
        s_tp = S.sem("probs_turned")
        s_te = S.sem("turned_out")
        s_ov = S.sem("values")
        s_oe = S.sem("values_out")
        s_v = S.sem("dve_chain")

        units = [("win", i) for i in range(4)] + [("mem", i) for i in range(4)] + [("swin", 4), ("smem", 4)]
        NU = len(units)

        def shape(kind, i):
            if kind == "win":
                return 4, 256, (128 if i == 0 else 0)
            if kind == "mem":
                return 4, 256, 0
            if kind == "swin":
                return 1, WIN + NSMP, 0
            return 1, 256, 0

        def probs(buf, kind, i, n):
            h, w, lo = shape(kind, i)
            if h == 4:
                return buf[:, n % 2, :].rearrange("p (h k) -> p h k", h=4)[:, :, lo:]
            return buf[:, n % 2, 0:w].unsqueeze(1)

        with S.block() as block:
            @block.sync
            def _(sp):
                sp.dma_start(mask[:, :], d["mask"]).then_inc(s_in, 16)
                sp.dma_start(sinks[:, :], d["sinks"]).then_inc(s_in, 16)
                sp.dma_start(smask[:, :], d["smask"]).then_inc(s_in, 16)
                sp.dma_start(bmask[:, :], d["bmask"]).then_inc(s_in, 16)
                sp.dma_start(kcT[:, :, :], d["kcT"]).then_inc(s_cache, 16)
                sp.dma_start(vc[:, :, :], d["vc"]).then_inc(s_cache, 16)
                sp.dma_start(mcT[:, :, :, :], d["mcT"]).then_inc(s_cache, 16)
                sp.dma_start(mcv[:, :, :, :], d["mcv"]).then_inc(s_cache, 16)

            @block.tensor
            def _(pe):
                def scores(n):
                    kind, i = units[n]
                    at = (n % 2) * 1024
                    if n >= 2:
                        pe.wait_ge(s_sm, n - 1)
                    if kind in ("swin", "smem"):
                        pe.wait_ge(s_sm, n)
                        pe.wait_ge(s_cache, 64)
                    tok = slice(i * P, i * P + ROWS[i])
                    for h in range(4):
                        lo, hi = (h % 2) * HD, (h % 2) * HD + HD
                        slot = (h % 2) * 2 + h // 2
                        if kind == "win":
                            a = 128 if i == 0 else 0
                            mm = pe.matmul(sc[:, at + slot * 256 + a:at + slot * 256 + 256], K.qkT[lo:hi, h // 2, tok],
                                           K.qkT[lo:hi, 2, (i - 1) * P + a:(i + 1) * P], start=True, stop=True)
                        elif kind == "mem":
                            mm = pe.matmul(sc[:, at + slot * 256:at + slot * 256 + 256], K.qkT[lo:hi, 3 + h // 2, tok],
                                           K.mkT[lo:hi, h // 2, :], start=True, stop=True)
                        elif kind == "swin":
                            for c in range(2):
                                pe.matmul(sc[h * 32:h * 32 + 32, c * 512:(c + 1) * 512], K.qkT[lo:hi, h // 2, tok],
                                          kcT[lo:hi, c * 4:(c + 1) * 4, :], start=True, stop=True)
                            mm = pe.matmul(sc[h * 32:h * 32 + 32, 1024:1024 + NSMP], K.qkT[lo:hi, h // 2, tok],
                                           K.qkT[lo:hi, 2, SEQ:T], start=True, stop=True)
                        else:
                            for c in range(4):
                                mm = pe.matmul(sc[h * 32:h * 32 + 32, c * 512:(c + 1) * 512], K.qkT[lo:hi, 3 + h // 2, tok],
                                               mcT[lo:hi, h // 2, c * 2:(c + 1) * 2, :], start=True, stop=True)
                    mm.then_inc(s_sc, 1)

                def turn(n):
                    kind, i = units[n]
                    h, w, lo = shape(kind, i)
                    pe.wait_ge(s_pr, n + 1)
                    if n >= 1:
                        pe.wait_ge(s_te, n)
                    if h == 4:
                        for x in range(4):
                            for m in range(lo // 128, 2):
                                mm = pe.transpose(tp[:, (2 * x + m) * P:(2 * x + m + 1) * P],
                                                  pr[:, n % 2, x * 256 + m * P:x * 256 + (m + 1) * P], K.ident[:, :])
                    else:
                        pe.transpose(tp[:, 0:P], pr[:, n % 2, 0:P], K.ident[:, :])
                        mm = pe.transpose(tp[0:w - P, P:2 * P], pr[:, n % 2, P:w], K.ident[:, :])
                    mm.then_inc(s_tp, 1)

                def values(n):
                    kind, i = units[n]
                    pe.wait_ge(s_te, n + 1)
                    if n >= 2:
                        pe.wait_ge(s_oe, n - 1)
                    o = ov[:, n % 2, 0:256].rearrange("p (c q) -> p c q", c=2)
                    pT = prT[:, n % 2, :]
                    for h in range(4):
                        for m in range(2):
                            cols = slice((2 * h + m) * P, (2 * h + m + 1) * P)
                            if kind == "win":
                                kv, r = h // 2, h % 2
                                if i == 0 and m == 0:
                                    continue
                                mm = pe.matmul(o[r * HD:r * HD + HD, kv, :], K.v[:, i - 1 + m, kv * HD:kv * HD + HD],
                                               pT[:, cols], start=(m == 0 or i == 0), stop=(m == 1))
                            elif kind == "mem":
                                hp, c = h // 2, h % 2
                                x = c * 2 + hp
                                mm = pe.matmul(o[hp * HD:hp * HD + HD, c, :], K.mv[:, m, x * HD:x * HD + HD],
                                               pT[:, cols], start=(m == 0), stop=(m == 1))
                        if kind == "swin":
                            r, kv = h // 2, h % 2
                            dst = o[r * HD:r * HD + HD, kv, :]
                            pe.matmul(dst[:, 0:NSMP], K.v[0:NSMP, 4, kv * HD:kv * HD + HD],
                                      pT[0:NSMP, P + h * 32:P + h * 32 + 32], start=True, stop=False)
                            for b in range(NSEQ):
                                q = slice(b * DSEQ, (b + 1) * DSEQ)
                                mm = pe.matmul(dst[:, q], vc[:, b, kv * HD:kv * HD + HD],
                                               pT[:, h * 32 + b * DSEQ:h * 32 + (b + 1) * DSEQ],
                                               start=False, stop=(b == NSEQ - 1))
                        elif kind == "smem":
                            hp = h % 2
                            for b in range(NSEQ):
                                q = slice(b * DSEQ, (b + 1) * DSEQ)
                                for m in range(2):
                                    mm = pe.matmul(o[hp * HD:hp * HD + HD, h // 2, q], mcv[:, m, b, h * HD:h * HD + HD],
                                                   pT[:, m * P + h * 32 + b * DSEQ:m * P + h * 32 + (b + 1) * DSEQ],
                                                   start=(m == 0), stop=(m == 1))
                    mm.then_inc(s_ov, 1)

                scores(0)
                for n in range(NU):
                    if n + 1 < NU:
                        scores(n + 1)
                    turn(n)
                    values(n)

            @block.vector
            def _(dve):
                step = Chain(dve, s_v)
                dve.wait_ge(s_in, 64)
                SCALE = float(HD) ** -0.5

                def maxima(n):
                    kind, i = units[n]
                    h, w, lo = shape(kind, i)
                    at = (n % 2) * 1024
                    if n >= 2:
                        dve.wait_ge(s_ex, n - 1)
                    dve.wait_ge(s_sc, n + 1)
                    dst = probs(sm, kind, i, n)
                    if kind == "win":
                        src = sc[:, at:at + 1024].rearrange("p (h k) -> p h k", h=4)[:, :, lo:]
                        ins = dve.scalar_tensor_tensor(dst, src, SCALE, widen(mask[:, lo:], 1, 4), ALU.mult, ALU.add)
                    elif kind == "mem":
                        ins = dve.tensor_scalar(sm[:, n % 2, :], sc[:, at:at + 1024], SCALE, None, ALU.mult)
                    elif kind == "swin":
                        W = NSEQ * WIN
                        ins = dve.scalar_tensor_tensor(big[:, 0:W + NSMP], sc[:, 0:W + NSMP], SCALE, smask[:, :], ALU.mult, ALU.add)
                    else:
                        ins = dve.scalar_tensor_tensor(big[:, :].rearrange("p (b k) -> p b k", b=NSEQ),
                                                       sc[:, :].rearrange("p (b k) -> p b k", b=NSEQ), SCALE,
                                                       widen(bmask[:, :], 2, MEM), ALU.mult, ALU.add)
                    ins.then_inc(s_sm, 1)
                    dve.wait_ge(s_sm, n + 1)
                    if h == 1:
                        k = WIN if kind == "swin" else MEM
                        ins = dve.tensor_reduce(sm[:, n % 2, 0:k], big[:, 0:NSEQ * k].rearrange("p (b k) -> p k b", b=NSEQ), AX.X, ALU.max)
                        if kind == "swin":
                            ins = dve.tensor_copy(sm[:, n % 2, k:k + NSMP], big[:, NSEQ * k:NSEQ * k + NSMP])
                        step(ins)
                    step(dve.tensor_reduce(mx[:, n % 2, 0:h], dst, AX.X, ALU.max))
                    if kind in ("win", "swin"):
                        snk = sinks[:, 0:4] if h == 4 else sinks[:, 4:5]
                        step(dve.tensor_tensor(mx[:, n % 2, 0:h], mx[:, n % 2, 0:h], snk, ALU.max))
                        dve.tensor_tensor(es[:, n % 2, 0:h], snk, mx[:, n % 2, 0:h], ALU.subtract)
                    dve.tensor_scalar(nm[:, n % 2, 0:h], mx[:, n % 2, 0:h], -1.0, None, ALU.mult).then_inc(s_mx, 1)

                def normalise(n):
                    kind, i = units[n]
                    h, w, lo = shape(kind, i)
                    dve.wait_ge(s_ex, n + 1)
                    if kind in ("win", "swin"):
                        step(dve.tensor_tensor(den[:, n % 2, 0:h], den[:, n % 2, 0:h], es[:, n % 2, 0:h], ALU.add))
                    step(dve.reciprocal(den[:, n % 2, 0:h], den[:, n % 2, 0:h]))
                    p = probs(pr, kind, i, n)
                    dve.tensor_tensor(p, p, widen(den[:, n % 2, 0:h], 2, w - lo), ALU.mult).then_inc(s_pr, 1)

                maxima(0)
                for n in range(NU):
                    if n + 1 < NU:
                        maxima(n + 1)
                    normalise(n)

            @block.scalar
            def _(act):
                def exps(n):
                    kind, i = units[n]
                    h, w, lo = shape(kind, i)
                    act.wait_ge(s_mx, n + 1)
                    if n >= 2:
                        act.wait_ge(s_tp, n - 1)
                    src, dst = probs(sm, kind, i, n), probs(pr, kind, i, n)
                    if kind in ("win", "swin"):
                        act.activation(es[:, n % 2, 0:h], es[:, n % 2, 0:h], ACT.Exp)
                    for x in range(h):
                        ins = act.activation(dst[:, x, :], src[:, x, :], ACT.Exp, bias=nm[:, n % 2, x:x + 1],
                                             accum_out=den[:, n % 2, x:x + 1])
                    ins.then_inc(s_ex, 1)

                def evacuate(n):
                    kind, i = units[n]
                    h, w, lo = shape(kind, i)
                    act.wait_ge(s_tp, n + 1)
                    if n >= 2:
                        act.wait_ge(s_ov, n - 1)
                    if h == 4:
                        v = lambda t: t.rearrange("p (h m q) -> p h m q", h=4, m=2)[:, :, lo // 128:, :]
                        ins = act.activation(v(prT[:, n % 2, :]), v(tp[:, :]), ACT.Copy)
                    elif kind == "swin":
                        act.activation(prT[:, n % 2, 0:P], tp[:, 0:P], ACT.Copy)
                        ins = act.activation(prT[0:NSMP, n % 2, P:2 * P], tp[0:NSMP, P:2 * P], ACT.Copy)
                    else:
                        ins = act.activation(prT[:, n % 2, 0:2 * P], tp[:, 0:2 * P], ACT.Copy)
                    ins.then_inc(s_te, 1)
                    act.wait_ge(s_ov, n + 1)
                    base = 6 if "mem" in kind else 4
                    r = ROWS[i]
                    o = ov[:, n % 2, 0:256].rearrange("p (c q) -> p c q", c=2)
                    act.activation(K.mixedT[:, base:base + 2, i * P:i * P + r], o[:, :, 0:r], ACT.Copy).then_inc(s_oe, 1)

                exps(0)
                for n in range(NU):
                    if n + 1 < NU:
                        exps(n + 1)
                    evacuate(n)


def two_pi_parts():
    full = 2 * np.pi
    a = 6.28125
    b = float(np.floor((full - a) * 2 ** 20) / 2 ** 20)
    return a, b, float(np.float32(full - a - b))


def ssm(nc, d, K):
    with Stage(nc, "ssm") as S:
        par = S.sb("par", [P, 3, GP])
        bc = S.sb("bc", [P, 4, GP, C])
        dsk = S.sb("dsk", [C, G])
        s0 = S.sb("s0", [P, 2, GP, NSEQ])
        w = S.sb("w", [P, 24, GP])
        L = S.sb("L", [P, 3, CH + 1, GP])
        Lrev = S.sb("Lrev", [P, 2, CH, GP])
        bb = S.sb("bb", [P, 2, GP, C])
        Q = S.sb("Q", [P, 2, GP, CH + 1, C])
        tmp = S.sb("tmp", [P, 2, GP, CH + 1, C])
        W = S.sb("W", [P, 2, GP, CH, C])
        WT = S.sb("WT", [P, 2, GP, P])
        ZK = S.sb("ZK", [C, G, (CH - 1) * C + P])
        dI = S.sb("dI", [C, G, C])
        MT = S.sb("MT", [P, G, P])
        uch = S.sb("uch", [NJ + 2 * NSEQ, CH, UW])
        U = S.sb("U", [P, G, NJ + 2 * NSEQ])
        V = tmp[:, :, :, :, :].rearrange("p a g t c -> p (a g t c)")[:, 0:2 * GP * (NJ + 2 * NSEQ)]\
            .rearrange("p (r g j) -> p r g j", r=2, g=GP)
        A8 = S.sb("A8", [P, 2, 2, GP])
        SPv = W[:, :, :, :, :].rearrange("p a g t c -> p (a g t c)")[:, 0:2 * GP * COLS]\
            .rearrange("p (r g j) -> p r g j", r=2, g=GP)
        prod = S.sb("prod", [P, 2, 2, GP])
        part = S.sb("part", [P, 2, GP])
        fin = S.sb("fin", [P, 2, GP])
        room = tmp[:, :, :, :, :].rearrange("p a g t c -> p (a g t c)")[:, 2560:2560 + 4 * GP * NSEQ]\
            .rearrange("p (x r g b) -> p x r g b", x=2, r=2, g=GP)
        sfin, st = room[:, 0, :, :, :], room[:, 1, :, :, :]
        NC = NJ + 2 * NSEQ
        ug = K.y[:, :, :].rearrange("p t c -> p (t c)").rearrange("p (g x) -> p g x", g=G)
        pp = S.ps("pp", [P, 8, 512])

        s_ug = S.sem("chunks_grouped")
        s_in = S.sem("params_landed")
        s_uch = S.sem("chunks_landed")
        s_mt = S.sem("toeplitz_landed")
        s_a = S.sem("act_to_dve")
        s_b = S.sem("dve_to_act")
        s_v = S.sem("dve_chain")
        s_g = S.sem("pool_chain")
        s_bb = S.sem("bb_ready")
        s_q = S.sem("q_ready")
        s_w = S.sem("w_ready")
        s_uz = S.sem("uch_zeroed")
        s_ut = S.sem("u_turned")
        s_ue = S.sem("u_out")
        s_wt = S.sem("w_turned")
        s_we = S.sem("w_out")
        s_kt = S.sem("kernels")
        s_ke = S.sem("kernels_out")
        s_z = S.sem("kernels_ready")
        s_vm = S.sem("inputs_summed")
        s_ve = S.sem("inputs_out")
        s_A = S.sem("a8_ready")
        s_scan = S.sem("scanned")
        s_ym = S.sem("y_summed")
        s_ye = S.sem("y_out")
        s_sf = S.sem("sample_state")
        s_out = S.sem("stored")
        s_p = S.sem("pool_tables")

        NB = 8
        UB = 6
        ub = [range(i, min(i + UB, G)) for i in range(0, G, UB)]
        VB = 3
        vb = [range(i, min(i + VB, GP)) for i in range(0, GP, VB)]

        with S.block() as block:
            @block.sync
            def _(sp):
                sp.dma_start(par[:, :, :], d["ssm_par"]).then_inc(s_in, 16)
                sp.dma_start(bc[:, :, :, :], d["ssm_bc"]).then_inc(s_in, 16)
                sp.dma_start(dsk[:, :], d["ssm_d"]).then_inc(s_in, 16)
                sp.dma_start(s0[:, :, :, :], d["ssm_s0"]).then_inc(s_in, 16)
                us = d["u_scratch"]
                sp.dma_start(uch[0:NJ, :, :], us[0:SEQ, :].rearrange("(j t) c -> j t c", t=CH)).then_inc(s_uch, 16)
                sp.wait_ge(s_uz, 1)
                smp = us[SEQ:T, :].rearrange("(b t) c -> b t c", t=DSEQ)
                sp.dma_start(uch[NJ:NJ + NSEQ, 0:DSEQ, :], smp).then_inc(s_uch, 16)
                sp.dma_start(uch[NJ + NSEQ:NC, DSEQ:CH, :], smp).then_inc(s_uch, 16)
                sp.wait_ge(s_z, 1)
                for t in range(CH):
                    o = (CH - 1 - t) * C
                    sp.dma_start(MT[t * C:(t + 1) * C, :, :], ZK[:, :, o:o + P]).then_inc(s_mt, 16)
                sp.wait_ge(s_scan, 1)
                sp.dma_start(d["p_ssm"], fin[:, :, :]).then_inc(s_out, 16)
                sp.wait_ge(s_sf, 1)
                sp.dma_start(d["s_ssm"], sfin[:, :, :, :]).then_inc(s_out, 16)
                sp.wait_ge(s_out, 32)

            @block.scalar
            def _(act):
                act.wait_ge(s_in, 64)
                act.activation(w[:, 0, :], par[:, 0, :], ACT.Exp).then_inc(s_a, 1)
                act.wait_ge(s_b, 1)
                act.activation(w[:, 3, :], w[:, 1, :], ACT.Exp).then_inc(s_a, 1)
                act.wait_ge(s_b, 2)
                act.activation(w[:, 6:8, :], w[:, 4:6, :], ACT.Sin).then_inc(s_a, 1)
                act.wait_ge(s_uch, 48)
                act.activation(ug.rearrange("p g (t c) -> p g t c", c=C), uch[:, :, :].rearrange("p t (g c) -> p g t c", c=C),
                               ACT.Copy).then_inc(s_ug, 1)
                for n, gs in enumerate(ub):
                    act.wait_ge(s_ut, n + 1)
                    k = len(gs)
                    act.activation(U[:, gs[0]:gs[0] + k, :], pp[:, n, 0:k * NC].rearrange("p (g j) -> p g j", j=NC),
                                   ACT.Copy).then_inc(s_ue, 1)
                for n in range(8):
                    act.wait_ge(s_wt, n + 1)
                    act.activation(WT[:, n // 4, (n % 4) * 4:(n % 4) * 4 + 4, :],
                                   pp[:, n, :].rearrange("p (g j) -> p g j", j=P), ACT.Copy).then_inc(s_we, 1)
                for n in range(8):
                    act.wait_ge(s_kt, n + 1)
                    act.activation(ZK[:, :, (CH - 1) * C:].rearrange("p (a m e) x -> p a e m x", m=4, e=2)[:, n // 2, n % 2, :, :], pp[0:C, n, :].rearrange("p (g j) -> p g j", j=P),
                                   ACT.Copy).then_inc(s_ke, 1)
                for n, gs in enumerate(vb):
                    act.wait_ge(s_vm, n + 1)
                    k = len(gs)
                    act.activation(V[:, :, gs[0]:gs[0] + k, :].rearrange("p r g j -> p g r j"),
                                   pp[:, n, 0:k * 2 * NC].rearrange("p (g r j) -> p g r j", r=2, j=NC),
                                   ACT.Copy).then_inc(s_ve, 1)
                for n in range(8):
                    act.wait_ge(s_ym, n + 1)
                    act.activation(K.y[0:COLS, :, :].rearrange("p t (a m e c) -> p a e m t c", m=4, e=2, c=C)[:, n // 2, n % 2, :, :, :],
                                   pp[0:COLS, n, :].rearrange("p (g t c) -> p g t c", t=CH, c=C), ACT.Gelu).then_inc(s_ye, 1)

            @block.vector
            def _(dve):
                step = Chain(dve, s_v)
                tt = dve.tensor_tensor
                dve.memset(ZK[:, :, 0:(CH - 1) * C], 0.0)
                dve.memset(L[:, 0, 0, :], 1.0)
                step(dve.memset(L[:, 1:3, 0, :], 0.0))
                dve.wait_ge(s_in, 64)
                dve.wait_ge(s_a, 1)
                tt(w[:, 1, :], par[:, 1, :], w[:, 0, :], ALU.mult).then_inc(s_b, 1)
                step(tt(w[:, 2, :], par[:, 2, :], w[:, 0, :], ALU.mult))
                a, b, c = two_pi_parts()
                for n, quarter in enumerate((0.0, 0.25)):
                    k = w[:, 8 + n, :]
                    step(dve.tensor_scalar(k, w[:, 2, :], float(1 / (2 * np.pi)), quarter, ALU.mult, ALU.add))
                    step(dve.tensor_scalar(k, k, 12582912.0, None, ALU.add))
                    step(dve.tensor_scalar(k, k, -12582912.0, None, ALU.add))
                    r = w[:, 4 + n, :]
                    step(dve.scalar_tensor_tensor(r, k, -a, w[:, 2, :], ALU.mult, ALU.add))
                    step(dve.scalar_tensor_tensor(r, k, -b, r, ALU.mult, ALU.add))
                    step(dve.scalar_tensor_tensor(r, k, -c, r, ALU.mult, ALU.add))
                    if n:
                        step(dve.tensor_scalar(r, r, float(np.pi / 2), None, ALU.add))
                    ins = dve.tensor_scalar(r, r, 3.1415925, -3.1415925, ALU.min, ALU.max)
                    if n:
                        ins.then_inc(s_b, 1)
                    else:
                        step(ins)
                dve.wait_ge(s_a, 3)
                tt(L[:, 0, 1, :], w[:, 3, :], w[:, 7, :], ALU.mult)
                step(tt(L[:, 1, 1, :], w[:, 3, :], w[:, 6, :], ALU.mult))
                ar, ai = par[:, 1, :], par[:, 2, :]
                step(dve.tensor_scalar(w[:, 10, :], L[:, 0, 1, :], 1.0, None, ALU.subtract))
                lm, li = w[:, 10, :], L[:, 1, 1, :]
                tt(w[:, 11, :], ar, ar, ALU.mult)
                tt(w[:, 12, :], ai, ai, ALU.mult)
                tt(w[:, 13, :], lm, ar, ALU.mult)
                tt(w[:, 14, :], li, ai, ALU.mult)
                tt(w[:, 15, :], li, ar, ALU.mult)
                step(tt(w[:, 16, :], lm, ai, ALU.mult))
                tt(w[:, 11, :], w[:, 11, :], w[:, 12, :], ALU.add)
                tt(w[:, 13, :], w[:, 13, :], w[:, 14, :], ALU.add)
                step(tt(w[:, 15, :], w[:, 15, :], w[:, 16, :], ALU.subtract))
                step(dve.reciprocal(w[:, 11, :], w[:, 11, :]))
                tt(w[:, 17, :], w[:, 13, :], w[:, 11, :], ALU.mult)
                step(tt(w[:, 18, :], w[:, 15, :], w[:, 11, :], ALU.mult))
                zr, zi = widen(w[:, 17, :], 2, C), widen(w[:, 18, :], 2, C)
                t4 = [tmp[:, n // 2, :, n % 2, :] for n in range(4)]
                br, bi = bc[:, 0, :, :], bc[:, 1, :, :]
                tt(t4[0], zr, br, ALU.mult)
                tt(t4[1], zi, bi, ALU.mult)
                tt(t4[2], zr, bi, ALU.mult)
                step(tt(t4[3], zi, br, ALU.mult))
                tt(bb[:, 0, :, :], t4[0], t4[1], ALU.subtract)
                step(tt(bb[:, 1, :, :], t4[2], t4[3], ALU.add))
                for m in (1, 2, 4):
                    lo, hi = slice(1, m + 1), slice(m + 1, 2 * m + 1)
                    mr, mi = widen(L[:, 0, m, :], 1, m), widen(L[:, 1, m, :], 1, m)
                    q = [tmp[:, n // 2, 0:m, (n % 2), :] for n in range(4)]
                    tt(q[0], L[:, 0, lo, :], mr, ALU.mult)
                    tt(q[1], L[:, 1, lo, :], mi, ALU.mult)
                    tt(q[2], L[:, 0, lo, :], mi, ALU.mult)
                    step(tt(q[3], L[:, 1, lo, :], mr, ALU.mult))
                    tt(L[:, 0, hi, :], q[0], q[1], ALU.subtract)
                    step(tt(L[:, 1, hi, :], q[2], q[3], ALU.add))
                dve.tensor_scalar(L[:, 2, 1:, :], L[:, 1, 1:, :], -1.0, None, ALU.mult)
                for t in range(CH):
                    ins = dve.tensor_copy(Lrev[:, :, t, :], L[:, 0:2, CH - 1 - t, :])
                step(ins)
                for o in range(2):
                    dve.tensor_copy(A8[:, o, o, :], L[:, 0, CH, :])
                dve.tensor_copy(A8[:, 0, 1, :], L[:, 2, CH, :])
                dve.tensor_copy(A8[:, 1, 0, :], L[:, 1, CH, :]).then_inc(s_A, 1)
                lr = widen(Lrev[:, 0, :, :].rearrange("p t g -> p g t"), 3, C)
                li = widen(Lrev[:, 1, :, :].rearrange("p t g -> p g t"), 3, C)
                b_r, b_i = widen(bb[:, 0, :, :], 2, CH), widen(bb[:, 1, :, :], 2, CH)
                t0, t1 = tmp[:, 0, :, 0:CH, :], tmp[:, 1, :, 0:CH, :]
                for n, (x, y, op) in enumerate(((b_r, b_i, ALU.subtract), (b_i, b_r, ALU.add))):
                    tt(t0, lr, x, ALU.mult)
                    step(tt(t1, li, y, ALU.mult))
                    step(tt(W[:, n, :, :, :], t0, t1, op))
                dve.engine_nop().then_inc(s_w, 1)
                tt(dI[:, :, :], widen(K.ident[0:C, 0:C], 1, G), widen(dsk[:, :], 2, C), ALU.mult)
                lr = widen(L[:, 0, :, :].rearrange("p t g -> p g t"), 3, C)
                li = widen(L[:, 1, :, :].rearrange("p t g -> p g t"), 3, C)
                ln = widen(L[:, 2, :, :].rearrange("p t g -> p g t"), 3, C)
                c_r, c_i = widen(bc[:, 2, :, :], 2, CH + 1), widen(bc[:, 3, :, :], 2, CH + 1)
                t0, t1 = tmp[:, 0, :, :, :], tmp[:, 1, :, :, :]
                for n, (x, y) in enumerate(((lr, li), (ln, lr))):
                    tt(t0, c_r, x, ALU.mult)
                    step(tt(t1, c_i, y, ALU.mult))
                    step(tt(Q[:, n, :, :, :], t0, t1, ALU.subtract))
                dve.engine_nop().then_inc(s_q, 1)
                dve.wait_ge(s_ke, 8)
                k0 = ZK[:, :, (CH - 1) * C:CH * C]
                tt(k0, k0, dI[:, :, :], ALU.add).then_inc(s_z, 1)
                dve.wait_ge(s_ve, len(vb))
                l4r, l4i = widen(L[:, 0, DSEQ, :], 2, NSEQ), widen(L[:, 1, DSEQ, :], 2, NSEQ)
                x0, x1 = s0[:, 0, :, :], s0[:, 1, :, :]
                v = V[:, :, :, NJ + NSEQ:NC]
                for n, (x, y, op) in enumerate(((x0, x1, ALU.subtract), (x1, x0, ALU.add))):
                    tt(st[:, 0, :, :], l4r, x, ALU.mult)
                    step(tt(st[:, 1, :, :], l4i, y, ALU.mult))
                    step(tt(sfin[:, n, :, :], st[:, 0, :, :], st[:, 1, :, :], op))
                tt(sfin[:, :, :, :], sfin[:, :, :, :], v, ALU.add).then_inc(s_sf, 1)

            @block.gpsimd
            def _(pool):
                n = 0
                pool.memset(uch[NJ:NC, :, :], 0.0).then_inc(s_uz, 1)
                pool.wait_ge(s_in, 64)
                pool.wait_ge(s_wt, 8)
                pool.tensor_copy(SPv[:, :, :, NJ:COLS], s0[:, :, :, :])
                pool.memset(SPv[:, :, :, 0:1], 0.0).then_inc(s_g, 1)
                n += 1
                pool.wait_ge(s_A, 1)
                pool.wait_ge(s_ve, len(vb))
                for j in range(NJ):
                    pool.wait_ge(s_g, n)
                    pool.tensor_tensor(prod[:, :, :, :], A8[:, :, :, :], widen(SPv[:, :, :, j], 1, 2), ALU.mult).then_inc(s_g, 1)
                    n += 1
                    pool.wait_ge(s_g, n)
                    pool.tensor_tensor(part[:, :, :], prod[:, :, 0, :], prod[:, :, 1, :], ALU.add).then_inc(s_g, 1)
                    n += 1
                    pool.wait_ge(s_g, n)
                    dst = SPv[:, :, :, j + 1] if j + 1 < NJ else fin[:, :, :]
                    pool.tensor_tensor(dst, part[:, :, :], V[:, :, :, j], ALU.add).then_inc(s_g, 1)
                    n += 1
                pool.wait_ge(s_g, n)
                pool.engine_nop().then_inc(s_scan, 1)

            @block.tensor
            def _(pe):
                pe.wait_ge(s_ug, 1)
                for n, gs in enumerate(ub):
                    for m, g in enumerate(gs):
                        mm = pe.transpose(pp[:, n, m * NC:(m + 1) * NC], ug[:, g, :], K.ident[:NC, :NC])
                    mm.then_inc(s_ut, 1)
                pe.wait_ge(s_w, 1)
                for n in range(8):
                    if n < len(ub):
                        pe.wait_ge(s_ue, n + 1)
                    for m in range(4):
                        mm = pe.transpose(pp[:, n, m * P:(m + 1) * P],
                                          W[:, n // 4, (n % 4) * 4 + m, :, :].rearrange("p t c -> p (t c)"), K.ident[:, :])
                    mm.then_inc(s_wt, 1)
                pe.wait_ge(s_q, 1)
                for n in range(8):
                    pe.wait_ge(s_we, n + 1)
                    for m in range(4):
                        g = (n // 2) * 8 + 2 * m + n % 2
                        h = slice((g % 2) * N, (g % 2) * N + N)
                        for ri in range(2):
                            mm = pe.matmul(pp[0:C, n, m * P:(m + 1) * P], bb[h, ri, g // 2, :], Q[h, ri, g // 2, 0:CH, :],
                                           start=(ri == 0), stop=(ri == 1))
                    mm.then_inc(s_kt, 1)
                for n, gs in enumerate(vb):
                    pe.wait_ge(s_ke, n + 1)
                    for m, gp in enumerate(gs):
                        for e in range(2):
                            h = slice(e * N, e * N + N)
                            for ri in range(2):
                                mm = pe.matmul(pp[h, n, (m * 2 + ri) * NC:(m * 2 + ri + 1) * NC], WT[:, ri, gp, h],
                                               U[:, gp * 2 + e, :], start=True, stop=True)
                    mm.then_inc(s_vm, 1)
                pe.wait_ge(s_mt, 16 * CH)
                pe.wait_ge(s_scan, 1)
                for n in range(8):
                    pe.wait_ge(s_ke, 8)
                    if n < len(vb):
                        pe.wait_ge(s_ve, n + 1)
                    for m in range(4):
                        g = (n // 2) * 8 + 2 * m + n % 2
                        h = slice((g % 2) * N, (g % 2) * N + N)
                        o = pp[0:COLS, n, m * P:(m + 1) * P]
                        pe.matmul(o, U[:, g, 0:COLS], MT[:, g, :], start=True, stop=False)
                        for ri in range(2):
                            mm = pe.matmul(o, SPv[h, ri, g // 2, :], Q[h, ri, g // 2, 1:CH + 1, :], start=False, stop=(ri == 1))
                    mm.then_inc(s_ym, 1)


def mix(nc, d, K):
    with Stage(nc, "mix", "right") as S:
        wg = S.sb("wg", [P, 4, 512])
        bg = S.sb("bg", [P, 4])
        wo = S.sb("wo", [P, KD, D])
        g2 = S.sb("g2", [P, D])
        yT = S.sb("yT", [P, 4, CH, COLS])
        sg = S.sb("sg", [P, 2, 4, COLS])
        square = S.sb("square", [P, D])
        ss = S.sb("ss", [P, NT])
        pp = S.ps("pp", [P, 2, 2, 512])
        pq = S.ps("pq", [P, 4, 512])

        s_in = S.sem("glu_landed")
        s_wo = S.sem("wout_landed")
        s_yt = S.sem("y_turned")
        s_ye = S.sem("y_out")
        s_gm = S.sem("glu_summed")
        s_sg = S.sem("sigmoids")
        s_gl = S.sem("glu_done")
        s_om = S.sem("out_summed")
        s_h = S.sem("residual")
        s_ss = S.sem("squares")
        s_std = S.sem("std")
        s_xn = S.sem("normed")
        s_xt = S.sem("normed_turned")
        s_xe = S.sem("normed_out")
        s_v = S.sem("dve_chain")

        with S.block() as block:
            @block.sync
            def _(sp):
                sp.dma_start(wg[:, :, :], d["w_glu"]).then_inc(s_in, 16)
                sp.dma_start(bg[:, :], d["b_glu"]).then_inc(s_in, 16)
                sp.dma_start(g2[:, :], d["g2"]).then_inc(s_in, 16)
                sp.dma_start(wo[:, :, :], d["w_out"]).then_inc(s_wo, 16)

            @block.tensor
            def _(pe):
                for n in range(8):
                    kc, th = n // 2, n % 2
                    if n >= 4:
                        pe.wait_ge(s_ye, n - 3)
                    for t in range(4):
                        mm = pe.transpose(pq[:, n % 4, t * COLS:(t + 1) * COLS],
                                          K.y[0:COLS, th * 4 + t, kc * P:(kc + 1) * P], K.ident[:COLS, :COLS])
                    mm.then_inc(s_yt, 1)
                pe.wait_ge(s_in, 48)
                pe.wait_ge(s_ye, 8)
                for n in range(8):
                    co, th = n // 2, n % 2
                    if n >= 4:
                        pe.wait_ge(s_sg, n - 3)
                    for kc in range(4):
                        mm = pe.matmul(pq[:, n % 4, 0:4 * COLS], wg[:, kc, co * P:(co + 1) * P],
                                       yT[:, kc, th * 4:(th + 1) * 4, :], start=(kc == 0), stop=(kc == 3))
                    mm.then_inc(s_gm, 1)
                pe.wait_ge(s_wo, 16)
                pe.wait_ge(s_gl, 8)

                def turn(i):
                    r = ROWS[i]
                    pe.wait_ge(s_xn, i + 1)
                    if i >= 2:
                        pe.wait_ge(s_xe, i - 1)
                    for k in range(KD):
                        mm = pe.transpose(pq[:, (i % 2) * 2 + k // 4, (k % 4) * P:(k % 4) * P + r],
                                          K.xn[:r, i, k * P:(k + 1) * P], K.ident[:r, :r])
                    mm.then_inc(s_xt, 1)

                for i in range(NT):
                    r = ROWS[i]
                    if i >= 2:
                        pe.wait_ge(s_h, i - 1)
                    for k in range(KD):
                        for c in range(2):
                            mm = pe.matmul(pp[:r, i % 2, c, :], K.mixedT[:, k, i * P:i * P + r], wo[:, k, c * 512:(c + 1) * 512],
                                           start=(k == 0), stop=(k == KD - 1))
                    mm.then_inc(s_om, 1)
                    if i >= 1:
                        turn(i - 1)
                turn(NT - 1)

            @block.scalar
            def _(act):
                for n in range(8):
                    kc, th = n // 2, n % 2
                    act.wait_ge(s_yt, n + 1)
                    act.activation(yT[:, kc, th * 4:(th + 1) * 4, :], pq[:, n % 4, 0:4 * COLS].rearrange("p (t j) -> p t j", j=COLS),
                                   ACT.Copy).then_inc(s_ye, 1)
                act.wait_ge(s_in, 48)
                for n in range(8):
                    co = n // 2
                    act.wait_ge(s_gm, n + 1)
                    if n >= 2:
                        act.wait_ge(s_gl, n - 1)
                    act.activation(sg[:, n % 2, :, :], pq[:, n % 4, 0:4 * COLS].rearrange("p (t j) -> p t j", j=COLS),
                                   ACT.Sigmoid, bias=bg[:, co:co + 1]).then_inc(s_sg, 1)

                def out(i):
                    r = ROWS[i]
                    act.wait_ge(s_xt, i + 1)
                    act.activation(K.xnT[:, :, i * P:i * P + r],
                                   pq[:, (i % 2) * 2:(i % 2) * 2 + 2, :].rearrange("p a (b t) -> p (a b) t", t=P)[:, :, :r],
                                   ACT.Copy).then_inc(s_xe, 1)

                for i in range(NT):
                    r = ROWS[i]
                    act.wait_ge(s_h, i + 1)
                    act.activation(square[:r, :], K.x[:r, i, :], ACT.Square, accum_out=ss[:r, i:i + 1]).then_inc(s_ss, 1)
                    act.wait_ge(s_ss, i + 1)
                    act.activation(ss[:r, i:i + 1], ss[:r, i:i + 1], ACT.Sqrt, bias=K.eps[:r, 0:1], scale=1.0 / D).then_inc(s_std, 1)
                    if i >= 1:
                        out(i - 1)
                out(NT - 1)

            @block.vector
            def _(dve):
                step = Chain(dve, s_v)
                for n in range(8):
                    co, th = n // 2, n % 2
                    dve.wait_ge(s_sg, n + 1)
                    prompt = K.mixedT[:, co, 0:SEQ].rearrange("p (j t) -> p t j", t=CH)[:, th * 4:(th + 1) * 4, :]
                    ins = dve.tensor_tensor(prompt, yT[:, co, th * 4:(th + 1) * 4, 0:NJ], sg[:, n % 2, :, 0:NJ], ALU.mult)
                    if th == 0:
                        smp = K.mixedT[:, co, SEQ:T].rearrange("p (b t) -> p t b", t=DSEQ)
                        ins = dve.tensor_tensor(smp, yT[:, co, 0:DSEQ, NJ:COLS], sg[:, n % 2, :, NJ:COLS], ALU.mult)
                    ins.then_inc(s_gl, 1)
                for i in range(NT):
                    r = ROWS[i]
                    dve.wait_ge(s_om, i + 1)
                    dve.tensor_tensor(K.x[:r, i, :], K.x[:r, i, :], pp[:r, i % 2, :, :].rearrange("p a b -> p (a b)"),
                                      ALU.add).then_inc(s_h, 1)
                    dve.wait_ge(s_std, i + 1)
                    step(dve.reciprocal(ss[:r, i:i + 1], ss[:r, i:i + 1]))
                    dve.scalar_tensor_tensor(K.xn[:r, i, :], K.x[:r, i, :], ss[:r, i:i + 1], g2[:r, :], ALU.mult,
                                             ALU.mult).then_inc(s_xn, 1)


def route(nc, d, K):
    with Stage(nc, "route") as S:
        wq = S.sb("wq", [P, KD, PH * 256])
        keys = S.sb("keys", [P, 2, PK])
        qT = S.sb("qT", [P, 2 * PH, T])
        iota = S.sb("iota", [P, TOPK], BF16)
        iotaf = S.sb("iotaf", [P, TOPK])
        NH2 = 2 * PH
        val = S.sb("val", [P, NH2, TOPK])
        idx = S.sb("idx", [P, NH2, TOPK], U32)
        idxb = S.sb("idxb", [P, NH2, TOPK], BF16)
        left = S.sb("left", [P, 4, PK])
        cand = S.sb("cand", [P, PH, CAND])
        cleft = S.sb("cleft", [P, 4, CAND])
        top = S.sb("top", [P, PH, TOPK])
        pos = S.sb("pos", [P, SLOTS], U32)
        t32 = S.sb("t32", [P, SLOTS], U32)
        f = S.sb("f", [P, 5, SLOTS])
        rcb = S.sb("rcb", [P, 2, SLOTS], BF16)
        hot = S.sb("hot", [P, SLOTS, TOPK], BF16)
        pick = S.sb("pick", [P, SLOTS, TOPK], BF16)
        ex = S.sb("ex", [P, PH, TOPK])
        dn = S.sb("dn", [P, PH])
        pq = S.ps("pq", [P, 2, 512])
        pqs = S.ps("pqs", [P, 2, 512])
        psc = S.ps("psc", [P, 4, 512])

        s_wq = [S.sem(f"wq{k}_landed") for k in range(4)]
        s_keys = S.sem("keys_landed")
        s_qm = S.sem("queries_summed")
        s_qe = S.sem("queries_out")
        s_sc = S.sem("scores")
        s_sr = S.sem("scores_read")
        s_e = S.sem("exps")
        s_d = S.sem("differences")
        s_v = S.sem("dve_chain")

        with S.block() as block:
            @block.sync
            def _(sp):
                sp.dma_start(keys[:, :, :], d["keys"]).then_inc(s_keys, 16)
                sp.dma_start(iotaf[:, :], d["iota"]).then_inc(s_keys, 16)
                for q in range(4):
                    sp.dma_start(wq[:, :, q * 512:(q + 1) * 512], d["wq"][:, :, q * 512:(q + 1) * 512]).then_inc(s_wq[q], 16)

            @block.tensor
            def _(pe):
                for m in range(NH2):
                    if m % 4 == 0:
                        pe.wait_ge(s_wq[m // 4], 16)
                    if m >= 2:
                        pe.wait_ge(s_qe, m - 1)
                    for k in range(KD):
                        pe.matmul(pq[:, m % 2, :], wq[:, k, m * P:(m + 1) * P], K.xnT[:, k, 0:SEQ], start=(k == 0), stop=(k == KD - 1))
                        mm = pe.matmul(pqs[:, m % 2, 0:NSMP], wq[:, k, m * P:(m + 1) * P], K.xnT[:, k, SEQ:T],
                                       start=(k == 0), stop=(k == KD - 1))
                    mm.then_inc(s_qm, 1)
                pe.wait_ge(s_keys, 32)
                pe.wait_ge(s_qe, NH2)
                for i in range(NT):
                    r = ROWS[i]
                    for b in range(4):
                        n = i * 4 + b
                        if n >= 4:
                            pe.wait_ge(s_sr, n - 3)
                        for m in range(4):
                            hh = b * 4 + m
                            mm = pe.matmul(psc[:r, b, m * P:(m + 1) * P], qT[:, hh, i * P:i * P + r], keys[:, hh % 2, :],
                                           start=True, stop=True)
                        mm.then_inc(s_sc, 1)

            @block.scalar
            def _(act):
                for m in range(NH2):
                    act.wait_ge(s_qm, m + 1)
                    act.activation(qT[:, m, 0:SEQ], pq[:, m % 2, :], ACT.Copy)
                    act.activation(qT[:, m, SEQ:T], pqs[:, m % 2, 0:NSMP], ACT.Copy).then_inc(s_qe, 1)
                for i in range(NT):
                    r = ROWS[i]
                    act.wait_ge(s_d, i + 1)
                    act.activation(ex[:r, :, :], ex[:r, :, :], ACT.Exp).then_inc(s_e, 1)

            @block.vector
            def _(dve):
                step = Chain(dve, s_v)
                tt, ts = dve.tensor_tensor, dve.tensor_scalar
                dve.wait_ge(s_keys, 32)
                step(dve.tensor_copy(iota[:, :], iotaf[:, :]))
                for i in range(NT):
                    r = ROWS[i]
                    for b in range(4):
                        n = i * 4 + b
                        dve.wait_ge(s_sc, n + 1)
                        hh = [b * 4 + m for m in range(4)]
                        sc = [psc[:r, b, m * P:(m + 1) * P] for m in range(4)]
                        for m in range(4):
                            ins = dve.max(val[:r, hh[m], 0:8], sc[m])
                        step(ins)
                        for m in range(4):
                            dve.max_index(idx[:r, hh[m], 0:8], val[:r, hh[m], 0:8], sc[m])
                            ins = dve.match_replace(left[:r, m, :], val[:r, hh[m], 0:8], sc[m], -BIG)
                        ins.then_inc(s_sr, 1)
                        dve.wait_ge(s_sr, n + 1)
                        for m in range(4):
                            ins = dve.max(val[:r, hh[m], 8:16], left[:r, m, :])
                        step(ins)
                        for m in range(4):
                            ins = dve.max_index(idx[:r, hh[m], 8:16], val[:r, hh[m], 8:16], left[:r, m, :])
                        step(ins)
                    v = val[:r, :, :].rearrange("p (h e) k -> p h e k", e=2)
                    v1, v2 = v[:, :, 0, :], v[:, :, 1, :]
                    tt(cand[:r, :, 0:16], v2, v1[:, :, 0:1].broadcast_to([r, PH, 16]), ALU.add)
                    tt(cand[:r, :, 16:72].rearrange("p h (a b) -> p h a b", b=8), widen(v1[:, :, 1:8], 3, 8),
                       widen(v2[:, :, 0:8], 2, 7), ALU.add)
                    tt(cand[:r, :, 72:80], v1[:, :, 8:16], v2[:, :, 0:1].broadcast_to([r, PH, 8]), ALU.add)
                    step(dve.tensor_copy(idxb[:r, :, :], idx[:r, :, :]))
                    p8 = pos[:r, :].rearrange("p (h k) -> p h k", k=TOPK)
                    for b in range(2):
                        hs = range(b * 4, b * 4 + 4)
                        for h in hs:
                            ins = dve.max(top[:r, h, 0:8], cand[:r, h, :])
                        step(ins)
                        for h in hs:
                            dve.max_index(p8[:, h, 0:8], top[:r, h, 0:8], cand[:r, h, :])
                            ins = dve.match_replace(cleft[:r, h % 4, :], top[:r, h, 0:8], cand[:r, h, :], -BIG)
                        step(ins)
                        for h in hs:
                            ins = dve.max(top[:r, h, 8:16], cleft[:r, h % 4, :])
                        step(ins)
                        for h in hs:
                            ins = dve.max_index(p8[:, h, 8:16], top[:r, h, 8:16], cleft[:r, h % 4, :])
                        step(ins)
                    tt(ex[:r, :, :], top[:r, :, :], top[:r, :, 0:1].broadcast_to([r, PH, TOPK]), ALU.subtract).then_inc(s_d, 1)
                    F = [f[:r, n, :] for n in range(5)]
                    dve.tensor_copy(F[0], pos[:r, :])
                    step(ts(t32[:r, :], pos[:r, :], 56.0, None, ALU.add))
                    step(ts(t32[:r, :], t32[:r, :], 3, None, ALU.logical_shift_right))
                    step(dve.tensor_copy(F[1], t32[:r, :]))
                    step(ts(F[1], F[1], -8.0, 0.0, ALU.add, ALU.max))
                    step(dve.scalar_tensor_tensor(F[1], F[0], -64.0, F[1], ALU.add, ALU.max))
                    ts(F[2], F[1], 1.0, 8.0, ALU.min, ALU.mult)
                    step(dve.scalar_tensor_tensor(F[3], F[1], -8.0, F[0], ALU.mult, ALU.add))
                    step(tt(F[3], F[3], F[2], ALU.subtract))
                    dve.tensor_copy(rcb[:r, 0, :], F[1])
                    step(ts(rcb[:r, 1, :], F[3], 0.0, None, ALU.max))
                    ib = idxb[:r, :, :].rearrange("p (h e) k -> p h e k", e=2)
                    for e in range(2):
                        step(tt(hot[:r, :, :], widen(rcb[:r, e, :], 2, TOPK), widen(iota[:r, :], 1, SLOTS), ALU.is_equal))
                        step(tt(pick[:r, :, :].rearrange("p (h k) j -> p h k j", k=TOPK),
                                hot[:r, :, :].rearrange("p (h k) j -> p h k j", k=TOPK),
                                widen(ib[:, :, e, :], 2, TOPK), ALU.mult))
                        step(dve.tensor_reduce(F[e], pick[:r, :, :], AX.X, ALU.add))
                    dve.scalar_tensor_tensor(K.expert[:r, i, :], F[0], float(PK), F[1], ALU.mult, ALU.add)
                    dve.wait_ge(s_e, i + 1)
                    step(dve.tensor_reduce(dn[:r, :], ex[:r, :, :], AX.X, ALU.add))
                    step(dve.reciprocal(dn[:r, :], dn[:r, :]))
                    step(tt(K.gate[:r, i, :].rearrange("p (h k) -> p h k", k=TOPK), ex[:r, :, :], widen(dn[:r, :], 2, TOPK), ALU.mult))


def experts(nc, d, K):
    with Stage(nc, "peer") as S:
        RU, RV = 8, 16
        GRP = TOPK
        steps = [(i, s) for i in range(4) for s in range(SLOTS)] + [(4, s) for s in range(SLOTS // 4)]
        NS = len(steps)
        NG = NS // GRP
        U = S.sb("U", [P, RU, D])
        V = S.sb("V", [P, RV, D])
        dg = S.sb("dg", [P, 4, P])
        a = S.sb("a", [P, 2, GRP])
        ga = S.sb("ga", [P, 2, GRP])
        wt = S.sb("wt", [P, 2, GRP])
        ident4 = S.sb("ident4", [P, NSMP])
        xs = S.sb("xs", [P, D])
        es = S.sb("es", [P, SLOTS // 4], U32)
        gs = S.sb("gs", [P, SLOTS // 4])
        junk = S.sb("junk", [P, 2, D])
        acc = S.ps("acc", [P, 2, 2, 512])

        s_in = S.sem("sample_spread")
        s_u = [S.sem(f"u_landed{n}") for n in range(RU)]
        s_vv = [S.sem(f"v_landed{n}") for n in range(RV)]
        s_dot = S.sem("dots")
        s_ga = S.sem("gelus")
        s_wt = S.sem("weights")
        s_dg = S.sem("diagonals")
        s_mm = S.sem("summed")
        s_y = S.sem("result")
        s_out = S.sem("stored")

        def group(n):
            return steps[n][0]

        with S.block() as block:
            @block.sync
            def _(sp):
                sp.dma_start(ident4[:, :], d["ident4"]).then_inc(s_in, 16)
                for q in range(4):
                    t = slice(q * NSMP, (q + 1) * NSMP)
                    c = slice(q * (SLOTS // 4), (q + 1) * (SLOTS // 4))
                    sp.dma_start(xs[t, :], K.xn[0:NSMP, 4, :]).then_inc(s_in, 16)
                    sp.dma_start(es[t, :], K.expert[0:NSMP, 4, c]).then_inc(s_in, 16)
                    sp.dma_start(gs[t, :], K.gate[0:NSMP, 4, c]).then_inc(s_in, 16)
                for i in range(4):
                    sp.wait_ge(s_y, i + 1)
                    sp.dma_start(d["y_p"][i * P:(i + 1) * P, :], K.x[:, i, :]).then_inc(s_out, 16)
                sp.wait_ge(s_y, 5)
                sp.dma_start(d["y_s"], K.x[0:NSMP, 4, :]).then_inc(s_out, 16)
                sp.wait_ge(s_out, 80)

            @block.gpsimd
            def _(pool):
                LAG = GRP // 2

                def rows(n):
                    i, s = steps[n]
                    return K.expert[:, i, s:s + 1] if i < 4 else es[:, s:s + 1]

                pool.wait_ge(s_in, 16 * 13)
                for n in range(NS + LAG):
                    if n < NS:
                        if n >= RU:
                            pool.wait_ge(s_dot, n - RU + 1)
                        pool.indirect_dma_start(U[:, n % RU, :], None, d["peer_u"],
                                                bass.IndirectOffsetOnAxis(ap=rows(n), axis=0)).then_inc(s_u[n % RU], 16)
                    m = n - LAG
                    if m >= 0:
                        if m >= RV:
                            pool.wait_ge(s_mm, m - RV + 1)
                        pool.indirect_dma_start(V[:, m % RV, :], None, d["peer_v"],
                                                bass.IndirectOffsetOnAxis(ap=rows(m), axis=0)).then_inc(s_vv[m % RV], 16)

            @block.vector
            def _(dve):
                dve.wait_ge(s_in, 16 * 13)

                def weights(g):
                    i, s = steps[g * GRP]
                    gate = K.gate[:, i, s:s + GRP] if i < 4 else gs[:, s:s + GRP]
                    dve.wait_ge(s_ga, g + 1)
                    if g >= 2:
                        dve.wait_ge(s_dg, GRP * (g - 1))
                    dve.tensor_tensor(wt[:, g % 2, :], ga[:, g % 2, :], gate, ALU.mult).then_inc(s_wt, 1)

                def result(i):
                    r = ROWS[i]
                    dve.wait_ge(s_mm, min((i + 1) * SLOTS, NS))
                    dve.tensor_tensor(K.x[:r, i, :], K.x[:r, i, :], acc[:r, i % 2, :, :].rearrange("p a b -> p (a b)"),
                                      ALU.add).then_inc(s_y, 1)

                for n in range(NS):
                    i, s = steps[n]
                    g = n // GRP
                    if n % GRP == 0 and g >= 2:
                        dve.wait_ge(s_ga, g - 1)
                    if n % GRP == 1 and g >= 1:
                        weights(g - 1)
                    if i >= 1 and s == 2 * GRP - 1:
                        result(i - 1)
                    dve.wait_ge(s_u[n % RU], 16 * (n // RU + 1))
                    if n >= 2:
                        dve.wait_ge(s_dot, n - 1)
                    x = K.xn[:, i, :] if i < 4 else xs[:, :]
                    dve.tensor_tensor_reduce(junk[:, n % 2, :], U[:, n % RU, :], x, 1.0, 0.0, ALU.mult, ALU.add,
                                             a[:, g % 2, n % GRP:n % GRP + 1]).then_inc(s_dot, 1)
                weights(NG - 1)
                result(4)

            @block.scalar
            def _(act):
                for g in range(NG):
                    act.wait_ge(s_dot, GRP * (g + 1))
                    if g >= 2:
                        act.wait_ge(s_wt, g - 1)
                    act.activation(ga[:, g % 2, :], a[:, g % 2, :], ACT.Gelu).then_inc(s_ga, 1)
                    act.wait_ge(s_wt, g + 1)
                    for k in range(GRP):
                        n = g * GRP + k
                        if n >= 4:
                            act.wait_ge(s_mm, n - 3)
                        i = steps[n][0]
                        dst, src = (dg[:, n % 4, :], K.ident[:, :]) if i < 4 else (dg[:, n % 4, 0:NSMP], ident4[:, :])
                        act.activation(dst, src, ACT.Copy, scale=wt[:, g % 2, k:k + 1]).then_inc(s_dg, 1)

            @block.tensor
            def _(pe):
                for n in range(NS):
                    i, s = steps[n]
                    r = ROWS[i]
                    pe.wait_ge(s_dg, n + 1)
                    pe.wait_ge(s_vv[n % RV], 16 * (n // RV + 1))
                    if s == 0 and i >= 2:
                        pe.wait_ge(s_y, i - 1)
                    end = s == (SLOTS if i < 4 else SLOTS // 4) - 1
                    for c in range(2):
                        mm = pe.matmul(acc[:r, i % 2, c, :], dg[:, n % 4, 0:r], V[:, n % RV, c * 512:(c + 1) * 512],
                                       start=(s == 0), stop=end)
                    mm.then_inc(s_mm, 1)


class Kept:
    pass


def build(nc, d):
    K = Kept()
    with Stage(nc, "kept") as S:
        K.x = S.sb("x", [P, NT, D])
        K.ident = S.sb("ident", [P, P])
        K.eps = S.sb("eps", [P, 1])
        with Stage(nc, "mixing", "right") as M:
            K.mixedT = M.sb("mixedT", [P, KD, T])
            with Stage(nc, "heads", "right") as H:
                K.qkT = H.sb("qkT", [P, 5, T])
                K.v = H.sb("v", [P, NT, 128])
                K.mkT = H.sb("mkT", [P, 2, MEM])
                K.mv = H.sb("mv", [P, 2, 256])
                project(nc, d, K)
                attend(nc, d, K)
            K.y = M.sb("y", [NJ + 2 * NSEQ, CH, UW])
            ssm(nc, d, K)
            K.xn = S.sb("xn", [P, NT, D])
            K.expert = S.sb("expert", [P, NT, SLOTS], U32)
            K.gate = S.sb("gate", [P, NT, SLOTS])
            R = Stage(nc, "routing").__enter__()
            K.xnT = R.sb("xnT", [P, KD, T])
            mix(nc, d, K)
        route(nc, d, K)
        R.__exit__(None, None, None)
        experts(nc, d, K)


def constants():
    half = HD // 2
    inv = (10000.0 ** (-np.arange(half, dtype=np.float32) / half)).astype(np.float32)
    pos = np.concatenate([np.arange(SEQ), np.tile(2048 + np.arange(DSEQ), NSEQ)]).astype(np.float32)
    ang = pos[:, None] * inv[None, :]
    rope = np.zeros((P, NT, 2, HD), np.float32)
    for i in range(NT):
        a = ang[i * P:i * P + ROWS[i]]
        rope[:ROWS[i], i, 0] = np.concatenate([np.cos(a), np.cos(a)], 1)
        rope[:ROWS[i], i, 1] = np.concatenate([np.sin(a), np.sin(a)], 1)
    q, k = np.arange(P)[:, None], np.arange(256)[None, :] - 128
    mask = np.where((q - k >= 0) & (q - k < WIN), 0.0, -BIG).astype(np.float32)
    row = np.arange(P) % NSMP
    rb, rq = (row // DSEQ)[:, None], (row % DSEQ)[:, None]
    kb, kw = np.arange(NSEQ * WIN)[None, :] // WIN, np.arange(NSEQ * WIN)[None, :] % WIN
    old = np.where((rb == kb) & (kw > rq), 0.0, -BIG)
    nb, ns = np.arange(NSMP)[None, :] // DSEQ, np.arange(NSMP)[None, :] % DSEQ
    new = np.where((rb == nb) & (ns <= rq), 0.0, -BIG)
    return {
        "rope": rope,
        "mask": mask,
        "smask": np.concatenate([old, new], 1).astype(np.float32),
        "bmask": np.where(rb == np.arange(NSEQ)[None, :], 0.0, -BIG).astype(np.float32),
        "iota": np.tile(np.arange(TOPK, dtype=np.float32), (P, 1)),
        "ident": np.eye(P, dtype=np.float32),
        "ident4": np.tile(np.eye(NSMP, dtype=np.float32), (4, 1)),
    }


def layouts(i):
    A = {k: np.asarray(v) for k, v in i.items()}

    def chunked(w):
        return w.reshape(w.shape[0] // P, P, -1).transpose(1, 0, 2)

    x = np.concatenate([A["x_prompt"].reshape(SEQ, D), A["x_sample"].reshape(NSMP, D)])
    mem = A["mem_prompt"].reshape(MEM, D)
    w = A["w_in"][0]
    q = w[:, 512:768].reshape(D, 2, 2, HD).transpose(0, 2, 1, 3).reshape(D, 256)
    w = np.concatenate([w[:, :512], q, w[:, 768:896], w[:, 1024:1280], w[:, 896:1024]], 1)
    pair = lambda a: a.reshape(GP, 2, N).transpose(1, 2, 0).reshape(P, GP)
    pairc = lambda a: a.reshape(GP, 2, N, C).transpose(1, 2, 0, 3).reshape(P, GP, C)
    pairs = lambda a: a.reshape(NSEQ, GP, 2, N).transpose(2, 3, 1, 0).reshape(P, GP, NSEQ)
    cT = lambda a: a[0].transpose(0, 2, 1)
    sink = A["swa_sinks"][0].reshape(2, 2).T.reshape(4)
    ck, cv = A["cache_win_k"][0], A["cache_win_v"][0]
    mk, mv = A["cache_mem_k"][0], A["cache_mem_v"][0]
    gains = np.concatenate([np.tile(A["swa_q_norm"], (4, 1)), np.tile(A["swa_k_norm"], (2, 1)),
                            np.tile(A["mem_q_norm"], (4, 1)), np.tile(A["mem_k_norm"], (4, 1))])
    out = {
        "x_tok": x,
        "xT": chunked(x.T),
        "memT": chunked(mem.T),
        "mem_tok": mem.reshape(2, P, D).transpose(1, 0, 2),
        "w_in": chunked(w),
        "w_mem": chunked(A["w_mem_kv"][0]),
        "g1T": np.stack([A["norm1_g"][0].reshape(KD, P).T, A["mem_norm_g"][0].reshape(KD, P).T], 1),
        "gains": np.broadcast_to(gains, (P,) + gains.shape),
        "sinks": np.concatenate([np.broadcast_to(A["swa_sinks"][0], (P, 4)), np.repeat(sink, NSMP)[:, None]], 1),
        "cache_k": ck.reshape(NSEQ, WIN, 128),
        "cache_v": cv.reshape(NSEQ, WIN, 128),
        "kcT": ck.transpose(2, 3, 0, 1).reshape(P, NSEQ, WIN),
        "vc": cv.transpose(1, 0, 2, 3).reshape(P, NSEQ, 128),
        "mcT": mk.reshape(NSEQ, MEM, 2, 2, HD).transpose(3, 4, 2, 0, 1).reshape(P, 2, NSEQ, MEM),
        "mcv": mv.reshape(NSEQ, 2, P, 256).transpose(2, 1, 0, 3),
        "ssm_par": np.stack([pair(A["ssm_log_dt"][0]), pair(A["ssm_a_re"][0]), pair(A["ssm_a_im"][0])], 1),
        "ssm_bc": np.stack([pairc(A["ssm_b_re"][0]), pairc(A["ssm_b_im"][0]), pairc(cT(A["ssm_c_re"])),
                            pairc(cT(A["ssm_c_im"]))], 1),
        "ssm_d": A["ssm_d"][0].T,
        "ssm_s0": np.stack([pairs(A["state_ssm_re"][0]), pairs(A["state_ssm_im"][0])], 1),
        "w_glu": chunked(A["w_glu"][0]),
        "b_glu": A["b_glu"][0].reshape(4, P).T,
        "w_out": chunked(A["w_out"][0]),
        "g2": np.broadcast_to(A["norm2_g"][0], (P, D)),
        "wq": chunked(A["peer_wq"][0]),
        "keys": np.stack([A["peer_k1"][0].T, A["peer_k2"][0].T], 1),
        "peer_u": A["peer_u"][0],
        "peer_v": A["peer_v"][0],
    }
    out.update(constants())
    return {k: np.ascontiguousarray(v) for k, v in out.items()}


OUTS = {
    "y_p": (SEQ, D), "y_s": (NSMP, D), "p_ssm": (P, 2, GP), "s_ssm": (P, 2, GP, NSEQ),
    "p_win_k": (WIN, 128), "p_win_v": (WIN, 128), "p_mem_k": (MEM, 256), "p_mem_v": (MEM, 256),
    "s_win_k": (NSEQ, WIN, 128), "s_win_v": (NSEQ, WIN, 128),
}


def program(nc, arrays):
    d = {k: nc.dram_tensor(k, v.shape, mybir.dt.from_np(v.dtype), kind="ExternalInput").ap() for k, v in arrays.items()}
    for k, shape in OUTS.items():
        d[k] = nc.dram_tensor("out_" + k, shape, F32, kind="ExternalOutput").ap()
    d["u_scratch"] = nc.dram_tensor("u_scratch", (T, UW), F32, kind="Internal").ap()
    build(nc, d)


def returned(r):
    ps, ss = r["p_ssm"], r["s_ssm"]
    back = lambda a: a.reshape(2, N, GP).transpose(2, 0, 1).reshape(1, 1, G, N)
    backs = lambda a: a.reshape(2, N, GP, NSEQ).transpose(3, 2, 0, 1).reshape(1, NSEQ, G, N)
    return (r["y_p"].reshape(1, SEQ, D), r["y_s"].reshape(NSEQ, DSEQ, D),
            back(ps[:, 0]), back(ps[:, 1]),
            r["p_win_k"].reshape(1, 1, WIN, 2, HD), r["p_win_v"].reshape(1, 1, WIN, 2, HD),
            r["p_mem_k"].reshape(1, 1, MEM, 4, HD), r["p_mem_v"].reshape(1, 1, MEM, 4, HD),
            backs(ss[:, 0]), backs(ss[:, 1]),
            r["s_win_k"].reshape(1, NSEQ, WIN, 2, HD), r["s_win_v"].reshape(1, NSEQ, WIN, 2, HD))


def kernel(**inputs):
    import concourse.bacc as bacc
    from concourse.bass_utils import run_bass_kernel_spmd

    nc = bacc.Bacc("TRN2", target_bir_lowering=False, num_devices=1)
    arrays = layouts(inputs)
    program(nc, arrays)
    r = run_bass_kernel_spmd(nc, [arrays], core_ids=[0]).results[0]
    return returned({k: np.asarray(r["out_" + k]) for k in OUTS})
```

```python
from contextlib import ExitStack

import numpy as np

import concourse.bass as bass
from concourse import mybir
from concourse.alu_op_type import AluOpType as ALU

ACT = mybir.ActivationFunctionType
AX = mybir.AxisListType
F32 = mybir.dt.float32
BF16 = mybir.dt.bfloat16
U32 = mybir.dt.uint32

P = 128
D = 1024
KD = D // P
SEQ, NSEQ, DSEQ = 512, 8, 4
NSMP = NSEQ * DSEQ
T = SEQ + NSMP
NT = 5
ROWS = [P, P, P, P, NSMP]
HD = 64
EPS = 1e-6
WIN = 128
MEM = 256
G, N, C = 32, 64, 16
GP = G // 2
CH = 8
NJ = SEQ // CH
COLS = NJ + NSEQ
ROWH, ROWK = 6, 10
ZW = 768
UW = 512
PH, PK, TOPK = 8, 128, 16
CAND = 80
BIG = 3.0e38
SLOTS = PH * TOPK


class Chain:

    def __init__(self, eng, sem):
        self.eng, self.sem, self.n = eng, sem, 0

    def __call__(self, ins):
        self.n += 1
        ins.then_inc(self.sem, 1)
        self.eng.wait_ge(self.sem, self.n)


def widen(ap, axis, n):
    v = ap.unsqueeze(axis)
    shape = list(v.shape)
    shape[axis] = n
    return v.broadcast_to(shape)


class Stage:

    def __init__(self, nc, name, side="left"):
        self.nc, self.name, self.side, self.ctx = nc, name, side, ExitStack()

    def __enter__(self):
        self.ctx.__enter__()
        return self

    def __exit__(self, *a):
        return self.ctx.__exit__(*a)

    def sb(self, name, shape, dt=F32):
        return self.ctx.enter_context(self.nc.sbuf_tensor(f"sb_{self.name}_{name}", shape, dt, side=self.side))

    def ps(self, name, shape, dt=F32):
        return self.ctx.enter_context(self.nc.psum_tensor(f"sb_{self.name}_{name}", shape, dt))

    def sem(self, name):
        return self.ctx.enter_context(self.nc.semaphore(f"sb_{self.name}_{name}"))

    def block(self):
        return self.nc.Block()


def two_pi_parts():
    full = 2 * np.pi
    a = 6.28125
    b = float(np.floor((full - a) * 2 ** 20) / 2 ** 20)
    return a, b, float(np.float32(full - a - b))


def project(nc, d, K):
    par, bc, w, L, Lrev, bb, Q, W, A8 = K.par, K.bc, K.w, K.L, K.Lrev, K.bb, K.Q, K.W, K.A8
    with Stage(nc, "proj") as S:
        xT = S.sb("xT", [P, KD, T])
        w_in = S.sb("w_in", [P, KD, UW + ZW])
        memT = S.sb("memT", [P, KD, MEM])
        w_mem = S.sb("w_mem", [P, KD, 512])
        g1 = S.sb("g1", [P, 2, KD])
        gains = S.sb("gains", [P, ROWK + 4, HD])
        rope = S.sb("rope", [P, NT, 2, HD])
        square = S.sb("square", [P, D])
        x = S.sb("x", [P, 3, D])
        tmp = S.sb("tmp", [P, GP, CH + 1, C])
        NJOB = NT + 2
        ss = S.sb("ss", [P, NJOB])
        rstd = S.sb("rstd", [P, NJOB])
        z = S.sb("z", [P, 2, ZW])
        u = S.sb("u", [P, 2, UW])
        sq = S.sb("sq", [P, ROWK, HD])
        hs = S.sb("hs", [P, ROWK])
        hr = S.sb("hr", [P, ROWK])
        rc = S.sb("rc", [P, ROWH, HD])
        rs = S.sb("rs", [P, ROWH, HD])
        zn = S.sb("zn", [P, 4, ROWK * HD])
        pz = [S.ps(f"pz{i}", [P, 3 * 512]) for i in range(2)]
        pt = S.ps("pt", [P, 2 * 512])

        s_small = S.sem("small_landed")
        s_x = [S.sem(f"rows{j}_landed") for j in range(NJOB)]
        s_id = S.sem("ident_landed")
        s_par = S.sem("params_landed")
        s_ta = S.sem("tables_act")
        s_tv = S.sem("tables_dve")
        s_pw = S.sem("powers")
        s_pool = S.sem("pool_chain")
        s_k = [S.sem(f"k{k}_landed") for k in range(KD)]
        s_m = [S.sem(f"m{k}_landed") for k in range(2)]
        s_gain = S.sem("gained")
        s_ss = S.sem("squares")
        s_std = S.sem("std")
        s_rstd = S.sem("rstd")
        s_mm = S.sem("projected")
        s_z = S.sem("evacuated")
        s_u = [S.sem(f"u_stored{i}") for i in range(2)]
        s_hs = S.sem("head_squares")
        s_hq = S.sem("head_std")
        s_zn = S.sem("normed")
        s_t = S.sem("transposed")
        s_te = S.sem("transposes_out")
        s_out = S.sem("stored")
        s_v = S.sem("dve_chain")
        s_init = S.sem("init")

        rows = ROWS + [P, P]

        with S.block() as block:
            @block.sync
            def _(sp):
                sp.dma_start(K.ident[:, :], d["ident"]).then_inc(s_id, 16)
                sp.dma_start(g1[:, :, :], d["g1T"]).then_inc(s_small, 16)
                for k in range(KD):
                    sp.dma_start(xT[:, k, :], d["xT"][:, k, :]).then_inc(s_k[k], 16)
                    sp.dma_start(w_in[:, k, :], d["w_in"][:, k, :]).then_inc(s_k[k], 16)
                    if k == 3:
                        sp.dma_start(x[:, 0, :], d["x_tok"][0:P, :]).then_inc(s_x[0], 16)
                sp.dma_start(gains[:, :, :], d["gains"]).then_inc(s_small, 16)
                sp.dma_start(rope[:, :, :, :], d["rope"]).then_inc(s_small, 16)
                sp.dma_start(x[:, 1, :], d["x_tok"][P:2 * P, :]).then_inc(s_x[1], 16)
                sp.dma_start(x[:, 2, :], d["x_tok"][2 * P:3 * P, :]).then_inc(s_x[2], 16)
                sp.dma_start(memT[:, :, :], d["memT"]).then_inc(s_m[0], 16)
                sp.dma_start(w_mem[:, :, :], d["w_mem"]).then_inc(s_m[1], 16)
                for j in (3, 4):
                    sp.wait_ge(s_ss, j - 2)
                    sp.dma_start(x[:rows[j], j % 3, :], d["x_tok"][j * P:j * P + rows[j], :]).then_inc(s_x[j], 16)
                for j in range(NT):
                    sp.wait_ge(s_z, j + 1)
                    r = rows[j]
                    sp.dma_start(d["u_scratch"][j * P:j * P + r, :], u[:r, j % 2, :]).then_inc(s_u[j % 2], 16)
                    if j < 2:
                        sp.wait_ge(s_ss, j + 3)
                        sp.dma_start(x[:, (NT + j) % 3, :], d["mem_tok"][:, j, :]).then_inc(s_x[NT + j], 16)
                sp.wait_ge(s_zn, NT)
                sp.dma_start(d["p_win_k"], zn[:, 3, 256:384]).then_inc(s_out, 16)
                sp.dma_start(d["p_win_v"], K.v[:, 3, :]).then_inc(s_out, 16)
                for b in range(NSEQ):
                    q = slice(b * DSEQ, (b + 1) * DSEQ)
                    sp.dma_start(d["s_win_k"][b, WIN - DSEQ:, :], zn[q, 0, 256:384]).then_inc(s_out, 16)
                    sp.dma_start(d["s_win_v"][b, WIN - DSEQ:, :], K.v[q, 4, :]).then_inc(s_out, 16)
                sp.dma_start(d["s_win_k"][:, 0:WIN - DSEQ, :], d["cache_k"][:, DSEQ:, :]).then_inc(s_out, 16)
                sp.dma_start(d["s_win_v"][:, 0:WIN - DSEQ, :], d["cache_v"][:, DSEQ:, :]).then_inc(s_out, 16)
                sp.wait_ge(s_zn, NJOB)
                for m in range(2):
                    sp.dma_start(d["p_mem_k"][m * P:(m + 1) * P, :], zn[:, (NT + m) % 4, 0:256]).then_inc(s_out, 16)
                    sp.dma_start(d["p_mem_v"][m * P:(m + 1) * P, :], K.mv[:, m, :]).then_inc(s_out, 16)
                for i in range(2):
                    sp.wait_ge(s_u[i], 16 * (3 - i))
                sp.wait_ge(s_out, 16 * (2 + 2 * NSEQ + 2 + 4))

            @block.gpsimd
            def _(pool):
                tt = pool.tensor_tensor
                pool.dma_start(par[:, :, :], d["ssm_par"]).then_inc(s_par, 16)
                pool.dma_start(bc[:, :, :, :], d["ssm_bc"]).then_inc(s_par, 16)
                pool.dma_start(K.dsk[:, :], d["ssm_d"]).then_inc(s_par, 16)
                pool.dma_start(K.s0[:, :, :, :], d["ssm_s0"]).then_inc(s_par, 16)
                step = Chain(pool, s_pool)
                pool.wait_ge(s_pw, 1)
                lr = widen(Lrev[:, 0, :, :].rearrange("p t g -> p g t"), 3, C)
                li = widen(Lrev[:, 1, :, :].rearrange("p t g -> p g t"), 3, C)
                b_r, b_i = widen(bb[:, 0, :, :], 2, CH), widen(bb[:, 1, :, :], 2, CH)
                t1 = tmp[:, :, 0:CH, :]
                for n, (x0, y0, op) in enumerate(((b_r, b_i, ALU.subtract), (b_i, b_r, ALU.add))):
                    o = W[:, n, :, :, :]
                    tt(o, lr, x0, ALU.mult)
                    step(tt(t1, li, y0, ALU.mult))
                    step(tt(o, o, t1, op))
                lr = widen(L[:, 0, :, :].rearrange("p t g -> p g t"), 3, C)
                li = widen(L[:, 1, :, :].rearrange("p t g -> p g t"), 3, C)
                ln = widen(L[:, 2, :, :].rearrange("p t g -> p g t"), 3, C)
                c_r, c_i = widen(bc[:, 2, :, :], 2, CH + 1), widen(bc[:, 3, :, :], 2, CH + 1)
                for n, (x0, y0) in enumerate(((lr, li), (ln, lr))):
                    o = Q[:, n, :, :, :]
                    tt(o, c_r, x0, ALU.mult)
                    step(tt(tmp[:, :, :, :], c_i, y0, ALU.mult))
                    step(tt(o, o, tmp[:, :, :, :], ALU.subtract))

            @block.scalar
            def _(act):
                act.wait_ge(s_par, 64)
                act.activation(w[:, 0, :], par[:, 0, :], ACT.Exp).then_inc(s_ta, 1)
                act.wait_ge(s_tv, 1)
                act.activation(w[:, 3, :], w[:, 1, :], ACT.Exp).then_inc(s_ta, 1)
                act.wait_ge(s_tv, 2)
                act.activation(w[:, 6:8, :], w[:, 4:6, :], ACT.Sin).then_inc(s_ta, 1)

                def row_norm(j):
                    r = rows[j]
                    src = x[:r, j % 3, :]
                    act.wait_ge(s_x[j], 16)
                    act.activation(square[:r, :], src, ACT.Square, accum_out=ss[:r, j:j + 1]).then_inc(s_ss, 1)
                    act.wait_ge(s_ss, j + 1)
                    act.activation(rstd[:r, j:j + 1], ss[:r, j:j + 1], ACT.Sqrt, bias=K.eps[:r, 0:1],
                                   scale=1.0 / D).then_inc(s_std, 1)

                def out_of_transposes(j):
                    act.wait_ge(s_t, j + 1)
                    r = rows[j]
                    if j < NT:
                        act.activation(K.qkT[:, :, j * P:j * P + r], pt[:, 0:5 * P].rearrange("p (c t) -> p c t", t=P)[:, :, :r],
                                       ACT.Copy).then_inc(s_te, 1)
                    else:
                        m = j - NT
                        act.activation(K.mkT[:, :, m * P:(m + 1) * P], pt[:, 0:2 * P].rearrange("p (c t) -> p c t", t=P),
                                       ACT.Copy).then_inc(s_te, 1)

                act.wait_ge(s_init, 1)
                row_norm(0)
                for j in range(NJOB):
                    r = rows[j]
                    if j + 1 < NJOB:
                        row_norm(j + 1)
                    act.wait_ge(s_rstd, j + 1)
                    act.wait_ge(s_mm, j + 1)
                    if j >= 2:
                        act.wait_ge(s_zn, j - 1)
                        if j < NT:
                            act.wait_ge(s_u[j % 2], 16 * (j // 2))
                    if j < NT:
                        act.activation(u[:r, j % 2, :], pz[j % 2][:r, 0:UW], ACT.Copy, scale=rstd[:r, j:j + 1])
                        act.activation(K.v[:r, j, :], pz[j % 2][:r, UW + 640:UW + ZW], ACT.Copy, scale=rstd[:r, j:j + 1])
                        act.activation(z[:r, j % 2, 0:640], pz[j % 2][:r, UW:UW + 640], ACT.Copy,
                                       scale=rstd[:r, j:j + 1]).then_inc(s_z, 1)
                    else:
                        act.activation(K.mv[:, j - NT, :], pz[j % 2][:, 256:512], ACT.Copy, scale=rstd[:, j:j + 1])
                        act.activation(z[:, j % 2, 0:256], pz[j % 2][:, 0:256], ACT.Copy,
                                       scale=rstd[:, j:j + 1]).then_inc(s_z, 1)
                    nh = ROWK if j < NT else 4
                    act.wait_ge(s_hs, j + 1)
                    act.activation(hr[:r, :nh], hs[:r, :nh], ACT.Sqrt, bias=K.eps[:r, 0:1], scale=1.0 / HD).then_inc(s_hq, 1)
                    if j >= 1:
                        out_of_transposes(j - 1)
                out_of_transposes(NJOB - 1)

            @block.vector
            def _(dve):
                step = Chain(dve, s_v)
                tt = dve.tensor_tensor
                dve.memset(L[:, 0, 0, :], 1.0)
                dve.memset(L[:, 1:3, 0, :], 0.0)
                dve.memset(K.eps[:, :], EPS).then_inc(s_init, 1)
                dve.wait_ge(s_small, 16)
                for k in range(KD):
                    dve.wait_ge(s_k[k], 32)
                    dve.tensor_scalar(xT[:, k, :], xT[:, k, :], g1[:, 0, k:k + 1], None, ALU.mult).then_inc(s_gain, 1)
                dve.wait_ge(s_par, 64)
                dve.wait_ge(s_ta, 1)
                tt(w[:, 1, :], par[:, 1, :], w[:, 0, :], ALU.mult).then_inc(s_tv, 1)
                step(tt(w[:, 2, :], par[:, 2, :], w[:, 0, :], ALU.mult))
                a, b, c = two_pi_parts()
                for n, quarter in enumerate((0.0, 0.25)):
                    k = w[:, 8 + n, :]
                    step(dve.tensor_scalar(k, w[:, 2, :], float(1 / (2 * np.pi)), quarter, ALU.mult, ALU.add))
                    step(dve.tensor_scalar(k, k, 12582912.0, None, ALU.add))
                    step(dve.tensor_scalar(k, k, -12582912.0, None, ALU.add))
                    r = w[:, 4 + n, :]
                    step(dve.scalar_tensor_tensor(r, k, -a, w[:, 2, :], ALU.mult, ALU.add))
                    step(dve.scalar_tensor_tensor(r, k, -b, r, ALU.mult, ALU.add))
                    step(dve.scalar_tensor_tensor(r, k, -c, r, ALU.mult, ALU.add))
                    if n:
                        step(dve.tensor_scalar(r, r, float(np.pi / 2), None, ALU.add))
                    ins = dve.tensor_scalar(r, r, 3.1415925, -3.1415925, ALU.min, ALU.max)
                    if n:
                        ins.then_inc(s_tv, 1)
                    else:
                        step(ins)
                dve.wait_ge(s_std, 1)
                dve.reciprocal(rstd[:, 0:1], rstd[:, 0:1]).then_inc(s_rstd, 1)
                dve.wait_ge(s_ta, 3)
                tt(L[:, 0, 1, :], w[:, 3, :], w[:, 7, :], ALU.mult)
                step(tt(L[:, 1, 1, :], w[:, 3, :], w[:, 6, :], ALU.mult))
                ar, ai = par[:, 1, :], par[:, 2, :]
                step(dve.tensor_scalar(w[:, 10, :], L[:, 0, 1, :], 1.0, None, ALU.subtract))
                lm, li = w[:, 10, :], L[:, 1, 1, :]
                tt(w[:, 11, :], ar, ar, ALU.mult)
                tt(w[:, 12, :], ai, ai, ALU.mult)
                tt(w[:, 13, :], lm, ar, ALU.mult)
                tt(w[:, 14, :], li, ai, ALU.mult)
                tt(w[:, 15, :], li, ar, ALU.mult)
                step(tt(w[:, 16, :], lm, ai, ALU.mult))
                tt(w[:, 11, :], w[:, 11, :], w[:, 12, :], ALU.add)
                tt(w[:, 13, :], w[:, 13, :], w[:, 14, :], ALU.add)
                step(tt(w[:, 15, :], w[:, 15, :], w[:, 16, :], ALU.subtract))
                step(dve.reciprocal(w[:, 11, :], w[:, 11, :]))
                tt(w[:, 17, :], w[:, 13, :], w[:, 11, :], ALU.mult)
                step(tt(w[:, 18, :], w[:, 15, :], w[:, 11, :], ALU.mult))
                zr, zi = widen(w[:, 17, :], 2, C), widen(w[:, 18, :], 2, C)
                t4 = [tmp[:, :, n, :] for n in range(4)]
                br, bi = bc[:, 0, :, :], bc[:, 1, :, :]
                tt(t4[0], zr, br, ALU.mult)
                tt(t4[1], zi, bi, ALU.mult)
                tt(t4[2], zr, bi, ALU.mult)
                step(tt(t4[3], zi, br, ALU.mult))
                tt(bb[:, 0, :, :], t4[0], t4[1], ALU.subtract)
                step(tt(bb[:, 1, :, :], t4[2], t4[3], ALU.add))
                for m in (1, 2, 4):
                    lo, hi = slice(1, m + 1), slice(m + 1, 2 * m + 1)
                    mr, mi = widen(L[:, 0, m, :], 1, m), widen(L[:, 1, m, :], 1, m)
                    q = [tmp[:, 4 * n:4 * n + m, 0, :] for n in range(4)]
                    tt(q[0], L[:, 0, lo, :], mr, ALU.mult)
                    tt(q[1], L[:, 1, lo, :], mi, ALU.mult)
                    tt(q[2], L[:, 0, lo, :], mi, ALU.mult)
                    step(tt(q[3], L[:, 1, lo, :], mr, ALU.mult))
                    tt(L[:, 0, hi, :], q[0], q[1], ALU.subtract)
                    step(tt(L[:, 1, hi, :], q[2], q[3], ALU.add))
                dve.tensor_scalar(L[:, 2, 1:, :], L[:, 1, 1:, :], -1.0, None, ALU.mult)
                for t in range(CH):
                    ins = dve.tensor_copy(Lrev[:, :, t, :], L[:, 0:2, CH - 1 - t, :])
                step(ins)
                for o in range(2):
                    dve.tensor_copy(A8[:, o, o, :], L[:, 0, CH, :])
                dve.tensor_copy(A8[:, 0, 1, :], L[:, 2, CH, :])
                dve.tensor_copy(A8[:, 1, 0, :], L[:, 1, CH, :]).then_inc(s_pw, 1)
                dve.wait_ge(s_small, 48)
                dve.wait_ge(s_m[0], 16)
                for k in range(KD):
                    dve.tensor_scalar(memT[:, k, :], memT[:, k, :], g1[:, 1, k:k + 1], None, ALU.mult).then_inc(s_gain, 1)

                def rstd_of(j):
                    dve.wait_ge(s_std, j + 1)
                    dve.reciprocal(rstd[:rows[j], j:j + 1], rstd[:rows[j], j:j + 1]).then_inc(s_rstd, 1)

                for j in range(NJOB):
                    r = rows[j]
                    nh = ROWK if j < NT else 4
                    g0 = 0 if j < NT else ROWK
                    zj = z[:r, j % 2, 0:nh * HD].rearrange("p (h c) -> p h c", c=HD)
                    if j + 1 < NJOB:
                        rstd_of(j + 1)
                    if j >= 4:
                        dve.wait_ge(s_t, j - 3)
                    out = zn[:r, j % 4, 0:nh * HD].rearrange("p (h c) -> p h c", c=HD)
                    dve.wait_ge(s_z, j + 1)
                    step(dve.tensor_tensor(sq[:r, :nh, :], zj, zj, ALU.mult))
                    dve.tensor_reduce(hs[:r, :nh], sq[:r, :nh, :], AX.X, ALU.add).then_inc(s_hs, 1)
                    dve.wait_ge(s_hq, j + 1)
                    step(dve.reciprocal(hr[:r, :nh], hr[:r, :nh]))
                    step(dve.tensor_tensor(out, zj, widen(hr[:r, :nh], 2, HD), ALU.mult))
                    last = dve.tensor_tensor(out, out, gains[:r, g0:g0 + nh, :], ALU.mult)
                    if j < NT:
                        step(last)
                        rot = out[:, 0:ROWH, :]
                        dve.tensor_tensor(rc[:r, :, :], rot, widen(rope[:r, j, 0, :], 1, ROWH), ALU.mult)
                        step(dve.tensor_tensor(rs[:r, :, :], rot, widen(rope[:r, j, 1, :], 1, ROWH), ALU.mult))
                        h = HD // 2
                        dve.tensor_tensor(rot[:, :, 0:h], rc[:r, :, 0:h], rs[:r, :, h:HD], ALU.subtract)
                        last = dve.tensor_tensor(rot[:, :, h:HD], rc[:r, :, h:HD], rs[:r, :, 0:h], ALU.add)
                    last.then_inc(s_zn, 1)

            @block.tensor
            def _(pe):
                def transposes(j):
                    r = rows[j]
                    pe.wait_ge(s_zn, j + 1)
                    if j >= 1:
                        pe.wait_ge(s_te, j)
                    for c in range(5 if j < NT else 2):
                        mm = pe.transpose(pt[:, c * P:c * P + r], zn[:r, j % 4, c * P:(c + 1) * P], K.ident[:r, :r])
                    mm.then_inc(s_t, 1)

                pe.wait_ge(s_id, 16)
                for j in range(NJOB):
                    r = rows[j]
                    if j >= 2:
                        pe.wait_ge(s_z, j - 1)
                    if j >= NT:
                        pe.wait_ge(s_m[1], 16)
                        pe.wait_ge(s_gain, 2 * KD)
                    for k in range(KD):
                        if j == 0:
                            pe.wait_ge(s_k[k], 32)
                            pe.wait_ge(s_gain, k + 1)
                        if j < NT:
                            for c in range(0, UW + ZW, 512):
                                w = min(512, UW + ZW - c)
                                mm = pe.matmul(pz[j % 2][:r, c:c + w], xT[:, k, j * P:j * P + r], w_in[:, k, c:c + w],
                                               start=(k == 0), stop=(k == KD - 1))
                        else:
                            m = j - NT
                            mm = pe.matmul(pz[j % 2][:, 0:512], memT[:, k, m * P:(m + 1) * P], w_mem[:, k, :],
                                           start=(k == 0), stop=(k == KD - 1))
                    mm.then_inc(s_mm, 1)
                    if j >= 1:
                        transposes(j - 1)
                transposes(NJOB - 1)


def blend(nc, d, K):
    NC = NJ + 2 * NSEQ
    L, bb, Q, W, A8, s0 = K.L, K.bb, K.Q, K.W, K.A8, K.s0
    with Stage(nc, "blend") as S:
        uch = S.sb("uch", [P, CH, UW])
        ZK = S.sb("ZK", [P, G, (CH - 1) * C + P])
        dI = S.sb("dI", [C, G, C])
        MT = S.sb("MT", [P, G, P])
        WT = S.sb("WT", [P, 2, GP, P])
        U = S.sb("U", [P, G, NC])
        V = S.sb("V", [P, 2, GP, NC])
        prod = S.sb("prod", [P, 2, 2, GP])
        part = S.sb("part", [P, 2, GP])
        fin = S.sb("fin", [P, 2, GP])
        sfin = S.sb("sfin", [P, 2, GP, NSEQ])
        st = S.sb("st", [P, 2, GP, NSEQ])
        mask = S.sb("mask", [P, 256])
        bmask = S.sb("bmask", [P, NSEQ])
        sinks = S.sb("sinks", [P, 5])
        flat = lambda t, spec: t.rearrange("p " + spec + " -> p (" + spec + ")")
        SPv = flat(W[:, :, :, :, :], "a g t c")[:, 0:2 * GP * COLS].rearrange("p (r g j) -> p r g j", r=2, g=GP)
        mcT = flat(uch[:, :, :], "t c").rearrange("p (a b m) -> p a b m", a=2, b=NSEQ)
        mcv = flat(WT[:, :, :, :], "r g x").rearrange("p (a b m) -> p a b m", a=2, b=NSEQ)
        soft = flat(ZK[:, :, :], "g x")
        sm, pr, prT = (soft[:, 2048 * n:2048 * (n + 1)].rearrange("p (a x) -> p a x", a=2) for n in range(3))
        smask = soft[:, 6144:6144 + NSEQ * WIN + NSMP]
        yroom = flat(K.y[:, :, :], "t c")
        ug = yroom[0:NC, :].rearrange("p (g x) -> p g x", g=G)
        big = yroom[:, 0:2048]
        kcT = yroom[:, 2048:3072].rearrange("p (b w) -> p b w", b=NSEQ)
        vc = yroom[:, 3072:4096].rearrange("p (b w) -> p b w", b=NSEQ)
        mx = S.sb("mx", [P, 2, 4])
        nm = S.sb("nm", [P, 2, 4])
        den = S.sb("den", [P, 2, 4])
        es = S.sb("es", [P, 2, 4])
        pp = S.ps("pp", [P, 8, 512])
        banks = pp[:, :, :].rearrange("p b x -> p (b x)")
        sc, tp = banks[:, 0:2048], banks[:, 2048:3072]
        ov = pp[:, 6:8, :]

        s_mask = S.sem("masks_landed")
        s_cache = S.sem("caches_landed")
        s_sc = S.sem("scores")
        s_sm = S.sem("scores_read")
        s_mx = S.sem("maxima")
        s_ex = S.sem("exps")
        s_pr = S.sem("probs")
        s_tp = S.sem("probs_turned")
        s_te = S.sem("turned_out")
        s_ov = S.sem("values")
        s_oe = S.sem("values_out")

        s_smask = S.sem("sample_mask_landed")
        s_ug = S.sem("chunks_grouped")
        s_uch = S.sem("chunks_landed")
        s_mt = S.sem("toeplitz_landed")
        s_v = S.sem("dve_chain")
        s_g = S.sem("pool_chain")
        s_uz = S.sem("uch_zeroed")
        s_ut = S.sem("u_turned")
        s_ue = S.sem("u_out")
        s_wt = S.sem("w_turned")
        s_we = S.sem("w_out")
        s_kt = S.sem("kernels")
        s_ke = S.sem("kernels_out")
        s_z = S.sem("kernels_ready")
        s_vm = S.sem("inputs_summed")
        s_ve = S.sem("inputs_out")
        s_scan = S.sem("scanned")
        s_ym = S.sem("y_summed")
        s_ye = S.sem("y_out")
        s_sf = S.sem("sample_state")
        s_out = S.sem("stored")


        units = [("win", i) for i in range(4)] + [("mem", i) for i in range(4)] + [("swin", 4), ("smem", 4)]
        NU = len(units)

        def shape(kind, i):
            if kind == "win":
                return 4, 256, (128 if i == 0 else 0)
            if kind == "mem":
                return 4, 256, 0
            if kind == "swin":
                return 1, WIN + NSMP, 0
            return 1, 256, 0

        def probs(buf, kind, i, n):
            h, w, lo = shape(kind, i)
            if h == 4:
                return buf[:, n % 2, :].rearrange("p (h k) -> p h k", h=4)[:, :, lo:]
            return buf[:, n % 2, 0:w].unsqueeze(1)

        UB, VB = 6, 3
        ub = [range(i, min(i + UB, G)) for i in range(0, G, UB)]
        vb = [range(i, min(i + VB, GP)) for i in range(0, GP, VB)]

        with S.block() as block:
            @block.sync
            def _(sp):
                us = d["u_scratch"]
                smp = us[SEQ:T, :].rearrange("(b t) c -> b t c", t=DSEQ)
                sp.dma_start(uch[0:NJ, :, :], us[0:SEQ, :].rearrange("(j t) c -> j t c", t=CH)).then_inc(s_uch, 16)
                sp.wait_ge(s_uz, 1)
                sp.dma_start(uch[NJ:NJ + NSEQ, 0:DSEQ, :], smp).then_inc(s_uch, 16)
                sp.dma_start(uch[NJ + NSEQ:NC, DSEQ:CH, :], smp).then_inc(s_uch, 16)
                sp.dma_start(mask[:, :], d["mask"]).then_inc(s_mask, 16)
                sp.dma_start(sinks[:, :], d["sinks"]).then_inc(s_mask, 16)
                sp.dma_start(bmask[:, :], d["bmask"]).then_inc(s_mask, 16)
                sp.wait_ge(s_z, 1)
                for t in range(CH):
                    o = (CH - 1 - t) * C
                    sp.dma_start(MT[t * C:(t + 1) * C, :, :], ZK[0:C, :, o:o + P]).then_inc(s_mt, 16)
                sp.wait_ge(s_ug, 1)
                sp.dma_start(mcT, d["mcT"]).then_inc(s_cache, 16)
                sp.wait_ge(s_ut, len(ub))
                sp.dma_start(kcT, d["kcT"]).then_inc(s_cache, 16)
                sp.dma_start(vc, d["vc"]).then_inc(s_cache, 16)
                sp.wait_ge(s_mt, 16 * CH)
                sp.dma_start(smask, d["smask"]).then_inc(s_smask, 16)
                sp.wait_ge(s_vm, len(vb))
                sp.dma_start(mcv, d["mcv"]).then_inc(s_cache, 16)
                sp.wait_ge(s_scan, 1)
                sp.dma_start(d["p_ssm"], fin[:, :, :]).then_inc(s_out, 16)
                sp.wait_ge(s_sf, 1)
                sp.dma_start(d["s_ssm"], sfin[:, :, :, :]).then_inc(s_out, 16)
                sp.wait_ge(s_out, 32)

            @block.gpsimd
            def _(pool):
                n = 0
                pool.memset(uch[NJ:NC, :, :], 0.0).then_inc(s_uz, 1)
                pool.wait_ge(s_uz, 1)
                pool.wait_ge(s_wt, 8)
                pool.tensor_copy(SPv[:, :, :, NJ:COLS], s0[:, :, :, :])
                pool.memset(SPv[:, :, :, 0:1], 0.0).then_inc(s_g, 1)
                n += 1
                pool.wait_ge(s_ve, len(vb))
                for j in range(NJ):
                    pool.wait_ge(s_g, n)
                    pool.tensor_tensor(prod[:, :, :, :], A8[:, :, :, :], widen(SPv[:, :, :, j], 1, 2), ALU.mult).then_inc(s_g, 1)
                    n += 1
                    pool.wait_ge(s_g, n)
                    pool.tensor_tensor(part[:, :, :], prod[:, :, 0, :], prod[:, :, 1, :], ALU.add).then_inc(s_g, 1)
                    n += 1
                    pool.wait_ge(s_g, n)
                    dst = SPv[:, :, :, j + 1] if j + 1 < NJ else fin[:, :, :]
                    pool.tensor_tensor(dst, part[:, :, :], V[:, :, :, j], ALU.add).then_inc(s_g, 1)
                    n += 1
                pool.wait_ge(s_g, n)
                pool.engine_nop().then_inc(s_scan, 1)

            @block.tensor
            def _(pe):
                def scores(n):
                    kind, i = units[n]
                    at = (n % 2) * 1024
                    if n >= 2:
                        pe.wait_ge(s_sm, n - 1)
                    if kind in ("swin", "smem"):
                        pe.wait_ge(s_sm, n)
                        pe.wait_ge(s_cache, 64)
                    tok = slice(i * P, i * P + ROWS[i])
                    for h in range(4):
                        lo, hi = (h % 2) * HD, (h % 2) * HD + HD
                        slot = (h % 2) * 2 + h // 2
                        if kind == "win":
                            a = 128 if i == 0 else 0
                            mm = pe.matmul(sc[:, at + slot * 256 + a:at + slot * 256 + 256], K.qkT[lo:hi, h // 2, tok],
                                           K.qkT[lo:hi, 2, (i - 1) * P + a:(i + 1) * P], start=True, stop=True)
                        elif kind == "mem":
                            mm = pe.matmul(sc[:, at + slot * 256:at + slot * 256 + 256], K.qkT[lo:hi, 3 + h // 2, tok],
                                           K.mkT[lo:hi, h // 2, :], start=True, stop=True)
                        elif kind == "swin":
                            for c in range(2):
                                pe.matmul(sc[h * 32:h * 32 + 32, c * 512:(c + 1) * 512], K.qkT[lo:hi, h // 2, tok],
                                          kcT[lo:hi, c * 4:(c + 1) * 4, :], start=True, stop=True)
                            mm = pe.matmul(sc[h * 32:h * 32 + 32, 1024:1024 + NSMP], K.qkT[lo:hi, h // 2, tok],
                                           K.qkT[lo:hi, 2, SEQ:T], start=True, stop=True)
                        else:
                            for c in range(4):
                                mm = pe.matmul(sc[h * 32:h * 32 + 32, c * 512:(c + 1) * 512], K.qkT[lo:hi, 3 + h // 2, tok],
                                               mcT[lo:hi, h // 2, c * 2:(c + 1) * 2, :], start=True, stop=True)
                    mm.then_inc(s_sc, 1)

                def turn(n):
                    kind, i = units[n]
                    h, w, lo = shape(kind, i)
                    pe.wait_ge(s_pr, n + 1)
                    if n >= 1:
                        pe.wait_ge(s_te, n)
                    if h == 4:
                        for x in range(4):
                            for m in range(lo // 128, 2):
                                mm = pe.transpose(tp[:, (2 * x + m) * P:(2 * x + m + 1) * P],
                                                  pr[:, n % 2, x * 256 + m * P:x * 256 + (m + 1) * P], K.ident[:, :])
                    else:
                        pe.transpose(tp[:, 0:P], pr[:, n % 2, 0:P], K.ident[:, :])
                        mm = pe.transpose(tp[0:w - P, P:2 * P], pr[:, n % 2, P:w], K.ident[:, :])
                    mm.then_inc(s_tp, 1)

                def values(n):
                    kind, i = units[n]
                    pe.wait_ge(s_te, n + 1)
                    if n >= 2:
                        pe.wait_ge(s_oe, n - 1)
                    o = ov[:, n % 2, 0:256].rearrange("p (c q) -> p c q", c=2)
                    pT = prT[:, n % 2, :]
                    for h in range(4):
                        for m in range(2):
                            cols = slice((2 * h + m) * P, (2 * h + m + 1) * P)
                            if kind == "win":
                                kv, r = h // 2, h % 2
                                if i == 0 and m == 0:
                                    continue
                                mm = pe.matmul(o[r * HD:r * HD + HD, kv, :], K.v[:, i - 1 + m, kv * HD:kv * HD + HD],
                                               pT[:, cols], start=(m == 0 or i == 0), stop=(m == 1))
                            elif kind == "mem":
                                hp, c = h // 2, h % 2
                                x = c * 2 + hp
                                mm = pe.matmul(o[hp * HD:hp * HD + HD, c, :], K.mv[:, m, x * HD:x * HD + HD],
                                               pT[:, cols], start=(m == 0), stop=(m == 1))
                        if kind == "swin":
                            r, kv = h // 2, h % 2
                            dst = o[r * HD:r * HD + HD, kv, :]
                            pe.matmul(dst[:, 0:NSMP], K.v[0:NSMP, 4, kv * HD:kv * HD + HD],
                                      pT[0:NSMP, P + h * 32:P + h * 32 + 32], start=True, stop=False)
                            for b in range(NSEQ):
                                q = slice(b * DSEQ, (b + 1) * DSEQ)
                                mm = pe.matmul(dst[:, q], vc[:, b, kv * HD:kv * HD + HD],
                                               pT[:, h * 32 + b * DSEQ:h * 32 + (b + 1) * DSEQ],
                                               start=False, stop=(b == NSEQ - 1))
                        elif kind == "smem":
                            hp = h % 2
                            for b in range(NSEQ):
                                q = slice(b * DSEQ, (b + 1) * DSEQ)
                                for m in range(2):
                                    mm = pe.matmul(o[hp * HD:hp * HD + HD, h // 2, q], mcv[:, m, b, h * HD:h * HD + HD],
                                                   pT[:, m * P + h * 32 + b * DSEQ:m * P + h * 32 + (b + 1) * DSEQ],
                                                   start=(m == 0), stop=(m == 1))
                    mm.then_inc(s_ov, 1)

                for n in range(8):
                    for m in range(4):
                        mm = pe.transpose(pp[:, n, m * P:(m + 1) * P],
                                          W[:, n // 4, (n % 4) * 4 + m, :, :].rearrange("p t c -> p (t c)"), K.ident[:, :])
                    mm.then_inc(s_wt, 1)
                for n in range(8):
                    pe.wait_ge(s_we, n + 1)
                    for m in range(4):
                        g = (n // 2) * 8 + 2 * m + n % 2
                        h = slice((g % 2) * N, (g % 2) * N + N)
                        for ri in range(2):
                            mm = pe.matmul(pp[0:C, n, m * P:(m + 1) * P], bb[h, ri, g // 2, :], Q[h, ri, g // 2, 0:CH, :],
                                           start=(ri == 0), stop=(ri == 1))
                    mm.then_inc(s_kt, 1)
                pe.wait_ge(s_ug, 1)
                for n, gs in enumerate(ub):
                    pe.wait_ge(s_ke, n + 1)
                    for m, g in enumerate(gs):
                        mm = pe.transpose(pp[:, n, m * NC:(m + 1) * NC], ug[:, g, :], K.ident[:NC, :NC])
                    mm.then_inc(s_ut, 1)
                for n, gs in enumerate(vb):
                    pe.wait_ge(s_ue, min(n + 1, len(ub)))
                    for m, gp in enumerate(gs):
                        for e in range(2):
                            h = slice(e * N, e * N + N)
                            for ri in range(2):
                                mm = pe.matmul(pp[h, n, (m * 2 + ri) * NC:(m * 2 + ri + 1) * NC], WT[:, ri, gp, h],
                                               U[:, gp * 2 + e, :], start=True, stop=True)
                    mm.then_inc(s_vm, 1)
                pe.wait_ge(s_ke, 8)
                pe.wait_ge(s_ve, len(vb))
                scores(0)
                scores(1)
                turn(0)
                for n in range(NU):
                    if n + 2 < NU:
                        scores(n + 2)
                    if n + 1 < NU:
                        turn(n + 1)
                    values(n)
                pe.wait_ge(s_oe, NU)
                pe.wait_ge(s_mt, 16 * CH)
                pe.wait_ge(s_scan, 1)
                for n in range(8):
                    for m in range(4):
                        g = (n // 2) * 8 + 2 * m + n % 2
                        h = slice((g % 2) * N, (g % 2) * N + N)
                        o = pp[0:COLS, n, m * P:(m + 1) * P]
                        pe.matmul(o, U[:, g, 0:COLS], MT[:, g, :], start=True, stop=False)
                        for ri in range(2):
                            mm = pe.matmul(o, SPv[h, ri, g // 2, :], Q[h, ri, g // 2, 1:CH + 1, :], start=False, stop=(ri == 1))
                    mm.then_inc(s_ym, 1)

            @block.vector
            def _(dve):
                step = Chain(dve, s_v)
                tt = dve.tensor_tensor
                SCALE = float(HD) ** -0.5

                def maxima(n):
                    kind, i = units[n]
                    h, w, lo = shape(kind, i)
                    at = (n % 2) * 1024
                    if n >= 2:
                        dve.wait_ge(s_ex, n - 1)
                    dve.wait_ge(s_sc, n + 1)
                    dst = probs(sm, kind, i, n)
                    if kind == "win":
                        src = sc[:, at:at + 1024].rearrange("p (h k) -> p h k", h=4)[:, :, lo:]
                        ins = dve.scalar_tensor_tensor(dst, src, SCALE, widen(mask[:, lo:], 1, 4), ALU.mult, ALU.add)
                    elif kind == "mem":
                        ins = dve.tensor_scalar(sm[:, n % 2, :], sc[:, at:at + 1024], SCALE, None, ALU.mult)
                    elif kind == "swin":
                        W = NSEQ * WIN
                        dve.wait_ge(s_smask, 16)
                        ins = dve.scalar_tensor_tensor(big[:, 0:W + NSMP], sc[:, 0:W + NSMP], SCALE, smask, ALU.mult, ALU.add)
                    else:
                        ins = dve.scalar_tensor_tensor(big[:, :].rearrange("p (b k) -> p b k", b=NSEQ),
                                                       sc[:, :].rearrange("p (b k) -> p b k", b=NSEQ), SCALE,
                                                       widen(bmask[:, :], 2, MEM), ALU.mult, ALU.add)
                    ins.then_inc(s_sm, 1)
                    dve.wait_ge(s_sm, n + 1)
                    if h == 1:
                        k = WIN if kind == "swin" else MEM
                        ins = dve.tensor_reduce(sm[:, n % 2, 0:k], big[:, 0:NSEQ * k].rearrange("p (b k) -> p k b", b=NSEQ), AX.X, ALU.max)
                        if kind == "swin":
                            ins = dve.tensor_copy(sm[:, n % 2, k:k + NSMP], big[:, NSEQ * k:NSEQ * k + NSMP])
                        step(ins)
                    step(dve.tensor_reduce(mx[:, n % 2, 0:h], dst, AX.X, ALU.max))
                    if kind in ("win", "swin"):
                        snk = sinks[:, 0:4] if h == 4 else sinks[:, 4:5]
                        step(dve.tensor_tensor(mx[:, n % 2, 0:h], mx[:, n % 2, 0:h], snk, ALU.max))
                        dve.tensor_tensor(es[:, n % 2, 0:h], snk, mx[:, n % 2, 0:h], ALU.subtract)
                    dve.tensor_scalar(nm[:, n % 2, 0:h], mx[:, n % 2, 0:h], -1.0, None, ALU.mult).then_inc(s_mx, 1)

                def normalise(n):
                    kind, i = units[n]
                    h, w, lo = shape(kind, i)
                    dve.wait_ge(s_ex, n + 1)
                    if kind in ("win", "swin"):
                        step(dve.tensor_tensor(den[:, n % 2, 0:h], den[:, n % 2, 0:h], es[:, n % 2, 0:h], ALU.add))
                    step(dve.reciprocal(den[:, n % 2, 0:h], den[:, n % 2, 0:h]))
                    p = probs(pr, kind, i, n)
                    dve.tensor_tensor(p, p, widen(den[:, n % 2, 0:h], 2, w - lo), ALU.mult).then_inc(s_pr, 1)

                dve.memset(ZK[0:C, :, 0:(CH - 1) * C], 0.0)
                step(tt(dI[:, :, :], widen(K.ident[0:C, 0:C], 1, G), widen(K.dsk[:, :], 2, C), ALU.mult))
                dve.wait_ge(s_uch, 48)
                dve.tensor_copy(ug.rearrange("p g (t c) -> p g t c", c=C), uch[0:NC, :, :].rearrange("p t (g c) -> p g t c", c=C))\
                    .then_inc(s_ug, 1)
                dve.wait_ge(s_ke, 8)
                k0 = ZK[0:C, :, (CH - 1) * C:CH * C]
                tt(k0, k0, dI[:, :, :], ALU.add).then_inc(s_z, 1)
                dve.wait_ge(s_ve, len(vb))
                l4r, l4i = widen(L[:, 0, DSEQ, :], 2, NSEQ), widen(L[:, 1, DSEQ, :], 2, NSEQ)
                x0, x1 = s0[:, 0, :, :], s0[:, 1, :, :]
                for n, (x, y, op) in enumerate(((x0, x1, ALU.subtract), (x1, x0, ALU.add))):
                    tt(st[:, 0, :, :], l4r, x, ALU.mult)
                    step(tt(st[:, 1, :, :], l4i, y, ALU.mult))
                    step(tt(sfin[:, n, :, :], st[:, 0, :, :], st[:, 1, :, :], op))
                tt(sfin[:, :, :, :], sfin[:, :, :, :], V[:, :, :, NJ + NSEQ:NC], ALU.add).then_inc(s_sf, 1)
                dve.wait_ge(s_mask, 48)
                dve.wait_ge(s_mt, 16 * CH)
                maxima(0)
                maxima(1)
                normalise(0)
                for n in range(NU):
                    if n + 2 < NU:
                        maxima(n + 2)
                    if n + 1 < NU:
                        normalise(n + 1)

            @block.scalar
            def _(act):
                def exps(n):
                    kind, i = units[n]
                    h, w, lo = shape(kind, i)
                    act.wait_ge(s_mx, n + 1)
                    if n >= 2:
                        act.wait_ge(s_tp, n - 1)
                    src, dst = probs(sm, kind, i, n), probs(pr, kind, i, n)
                    if kind in ("win", "swin"):
                        act.activation(es[:, n % 2, 0:h], es[:, n % 2, 0:h], ACT.Exp)
                    for x in range(h):
                        ins = act.activation(dst[:, x, :], src[:, x, :], ACT.Exp, bias=nm[:, n % 2, x:x + 1],
                                             accum_out=den[:, n % 2, x:x + 1])
                    ins.then_inc(s_ex, 1)

                def turned(n):
                    kind, i = units[n]
                    h, w, lo = shape(kind, i)
                    act.wait_ge(s_tp, n + 1)
                    if n >= 2:
                        act.wait_ge(s_ov, n - 1)
                    if h == 4:
                        v = lambda t: t.rearrange("p (h m q) -> p h m q", h=4, m=2)[:, :, lo // 128:, :]
                        ins = act.activation(v(prT[:, n % 2, :]), v(tp[:, :]), ACT.Copy)
                    elif kind == "swin":
                        act.activation(prT[:, n % 2, 0:P], tp[:, 0:P], ACT.Copy)
                        ins = act.activation(prT[0:NSMP, n % 2, P:2 * P], tp[0:NSMP, P:2 * P], ACT.Copy)
                    else:
                        ins = act.activation(prT[:, n % 2, 0:2 * P], tp[:, 0:2 * P], ACT.Copy)
                    ins.then_inc(s_te, 1)

                def values_out(n):
                    kind, i = units[n]
                    act.wait_ge(s_ov, n + 1)
                    base = 6 if "mem" in kind else 4
                    r = ROWS[i]
                    o = ov[:, n % 2, 0:256].rearrange("p (c q) -> p c q", c=2)
                    act.activation(K.mixedT[:, base:base + 2, i * P:i * P + r], o[:, :, 0:r], ACT.Copy).then_inc(s_oe, 1)

                for n in range(8):
                    act.wait_ge(s_wt, n + 1)
                    act.activation(WT[:, n // 4, (n % 4) * 4:(n % 4) * 4 + 4, :],
                                   pp[:, n, :].rearrange("p (g j) -> p g j", j=P), ACT.Copy).then_inc(s_we, 1)
                for n in range(8):
                    act.wait_ge(s_kt, n + 1)
                    act.activation(ZK[0:C, :, (CH - 1) * C:].rearrange("p (a m e) x -> p a e m x", m=4, e=2)[:, n // 2, n % 2, :, :],
                                   pp[0:C, n, :].rearrange("p (g j) -> p g j", j=P), ACT.Copy).then_inc(s_ke, 1)
                for n, gs in enumerate(ub):
                    act.wait_ge(s_ut, n + 1)
                    k = len(gs)
                    act.activation(U[:, gs[0]:gs[0] + k, :], pp[:, n, 0:k * NC].rearrange("p (g j) -> p g j", j=NC),
                                   ACT.Copy).then_inc(s_ue, 1)
                for n, gs in enumerate(vb):
                    act.wait_ge(s_vm, n + 1)
                    k = len(gs)
                    act.activation(V[:, :, gs[0]:gs[0] + k, :].rearrange("p r g j -> p g r j"),
                                   pp[:, n, 0:k * 2 * NC].rearrange("p (g r j) -> p g r j", r=2, j=NC),
                                   ACT.Copy).then_inc(s_ve, 1)
                exps(0)
                exps(1)
                turned(0)
                for n in range(NU):
                    if n + 2 < NU:
                        exps(n + 2)
                    if n + 1 < NU:
                        turned(n + 1)
                    values_out(n)
                for n in range(8):
                    act.wait_ge(s_ym, n + 1)
                    act.activation(K.y[0:COLS, :, :].rearrange("p t (a m e c) -> p a e m t c", m=4, e=2, c=C)[:, n // 2, n % 2, :, :, :],
                                   pp[0:COLS, n, :].rearrange("p (g t c) -> p g t c", t=CH, c=C), ACT.Gelu).then_inc(s_ye, 1)


def mix(nc, d, K):
    with Stage(nc, "mix", "right") as S:
        wg = S.sb("wg", [P, 4, 512])
        bg = S.sb("bg", [P, 4])
        wo = S.sb("wo", [P, KD, D])
        g2 = S.sb("g2", [P, D])
        yT = S.sb("yT", [P, 4, CH, COLS])
        sg = S.sb("sg", [P, 2, 4, COLS])
        square = S.sb("square", [P, D])
        ss = S.sb("ss", [P, NT])
        pp = S.ps("pp", [P, 2, 2, 512])
        pq = S.ps("pq", [P, 4, 512])

        s_in = S.sem("glu_landed")
        s_wo = S.sem("wout_landed")
        s_xl = S.sem("x_landed")
        s_yt = S.sem("y_turned")
        s_ye = S.sem("y_out")
        s_gm = S.sem("glu_summed")
        s_sg = S.sem("sigmoids")
        s_gl = S.sem("glu_done")
        s_om = S.sem("out_summed")
        s_h = S.sem("residual")
        s_ss = S.sem("squares")
        s_std = S.sem("std")
        s_xn = S.sem("normed")
        s_v = S.sem("dve_chain")

        with S.block() as block:
            @block.sync
            def _(sp):
                sp.dma_start(wg[:, :, :], d["w_glu"]).then_inc(s_in, 16)
                sp.dma_start(K.x[:, 0:4, :], d["x_tok"][0:SEQ, :].rearrange("(i p) n -> p i n", p=P)).then_inc(s_xl, 16)
                sp.dma_start(K.x[0:NSMP, 4, :], d["x_tok"][SEQ:T, :]).then_inc(s_xl, 16)
                sp.dma_start(bg[:, :], d["b_glu"]).then_inc(s_in, 16)
                sp.dma_start(g2[:, :], d["g2"]).then_inc(s_in, 16)
                sp.dma_start(wo[:, :, :], d["w_out"]).then_inc(s_wo, 16)
                sp.dma_start(K.wq[:, :, :], d["wq"]).then_inc(K.s_wq, 16)

            @block.tensor
            def _(pe):
                for n in range(8):
                    kc, th = n // 2, n % 2
                    if n >= 4:
                        pe.wait_ge(s_ye, n - 3)
                    for t in range(4):
                        mm = pe.transpose(pq[:, n % 4, t * COLS:(t + 1) * COLS],
                                          K.y[0:COLS, th * 4 + t, kc * P:(kc + 1) * P], K.ident[:COLS, :COLS])
                    mm.then_inc(s_yt, 1)
                pe.wait_ge(s_in, 48)
                pe.wait_ge(s_ye, 8)
                for n in range(8):
                    co, th = n // 2, n % 2
                    if n >= 4:
                        pe.wait_ge(s_sg, n - 3)
                    for kc in range(4):
                        mm = pe.matmul(pq[:, n % 4, 0:4 * COLS], wg[:, kc, co * P:(co + 1) * P],
                                       yT[:, kc, th * 4:(th + 1) * 4, :], start=(kc == 0), stop=(kc == 3))
                    mm.then_inc(s_gm, 1)
                pe.wait_ge(s_wo, 16)
                pe.wait_ge(s_gl, 8)

                for i in range(NT):
                    r = ROWS[i]
                    if i >= 2:
                        pe.wait_ge(s_h, i - 1)
                    for k in range(KD):
                        for c in range(2):
                            mm = pe.matmul(pp[:r, i % 2, c, :], K.mixedT[:, k, i * P:i * P + r], wo[:, k, c * 512:(c + 1) * 512],
                                           start=(k == 0), stop=(k == KD - 1))
                    mm.then_inc(s_om, 1)

            @block.scalar
            def _(act):
                for n in range(8):
                    kc, th = n // 2, n % 2
                    act.wait_ge(s_yt, n + 1)
                    act.activation(yT[:, kc, th * 4:(th + 1) * 4, :], pq[:, n % 4, 0:4 * COLS].rearrange("p (t j) -> p t j", j=COLS),
                                   ACT.Copy).then_inc(s_ye, 1)
                act.wait_ge(s_in, 48)
                for n in range(8):
                    co = n // 2
                    act.wait_ge(s_gm, n + 1)
                    if n >= 2:
                        act.wait_ge(s_gl, n - 1)
                    act.activation(sg[:, n % 2, :, :], pq[:, n % 4, 0:4 * COLS].rearrange("p (t j) -> p t j", j=COLS),
                                   ACT.Sigmoid, bias=bg[:, co:co + 1]).then_inc(s_sg, 1)

                for i in range(NT):
                    r = ROWS[i]
                    act.wait_ge(s_h, i + 1)
                    act.activation(square[:r, :], K.x[:r, i, :], ACT.Square, accum_out=ss[:r, i:i + 1]).then_inc(s_ss, 1)
                    act.wait_ge(s_ss, i + 1)
                    act.activation(ss[:r, i:i + 1], ss[:r, i:i + 1], ACT.Sqrt, bias=K.eps[:r, 0:1], scale=1.0 / D).then_inc(s_std, 1)

            @block.vector
            def _(dve):
                step = Chain(dve, s_v)
                for n in range(8):
                    co, th = n // 2, n % 2
                    dve.wait_ge(s_sg, n + 1)
                    prompt = K.mixedT[:, co, 0:SEQ].rearrange("p (j t) -> p t j", t=CH)[:, th * 4:(th + 1) * 4, :]
                    ins = dve.tensor_tensor(prompt, yT[:, co, th * 4:(th + 1) * 4, 0:NJ], sg[:, n % 2, :, 0:NJ], ALU.mult)
                    if th == 0:
                        smp = K.mixedT[:, co, SEQ:T].rearrange("p (b t) -> p t b", t=DSEQ)
                        ins = dve.tensor_tensor(smp, yT[:, co, 0:DSEQ, NJ:COLS], sg[:, n % 2, :, NJ:COLS], ALU.mult)
                    ins.then_inc(s_gl, 1)
                dve.wait_ge(s_xl, 32)
                for i in range(NT):
                    r = ROWS[i]
                    dve.wait_ge(s_om, i + 1)
                    dve.tensor_tensor(K.x[:r, i, :], K.x[:r, i, :], pp[:r, i % 2, :, :].rearrange("p a b -> p (a b)"),
                                      ALU.add).then_inc(s_h, 1)
                    dve.wait_ge(s_std, i + 1)
                    step(dve.reciprocal(ss[:r, i:i + 1], ss[:r, i:i + 1]))
                    dve.scalar_tensor_tensor(K.xn[:r, i, :], K.x[:r, i, :], ss[:r, i:i + 1], g2[:r, :], ALU.mult,
                                             ALU.mult).then_inc(s_xn, 1)


def experts(nc, d, K):
    with Stage(nc, "peer") as S:
        RU, RV, RD = 7, 8, 4
        GRP = TOPK
        order = [4, 0, 1, 2, 3]
        count = [SLOTS // 4 if i == 4 else SLOTS for i in order]
        first = [sum(count[:k]) for k in range(NT + 1)]
        steps = [(k, s) for k in range(NT) for s in range(count[k])]
        NS, NG = len(steps), len(steps) // GRP
        NH2 = 2 * PH
        U = S.sb("U", [P, RU, D])
        V = S.sb("V", [P, RV, D])
        dg = S.sb("dg", [P, RD, P])
        a = S.sb("a", [P, 2, GRP])
        ga = S.sb("ga", [P, 2, GRP])
        wt = S.sb("wt", [P, 2, GRP])
        ident4 = S.sb("ident4", [P, NSMP])
        xs = S.sb("xs", [P, D])
        es = S.sb("es", [P, SLOTS // 4], U32)
        gs = S.sb("gs", [P, SLOTS // 4])
        keys = S.sb("keys", [P, 2, PK])
        xnT = S.sb("xnT", [P, KD, P])
        qT = S.sb("qT", [P, NH2, P])
        iota = S.sb("iota", [P, TOPK], BF16)
        iotaf = S.sb("iotaf", [P, TOPK])
        val = S.sb("val", [P, NH2, TOPK])
        idx = S.sb("idx", [P, NH2, TOPK], U32)
        idxb = S.sb("idxb", [P, NH2, TOPK], BF16)
        left = S.sb("left", [P, 4, PK])
        cand = S.sb("cand", [P, PH, CAND])
        cleft = S.sb("cleft", [P, 4, CAND])
        top = S.sb("top", [P, PH, TOPK])
        pos = S.sb("pos", [P, SLOTS], U32)
        t32 = S.sb("t32", [P, SLOTS], U32)
        f = S.sb("f", [P, 4, SLOTS])
        rcb = S.sb("rcb", [P, 2, SLOTS], BF16)
        hot = S.sb("hot", [P, SLOTS, TOPK], BF16)
        ex = S.sb("ex", [P, PH, TOPK])
        dn = S.sb("dn", [P, PH])
        acc = S.ps("acc", [P, 2, 512])
        pq = S.ps("pq", [P, 2, 512])
        psc = S.ps("psc", [P, 4, 512])

        s_keys = S.sem("keys_landed")
        s_xs = S.sem("sample_rows_spread")
        s_es = S.sem("sample_experts_spread")
        s_gs = S.sem("sample_gates_spread")
        s_xt = S.sem("rows_turned")
        s_xe = S.sem("rows_out")
        s_qm = S.sem("queries_summed")
        s_qe = S.sem("queries_out")
        s_sc = S.sem("scores")
        s_sr = S.sem("scores_read")
        s_df = S.sem("differences")
        s_ex = S.sem("exps")
        s_id = S.sem("experts_known")
        s_gt = S.sem("gates_known")
        s_u = [S.sem(f"u_landed{n}") for n in range(RU)]
        s_v = [S.sem(f"v_landed{n}") for n in range(RV)]
        s_dot = S.sem("dots")
        s_ga = S.sem("gelus")
        s_wt = S.sem("weights")
        s_dg = S.sem("diagonals")
        s_mm = S.sem("summed")
        s_y = S.sem("result")
        s_out = S.sem("stored")
        s_ch = S.sem("dve_chain")

        TURN, QUERY, SCORE = 0, (8, 14, 20, 26), (30, 32, 34, 36)
        TURN_OUT, QUERY_OUT, EXPS = 2, (11, 17, 23, 29), 96
        BEST, SUMS, NUMBERS, GATES, RESULT = (56, 62, 68, 74), 82, 92, 8, 30

        with S.block() as block:
            @block.sync
            def _(sp):
                sp.dma_start(keys[:, :, :], d["keys"]).then_inc(s_keys, 16)
                sp.dma_start(iotaf[:, :], d["iota"]).then_inc(s_keys, 16)
                sp.dma_start(ident4[:, :], d["ident4"]).then_inc(s_keys, 16)
                spread = [(slice(q * NSMP, (q + 1) * NSMP), slice(q * SLOTS // 4, (q + 1) * SLOTS // 4)) for q in range(4)]
                for t, c in spread:
                    sp.dma_start(xs[t, :], K.xn[0:NSMP, 4, :]).then_inc(s_xs, 16)
                sp.wait_ge(s_id, 1)
                for t, c in spread:
                    sp.dma_start(es[t, :], K.expert[0:NSMP, 4, c]).then_inc(s_es, 16)
                sp.wait_ge(s_gt, 1)
                for t, c in spread:
                    sp.dma_start(gs[t, :], K.gate[0:NSMP, 4, c]).then_inc(s_gs, 16)
                for k, i in enumerate(order):
                    sp.wait_ge(s_y, k + 1)
                    dst = d["y_s"] if i == 4 else d["y_p"][i * P:(i + 1) * P, :]
                    sp.dma_start(dst, K.x[:ROWS[i], i, :]).then_inc(s_out, 16)
                sp.wait_ge(s_out, 16 * NT)

            @block.gpsimd
            def _(pool):
                LAG = GRP + GRP // 2

                def rows(n):
                    k, s = steps[n]
                    return K.expert[:, order[k], s:s + 1] if k else es[:, s:s + 1]

                pool.wait_ge(s_es, 64)
                for n in range(NS + LAG):
                    if n < NS:
                        k, s = steps[n]
                        if k and s == 0:
                            pool.wait_ge(s_id, k + 1)
                        if n >= RU:
                            pool.wait_ge(s_dot, n - RU + 1)
                        pool.indirect_dma_start(U[:, n % RU, :], None, d["peer_u"],
                                                bass.IndirectOffsetOnAxis(ap=rows(n), axis=0)).then_inc(s_u[n % RU], 16)
                    m = n - LAG
                    if m >= 0:
                        if m >= RV:
                            pool.wait_ge(s_mm, m - RV + 1)
                        pool.indirect_dma_start(V[:, m % RV, :], None, d["peer_v"],
                                                bass.IndirectOffsetOnAxis(ap=rows(m), axis=0)).then_inc(s_v[m % RV], 16)

            @block.vector
            def _(dve):
                step = Chain(dve, s_ch)
                tt, ts = dve.tensor_tensor, dve.tensor_scalar

                def best(k, b):
                    r = ROWS[order[k]]
                    n = 4 * k + b
                    dve.wait_ge(s_sc, n + 1)
                    hh = [b * 4 + m for m in range(4)]
                    sc = [psc[:r, b, m * P:(m + 1) * P] for m in range(4)]
                    for m in range(4):
                        ins = dve.max(val[:r, hh[m], 0:8], sc[m])
                    step(ins)
                    for m in range(4):
                        dve.max_index(idx[:r, hh[m], 0:8], val[:r, hh[m], 0:8], sc[m])
                        ins = dve.match_replace(left[:r, m, :], val[:r, hh[m], 0:8], sc[m], -BIG)
                    ins.then_inc(s_sr, 1)
                    dve.wait_ge(s_sr, n + 1)
                    for m in range(4):
                        ins = dve.max(val[:r, hh[m], 8:16], left[:r, m, :])
                    step(ins)
                    for m in range(4):
                        ins = dve.max_index(idx[:r, hh[m], 8:16], val[:r, hh[m], 8:16], left[:r, m, :])
                    step(ins)

                def sums(k):
                    r = ROWS[order[k]]
                    v = val[:r, :, :].rearrange("p (h e) k -> p h e k", e=2)
                    v1, v2 = v[:, :, 0, :], v[:, :, 1, :]
                    tt(cand[:r, :, 0:16], v2, v1[:, :, 0:1].broadcast_to([r, PH, 16]), ALU.add)
                    tt(cand[:r, :, 16:72].rearrange("p h (a b) -> p h a b", b=8), widen(v1[:, :, 1:8], 3, 8),
                       widen(v2[:, :, 0:8], 2, 7), ALU.add)
                    tt(cand[:r, :, 72:80], v1[:, :, 8:16], v2[:, :, 0:1].broadcast_to([r, PH, 8]), ALU.add)
                    step(dve.tensor_copy(idxb[:r, :, :], idx[:r, :, :]))
                    p8 = pos[:r, :].rearrange("p (h k) -> p h k", k=TOPK)
                    for b in range(2):
                        hs = range(b * 4, b * 4 + 4)
                        for h in hs:
                            ins = dve.max(top[:r, h, 0:8], cand[:r, h, :])
                        step(ins)
                        for h in hs:
                            dve.max_index(p8[:, h, 0:8], top[:r, h, 0:8], cand[:r, h, :])
                            ins = dve.match_replace(cleft[:r, h % 4, :], top[:r, h, 0:8], cand[:r, h, :], -BIG)
                        step(ins)
                        for h in hs:
                            ins = dve.max(top[:r, h, 8:16], cleft[:r, h % 4, :])
                        step(ins)
                        for h in hs:
                            ins = dve.max_index(p8[:, h, 8:16], top[:r, h, 8:16], cleft[:r, h % 4, :])
                        step(ins)
                    tt(ex[:r, :, :], top[:r, :, :], top[:r, :, 0:1].broadcast_to([r, PH, TOPK]), ALU.subtract).then_inc(s_df, 1)

                def numbers(k):
                    i = order[k]
                    r = ROWS[i]
                    F = [f[:r, n, :] for n in range(4)]
                    dve.tensor_copy(F[0], pos[:r, :])
                    step(ts(t32[:r, :], pos[:r, :], 56.0, None, ALU.add))
                    step(ts(t32[:r, :], t32[:r, :], 3, None, ALU.logical_shift_right))
                    step(dve.tensor_copy(F[1], t32[:r, :]))
                    step(ts(F[1], F[1], -8.0, 0.0, ALU.add, ALU.max))
                    step(dve.scalar_tensor_tensor(F[1], F[0], -64.0, F[1], ALU.add, ALU.max))
                    ts(F[2], F[1], 1.0, 8.0, ALU.min, ALU.mult)
                    step(dve.scalar_tensor_tensor(F[3], F[1], -8.0, F[0], ALU.mult, ALU.add))
                    step(tt(F[3], F[3], F[2], ALU.subtract))
                    dve.tensor_copy(rcb[:r, 0, :], F[1])
                    step(ts(rcb[:r, 1, :], F[3], 0.0, None, ALU.max))
                    ib = idxb[:r, :, :].rearrange("p (h e) k -> p h e k", e=2)
                    for e in range(2):
                        step(tt(hot[:r, :, :], widen(rcb[:r, e, :], 2, TOPK), widen(iota[:r, :], 1, SLOTS), ALU.is_equal))
                        h4 = hot[:r, :, :].rearrange("p (h k) j -> p h k j", k=TOPK)
                        step(tt(h4, h4, widen(ib[:, :, e, :], 2, TOPK), ALU.mult))
                        step(dve.tensor_reduce(F[e], hot[:r, :, :], AX.X, ALU.add))
                    dve.scalar_tensor_tensor(K.expert[:r, i, :], F[0], float(PK), F[1], ALU.mult, ALU.add).then_inc(s_id, 1)

                def gates(k):
                    i = order[k]
                    r = ROWS[i]
                    dve.wait_ge(s_ex, k + 1)
                    step(dve.tensor_reduce(dn[:r, :], ex[:r, :, :], AX.X, ALU.add))
                    step(dve.reciprocal(dn[:r, :], dn[:r, :]))
                    tt(K.gate[:r, i, :].rearrange("p (h k) -> p h k", k=TOPK), ex[:r, :, :], widen(dn[:r, :], 2, TOPK),
                       ALU.mult).then_inc(s_gt, 1)

                def weights(g):
                    k, s = steps[g * GRP]
                    if s == 0:
                        if k:
                            dve.wait_ge(s_gt, k + 1)
                        else:
                            dve.wait_ge(s_gs, 64)
                    gate = K.gate[:, order[k], s:s + GRP] if k else gs[:, s:s + GRP]
                    dve.wait_ge(s_ga, g + 1)
                    if g >= 2:
                        dve.wait_ge(s_dg, GRP * (g - 1))
                    tt(wt[:, g % 2, :], ga[:, g % 2, :], gate, ALU.mult).then_inc(s_wt, 1)

                def result(k):
                    i = order[k]
                    r = ROWS[i]
                    dve.wait_ge(s_mm, first[k + 1])
                    tt(K.x[:r, i, :], K.x[:r, i, :], acc[:r, :, :].rearrange("p a b -> p (a b)"), ALU.add).then_inc(s_y, 1)

                dve.wait_ge(s_keys, 48)
                step(dve.tensor_copy(iota[:, :], iotaf[:, :]))
                for b in range(4):
                    best(0, b)
                sums(0)
                numbers(0)
                gates(0)
                dve.wait_ge(s_xs, 64)
                for n in range(NS):
                    k, s = steps[n]
                    g = n // GRP
                    if n % GRP == 0 and g >= 2:
                        dve.wait_ge(s_ga, g - 1)
                    if n % GRP == 1 and g >= 1:
                        weights(g - 1)
                    if k and s == GATES:
                        gates(k)
                    if k and s == RESULT:
                        result(k - 1)
                    if k + 1 < NT:
                        at = (2, 6, 10, 14) if k == 0 else BEST
                        if s in at:
                            best(k + 1, at.index(s))
                        if s == (20 if k == 0 else SUMS):
                            sums(k + 1)
                        if s == (24 if k == 0 else NUMBERS):
                            numbers(k + 1)
                    dve.wait_ge(s_u[n % RU], 16 * (n // RU + 1))
                    x = K.xn[:, order[k], :] if k else xs[:, :]
                    dve.tensor_tensor_reduce(U[:, n % RU, :], U[:, n % RU, :], x, 1.0, 0.0, ALU.mult, ALU.add,
                                             a[:, g % 2, n % GRP:n % GRP + 1]).then_inc(s_dot, 1)
                weights(NG - 1)
                result(NT - 1)

            @block.scalar
            def _(act):
                def turned_out(k):
                    r = ROWS[order[k]]
                    act.wait_ge(s_xt, k + 1)
                    act.activation(xnT[:, :, 0:r], pq[:, :, :].rearrange("p a (b t) -> p (a b) t", t=P)[:, :, 0:r],
                                   ACT.Copy).then_inc(s_xe, 1)

                def queries_out(k, b):
                    r = ROWS[order[k]]
                    act.wait_ge(s_qm, 4 * k + b + 1)
                    act.activation(qT[:, 4 * b:4 * b + 4, 0:r], pq[:, b % 2, :].rearrange("p (m t) -> p m t", t=P)[:, :, 0:r],
                                   ACT.Copy).then_inc(s_qe, 1)

                def exps(k):
                    r = ROWS[order[k]]
                    act.wait_ge(s_df, k + 1)
                    act.activation(ex[:r, :, :], ex[:r, :, :], ACT.Exp).then_inc(s_ex, 1)

                for k in range(2):
                    turned_out(k)
                    for b in range(4):
                        queries_out(k, b)
                exps(0)
                for n in range(NS):
                    k, s = steps[n]
                    g = n // GRP
                    if s == (GRP if k == 0 else EXPS) and k + 1 < NT:
                        exps(k + 1)
                    if k and k + 1 < NT:
                        if s == TURN_OUT:
                            turned_out(k + 1)
                        if s in QUERY_OUT:
                            queries_out(k + 1, QUERY_OUT.index(s))
                    if n % GRP == 0:
                        act.wait_ge(s_dot, GRP * (g + 1))
                        if g >= 2:
                            act.wait_ge(s_wt, g - 1)
                        act.activation(ga[:, g % 2, :], a[:, g % 2, :], ACT.Gelu).then_inc(s_ga, 1)
                        act.wait_ge(s_wt, g + 1)
                    if n >= RD:
                        act.wait_ge(s_mm, n - RD + 1)
                    dst, src = (dg[:, n % RD, :], K.ident[:, :]) if k else (dg[:, n % RD, 0:NSMP], ident4[:, :])
                    act.activation(dst, src, ACT.Copy, scale=wt[:, g % 2, n % GRP:n % GRP + 1]).then_inc(s_dg, 1)

            @block.tensor
            def _(pe):
                def turn(k):
                    i = order[k]
                    r = ROWS[i]
                    if k:
                        pe.wait_ge(s_qe, 4 * k)
                    for c in range(KD):
                        mm = pe.transpose(pq[:, c // 4, (c % 4) * P:(c % 4) * P + r], K.xn[:r, i, c * P:(c + 1) * P], K.ident[:r, :r])
                    mm.then_inc(s_xt, 1)

                def queries(k, b):
                    r = ROWS[order[k]]
                    if b == 0:
                        pe.wait_ge(s_xe, k + 1)
                        if k == 0:
                            pe.wait_ge(K.s_wq, 16)
                    if b >= 2:
                        pe.wait_ge(s_qe, 4 * k + b - 1)
                    for m in range(4):
                        for c in range(KD):
                            mm = pe.matmul(pq[:, b % 2, m * P:m * P + r], K.wq[:, c, (4 * b + m) * P:(4 * b + m + 1) * P],
                                           xnT[:, c, 0:r], start=(c == 0), stop=(c == KD - 1))
                    mm.then_inc(s_qm, 1)

                def scores(k, b):
                    r = ROWS[order[k]]
                    pe.wait_ge(s_qe, 4 * k + b + 1)
                    if k:
                        pe.wait_ge(s_sr, 4 * (k - 1) + b + 1)
                    for m in range(4):
                        hh = b * 4 + m
                        mm = pe.matmul(psc[:r, b, m * P:(m + 1) * P], qT[:, hh, 0:r], keys[:, hh % 2, :], start=True, stop=True)
                    mm.then_inc(s_sc, 1)

                pe.wait_ge(s_keys, 48)
                for k in range(2):
                    turn(k)
                    for b in range(4):
                        queries(k, b)
                    for b in range(4):
                        scores(k, b)
                for n in range(NS):
                    k, s = steps[n]
                    r = ROWS[order[k]]
                    if k and k + 1 < NT:
                        if s == TURN:
                            turn(k + 1)
                        if s in QUERY:
                            queries(k + 1, QUERY.index(s))
                        if s in SCORE:
                            scores(k + 1, SCORE.index(s))
                    pe.wait_ge(s_dg, n + 1)
                    pe.wait_ge(s_v[n % RV], 16 * (n // RV + 1))
                    if k and s == 0:
                        pe.wait_ge(s_y, k)
                    for c in range(2):
                        mm = pe.matmul(acc[:r, c, :], dg[:, n % RD, 0:r], V[:, n % RV, c * 512:(c + 1) * 512],
                                       start=(s == 0), stop=(s == count[k] - 1))
                    mm.then_inc(s_mm, 1)


class Kept:
    pass


def build(nc, d):
    K = Kept()
    with Stage(nc, "kept") as S:
        K.ident = S.sb("ident", [P, P])
        K.eps = S.sb("eps", [P, 1])
        with Stage(nc, "mixing", "right") as M:
            with Stage(nc, "tables") as B:
                K.par = B.sb("par", [P, 3, GP])
                K.bc = B.sb("bc", [P, 4, GP, C])
                K.dsk = B.sb("dsk", [C, G])
                K.s0 = B.sb("s0", [P, 2, GP, NSEQ])
                K.w = B.sb("w", [P, 24, GP])
                K.L = B.sb("L", [P, 3, CH + 1, GP])
                K.Lrev = B.sb("Lrev", [P, 2, CH, GP])
                K.bb = B.sb("bb", [P, 2, GP, C])
                K.Q = B.sb("Q", [P, 2, GP, CH + 1, C])
                K.W = B.sb("W", [P, 2, GP, CH, C])
                K.A8 = B.sb("A8", [P, 2, 2, GP])
                heads = Stage(nc, "heads").__enter__()
                K.qkT = heads.sb("qkT", [P, 5, T])
                K.v = heads.sb("v", [P, NT, 128])
                K.mkT = heads.sb("mkT", [P, 2, MEM])
                K.mv = heads.sb("mv", [P, 2, 256])
                project(nc, d, K)
                K.mixedT = M.sb("mixedT", [P, KD, T])
                K.y = M.sb("y", [P, CH, UW])
                blend(nc, d, K)
                heads.__exit__(None, None, None)
            K.x = S.sb("x", [P, NT, D])
            K.xn = S.sb("xn", [P, NT, D])
            K.expert = S.sb("expert", [P, NT, SLOTS], U32)
            K.gate = S.sb("gate", [P, NT, SLOTS])
            K.wq = S.sb("wq", [P, KD, PH * 256])
            K.s_wq = S.sem("wq_landed")
            mix(nc, d, K)
        experts(nc, d, K)


def constants():
    half = HD // 2
    inv = (10000.0 ** (-np.arange(half, dtype=np.float32) / half)).astype(np.float32)
    pos = np.concatenate([np.arange(SEQ), np.tile(2048 + np.arange(DSEQ), NSEQ)]).astype(np.float32)
    ang = pos[:, None] * inv[None, :]
    rope = np.zeros((P, NT, 2, HD), np.float32)
    for i in range(NT):
        a = ang[i * P:i * P + ROWS[i]]
        rope[:ROWS[i], i, 0] = np.concatenate([np.cos(a), np.cos(a)], 1)
        rope[:ROWS[i], i, 1] = np.concatenate([np.sin(a), np.sin(a)], 1)
    q, k = np.arange(P)[:, None], np.arange(256)[None, :] - 128
    mask = np.where((q - k >= 0) & (q - k < WIN), 0.0, -BIG).astype(np.float32)
    row = np.arange(P) % NSMP
    rb, rq = (row // DSEQ)[:, None], (row % DSEQ)[:, None]
    kb, kw = np.arange(NSEQ * WIN)[None, :] // WIN, np.arange(NSEQ * WIN)[None, :] % WIN
    old = np.where((rb == kb) & (kw > rq), 0.0, -BIG)
    nb, ns = np.arange(NSMP)[None, :] // DSEQ, np.arange(NSMP)[None, :] % DSEQ
    new = np.where((rb == nb) & (ns <= rq), 0.0, -BIG)
    return {
        "rope": rope,
        "mask": mask,
        "smask": np.concatenate([old, new], 1).astype(np.float32),
        "bmask": np.where(rb == np.arange(NSEQ)[None, :], 0.0, -BIG).astype(np.float32),
        "iota": np.tile(np.arange(TOPK, dtype=np.float32), (P, 1)),
        "ident": np.eye(P, dtype=np.float32),
        "ident4": np.tile(np.eye(NSMP, dtype=np.float32), (4, 1)),
    }


def layouts(i):
    A = {k: np.asarray(v) for k, v in i.items()}

    def chunked(w):
        return w.reshape(w.shape[0] // P, P, -1).transpose(1, 0, 2)

    x = np.concatenate([A["x_prompt"].reshape(SEQ, D), A["x_sample"].reshape(NSMP, D)])
    mem = A["mem_prompt"].reshape(MEM, D)
    w = A["w_in"][0]
    q = w[:, 512:768].reshape(D, 2, 2, HD).transpose(0, 2, 1, 3).reshape(D, 256)
    w = np.concatenate([w[:, :512], q, w[:, 768:896], w[:, 1024:1280], w[:, 896:1024]], 1)
    pair = lambda a: a.reshape(GP, 2, N).transpose(1, 2, 0).reshape(P, GP)
    pairc = lambda a: a.reshape(GP, 2, N, C).transpose(1, 2, 0, 3).reshape(P, GP, C)
    pairs = lambda a: a.reshape(NSEQ, GP, 2, N).transpose(2, 3, 1, 0).reshape(P, GP, NSEQ)
    cT = lambda a: a[0].transpose(0, 2, 1)
    sink = A["swa_sinks"][0].reshape(2, 2).T.reshape(4)
    ck, cv = A["cache_win_k"][0], A["cache_win_v"][0]
    mk, mv = A["cache_mem_k"][0], A["cache_mem_v"][0]
    gains = np.concatenate([np.tile(A["swa_q_norm"], (4, 1)), np.tile(A["swa_k_norm"], (2, 1)),
                            np.tile(A["mem_q_norm"], (4, 1)), np.tile(A["mem_k_norm"], (4, 1))])
    out = {
        "x_tok": x,
        "xT": chunked(x.T),
        "memT": chunked(mem.T),
        "mem_tok": mem.reshape(2, P, D).transpose(1, 0, 2),
        "w_in": chunked(w),
        "w_mem": chunked(A["w_mem_kv"][0]),
        "g1T": np.stack([A["norm1_g"][0].reshape(KD, P).T, A["mem_norm_g"][0].reshape(KD, P).T], 1),
        "gains": np.broadcast_to(gains, (P,) + gains.shape),
        "sinks": np.concatenate([np.broadcast_to(A["swa_sinks"][0], (P, 4)), np.repeat(sink, NSMP)[:, None]], 1),
        "cache_k": ck.reshape(NSEQ, WIN, 128),
        "cache_v": cv.reshape(NSEQ, WIN, 128),
        "kcT": ck.transpose(2, 3, 0, 1).reshape(P, NSEQ, WIN),
        "vc": cv.transpose(1, 0, 2, 3).reshape(P, NSEQ, 128),
        "mcT": mk.reshape(NSEQ, MEM, 2, 2, HD).transpose(3, 4, 2, 0, 1).reshape(P, 2, NSEQ, MEM),
        "mcv": mv.reshape(NSEQ, 2, P, 256).transpose(2, 1, 0, 3),
        "ssm_par": np.stack([pair(A["ssm_log_dt"][0]), pair(A["ssm_a_re"][0]), pair(A["ssm_a_im"][0])], 1),
        "ssm_bc": np.stack([pairc(A["ssm_b_re"][0]), pairc(A["ssm_b_im"][0]), pairc(cT(A["ssm_c_re"])),
                            pairc(cT(A["ssm_c_im"]))], 1),
        "ssm_d": A["ssm_d"][0].T,
        "ssm_s0": np.stack([pairs(A["state_ssm_re"][0]), pairs(A["state_ssm_im"][0])], 1),
        "w_glu": chunked(A["w_glu"][0]),
        "b_glu": A["b_glu"][0].reshape(4, P).T,
        "w_out": chunked(A["w_out"][0]),
        "g2": np.broadcast_to(A["norm2_g"][0], (P, D)),
        "wq": chunked(A["peer_wq"][0]),
        "keys": np.stack([A["peer_k1"][0].T, A["peer_k2"][0].T], 1),
        "peer_u": A["peer_u"][0],
        "peer_v": A["peer_v"][0],
    }
    out.update(constants())
    return {k: np.ascontiguousarray(v) for k, v in out.items()}


OUTS = {
    "y_p": (SEQ, D), "y_s": (NSMP, D), "p_ssm": (P, 2, GP), "s_ssm": (P, 2, GP, NSEQ),
    "p_win_k": (WIN, 128), "p_win_v": (WIN, 128), "p_mem_k": (MEM, 256), "p_mem_v": (MEM, 256),
    "s_win_k": (NSEQ, WIN, 128), "s_win_v": (NSEQ, WIN, 128),
}


def program(nc, arrays):
    d = {k: nc.dram_tensor(k, v.shape, mybir.dt.from_np(v.dtype), kind="ExternalInput").ap() for k, v in arrays.items()}
    for k, shape in OUTS.items():
        d[k] = nc.dram_tensor("out_" + k, shape, F32, kind="ExternalOutput").ap()
    d["u_scratch"] = nc.dram_tensor("u_scratch", (T, UW), F32, kind="Internal").ap()
    build(nc, d)


def returned(r):
    ps, ss = r["p_ssm"], r["s_ssm"]
    back = lambda a: a.reshape(2, N, GP).transpose(2, 0, 1).reshape(1, 1, G, N)
    backs = lambda a: a.reshape(2, N, GP, NSEQ).transpose(3, 2, 0, 1).reshape(1, NSEQ, G, N)
    return (r["y_p"].reshape(1, SEQ, D), r["y_s"].reshape(NSEQ, DSEQ, D),
            back(ps[:, 0]), back(ps[:, 1]),
            r["p_win_k"].reshape(1, 1, WIN, 2, HD), r["p_win_v"].reshape(1, 1, WIN, 2, HD),
            r["p_mem_k"].reshape(1, 1, MEM, 4, HD), r["p_mem_v"].reshape(1, 1, MEM, 4, HD),
            backs(ss[:, 0]), backs(ss[:, 1]),
            r["s_win_k"].reshape(1, NSEQ, WIN, 2, HD), r["s_win_v"].reshape(1, NSEQ, WIN, 2, HD))


def kernel(**inputs):
    import concourse.bacc as bacc
    from concourse.bass_utils import run_bass_kernel_spmd

    nc = bacc.Bacc("TRN2", target_bir_lowering=False, num_devices=1)
    arrays = layouts(inputs)
    program(nc, arrays)
    r = run_bass_kernel_spmd(nc, [arrays], core_ids=[0]).results[0]
    return returned({k: np.asarray(r["out_" + k]) for k in OUTS})
```

```python
from contextlib import ExitStack

import numpy as np

import concourse.bass as bass
from concourse import mybir
from concourse.alu_op_type import AluOpType as ALU

ACT = mybir.ActivationFunctionType
AX = mybir.AxisListType
F32 = mybir.dt.float32
BF16 = mybir.dt.bfloat16
U32 = mybir.dt.uint32

P = 128
D = 1024
KD = D // P
SEQ, NSEQ, DSEQ = 512, 8, 4
NSMP = NSEQ * DSEQ
T = SEQ + NSMP
NT = 5
ROWS = [P, P, P, P, NSMP]
HD = 64
EPS = 1e-6
WIN = 128
MEM = 256
G, N, C = 32, 64, 16
GP = G // 2
CH = 8
NJ = SEQ // CH
COLS = NJ + NSEQ
ROWH, ROWK = 6, 10
ZW = 768
UW = 512
PH, PK, TOPK = 8, 128, 16
CAND = 80
BIG = 3.0e38
SLOTS = PH * TOPK


class Chain:

    def __init__(self, eng, sem):
        self.eng, self.sem, self.n = eng, sem, 0

    def __call__(self, ins):
        self.n += 1
        ins.then_inc(self.sem, 1)
        self.eng.wait_ge(self.sem, self.n)


def widen(ap, axis, n):
    v = ap.unsqueeze(axis)
    shape = list(v.shape)
    shape[axis] = n
    return v.broadcast_to(shape)


class Stage:

    def __init__(self, nc, name, side="left"):
        self.nc, self.name, self.side, self.ctx = nc, name, side, ExitStack()

    def __enter__(self):
        self.ctx.__enter__()
        return self

    def __exit__(self, *a):
        return self.ctx.__exit__(*a)

    def sb(self, name, shape, dt=F32):
        return self.ctx.enter_context(self.nc.sbuf_tensor(f"sb_{self.name}_{name}", shape, dt, side=self.side))

    def ps(self, name, shape, dt=F32):
        return self.ctx.enter_context(self.nc.psum_tensor(f"sb_{self.name}_{name}", shape, dt))

    def sem(self, name):
        return self.ctx.enter_context(self.nc.semaphore(f"sb_{self.name}_{name}"))

    def block(self):
        return self.nc.Block()


def two_pi_parts():
    full = 2 * np.pi
    a = 6.28125
    b = float(np.floor((full - a) * 2 ** 20) / 2 ** 20)
    return a, b, float(np.float32(full - a - b))


def project(nc, d, K):
    par, bc, w, L, Lrev, bb, Q, W, A8 = K.par, K.bc, K.w, K.L, K.Lrev, K.bb, K.Q, K.W, K.A8
    with Stage(nc, "proj") as S:
        xT = S.sb("xT", [P, KD, T])
        w_in = S.sb("w_in", [P, KD, UW + ZW])
        memT = S.sb("memT", [P, KD, MEM])
        w_mem = S.sb("w_mem", [P, KD, 512])
        g1 = S.sb("g1", [P, 2, KD])
        gains = S.sb("gains", [P, ROWK + 4, HD])
        rope = S.sb("rope", [P, NT, 2, HD])
        square = S.sb("square", [P, D])
        x = S.sb("x", [P, 3, D])
        tmp = S.sb("tmp", [P, GP, CH + 1, C])
        NJOB = NT + 2
        QC = (UW + ZW) // 4
        ss = S.sb("ss", [P, NJOB])
        rstd = S.sb("rstd", [P, NJOB])
        z = S.sb("z", [P, 2, ZW])
        u = S.sb("u", [P, 2, UW])
        sq = S.sb("sq", [P, ROWK, HD])
        hs = S.sb("hs", [P, ROWK])
        hr = S.sb("hr", [P, ROWK])
        rc = S.sb("rc", [P, ROWH, HD])
        rs = S.sb("rs", [P, ROWH, HD])
        zn = S.sb("zn", [P, 4, ROWK * HD])
        pz = [S.ps(f"pz{i}", [P, 3 * 512]) for i in range(2)]
        pt = S.ps("pt", [P, 2 * 512])

        s_small = S.sem("small_landed")
        s_x = [S.sem(f"rows{j}_landed") for j in range(NJOB)]
        s_id = S.sem("ident_landed")
        s_par = S.sem("params_landed")
        s_ta = S.sem("tables_act")
        s_tv = S.sem("tables_dve")
        s_pw = S.sem("powers")
        s_pool = S.sem("pool_chain")
        s_k = [S.sem(f"k{k}_landed") for k in range(KD)]
        s_m = [S.sem(f"m{k}_landed") for k in range(2)]
        s_gain = S.sem("gained")
        s_ss = S.sem("squares")
        s_std = S.sem("std")
        s_rstd = S.sem("rstd")
        s_mm = S.sem("projected")
        s_z = S.sem("evacuated")
        s_u = [S.sem(f"u_stored{i}") for i in range(2)]
        s_hs = S.sem("head_squares")
        s_hq = S.sem("head_std")
        s_zn = S.sem("normed")
        s_t = S.sem("transposed")
        s_te = S.sem("transposes_out")
        s_out = S.sem("stored")
        s_v = S.sem("dve_chain")
        s_init = S.sem("init")

        rows = ROWS + [P, P]

        with S.block() as block:
            @block.sync
            def _(sp):
                sp.dma_start(K.ident[:, :], d["ident"]).then_inc(s_id, 16)
                sp.dma_start(g1[:, :, :], d["g1T"]).then_inc(s_small, 16)
                for k in range(KD):
                    sp.dma_start(xT[:, k, :], d["xT"][:, k, :]).then_inc(s_k[k], 16)
                    sp.dma_start(w_in[:, k, :], d["w_in"][:, k, :]).then_inc(s_k[k], 16)
                    if k == 3:
                        sp.dma_start(x[:, 0, :], d["x_tok"][0:P, :]).then_inc(s_x[0], 16)
                sp.dma_start(gains[:, :, :], d["gains"]).then_inc(s_small, 16)
                sp.dma_start(rope[:, :, :, :], d["rope"]).then_inc(s_small, 16)
                sp.dma_start(x[:, 1, :], d["x_tok"][P:2 * P, :]).then_inc(s_x[1], 16)
                sp.dma_start(x[:, 2, :], d["x_tok"][2 * P:3 * P, :]).then_inc(s_x[2], 16)
                sp.dma_start(memT[:, :, :], d["memT"]).then_inc(s_m[0], 16)
                sp.dma_start(w_mem[:, :, :], d["w_mem"]).then_inc(s_m[1], 16)
                for j in (3, 4):
                    sp.wait_ge(s_ss, j - 2)
                    sp.dma_start(x[:rows[j], j % 3, :], d["x_tok"][j * P:j * P + rows[j], :]).then_inc(s_x[j], 16)
                for j in range(NT):
                    sp.wait_ge(s_z, j + 1)
                    r = rows[j]
                    sp.dma_start(d["u_scratch"][j * P:j * P + r, :], u[:r, j % 2, :]).then_inc(s_u[j % 2], 16)
                    if j < 2:
                        sp.wait_ge(s_ss, j + 3)
                        sp.dma_start(x[:, (NT + j) % 3, :], d["mem_tok"][:, j, :]).then_inc(s_x[NT + j], 16)
                sp.wait_ge(s_zn, NT)
                sp.dma_start(d["p_win_k"], zn[:, 3, 256:384]).then_inc(s_out, 16)
                sp.dma_start(d["p_win_v"], K.v[:, 3, :]).then_inc(s_out, 16)
                for b in range(NSEQ):
                    q = slice(b * DSEQ, (b + 1) * DSEQ)
                    sp.dma_start(d["s_win_k"][b, WIN - DSEQ:, :], zn[q, 0, 256:384]).then_inc(s_out, 16)
                    sp.dma_start(d["s_win_v"][b, WIN - DSEQ:, :], K.v[q, 4, :]).then_inc(s_out, 16)
                sp.dma_start(d["s_win_k"][:, 0:WIN - DSEQ, :], d["cache_k"][:, DSEQ:, :]).then_inc(s_out, 16)
                sp.dma_start(d["s_win_v"][:, 0:WIN - DSEQ, :], d["cache_v"][:, DSEQ:, :]).then_inc(s_out, 16)
                sp.wait_ge(s_zn, NJOB)
                for m in range(2):
                    sp.dma_start(d["p_mem_k"][m * P:(m + 1) * P, :], zn[:, (NT + m) % 4, 0:256]).then_inc(s_out, 16)
                    sp.dma_start(d["p_mem_v"][m * P:(m + 1) * P, :], K.mv[:, m, :]).then_inc(s_out, 16)
                for i in range(2):
                    sp.wait_ge(s_u[i], 16 * (3 - i))
                sp.wait_ge(s_out, 16 * (2 + 2 * NSEQ + 2 + 4))

            @block.gpsimd
            def _(pool):
                tt = pool.tensor_tensor
                pool.dma_start(par[:, :, :], d["ssm_par"]).then_inc(s_par, 16)
                pool.dma_start(bc[:, :, :, :], d["ssm_bc"]).then_inc(s_par, 16)
                pool.dma_start(K.dsk[:, :], d["ssm_d"]).then_inc(s_par, 16)
                pool.dma_start(K.s0[:, :, :, :], d["ssm_s0"]).then_inc(s_par, 16)
                step = Chain(pool, s_pool)
                pool.wait_ge(s_pw, 1)
                lr = widen(Lrev[:, 0, :, :].rearrange("p t g -> p g t"), 3, C)
                li = widen(Lrev[:, 1, :, :].rearrange("p t g -> p g t"), 3, C)
                b_r, b_i = widen(bb[:, 0, :, :], 2, CH), widen(bb[:, 1, :, :], 2, CH)
                t1 = tmp[:, :, 0:CH, :]
                for n, (x0, y0, op) in enumerate(((b_r, b_i, ALU.subtract), (b_i, b_r, ALU.add))):
                    o = W[:, n, :, :, :]
                    tt(o, lr, x0, ALU.mult)
                    step(tt(t1, li, y0, ALU.mult))
                    step(tt(o, o, t1, op))
                lr = widen(L[:, 0, :, :].rearrange("p t g -> p g t"), 3, C)
                li = widen(L[:, 1, :, :].rearrange("p t g -> p g t"), 3, C)
                ln = widen(L[:, 2, :, :].rearrange("p t g -> p g t"), 3, C)
                c_r, c_i = widen(bc[:, 2, :, :], 2, CH + 1), widen(bc[:, 3, :, :], 2, CH + 1)
                for n, (x0, y0) in enumerate(((lr, li), (ln, lr))):
                    o = Q[:, n, :, :, :]
                    tt(o, c_r, x0, ALU.mult)
                    step(tt(tmp[:, :, :, :], c_i, y0, ALU.mult))
                    step(tt(o, o, tmp[:, :, :, :], ALU.subtract))

            @block.scalar
            def _(act):
                act.wait_ge(s_par, 64)
                act.activation(w[:, 0, :], par[:, 0, :], ACT.Exp).then_inc(s_ta, 1)
                act.wait_ge(s_tv, 1)
                act.activation(w[:, 3, :], w[:, 1, :], ACT.Exp).then_inc(s_ta, 1)
                act.wait_ge(s_tv, 2)
                act.activation(w[:, 6:8, :], w[:, 4:6, :], ACT.Sin).then_inc(s_ta, 1)

                def row_norm(j):
                    r = rows[j]
                    src = x[:r, j % 3, :]
                    act.wait_ge(s_x[j], 16)
                    act.activation(square[:r, :], src, ACT.Square, accum_out=ss[:r, j:j + 1]).then_inc(s_ss, 1)
                    act.wait_ge(s_ss, j + 1)
                    act.activation(rstd[:r, j:j + 1], ss[:r, j:j + 1], ACT.Sqrt, bias=K.eps[:r, 0:1],
                                   scale=1.0 / D).then_inc(s_std, 1)

                def out_of_transposes(j):
                    act.wait_ge(s_t, j + 1)
                    r = rows[j]
                    if j < NT:
                        act.activation(K.qkT[:, :, j * P:j * P + r], pt[:, 0:5 * P].rearrange("p (c t) -> p c t", t=P)[:, :, :r],
                                       ACT.Copy).then_inc(s_te, 1)
                    else:
                        m = j - NT
                        act.activation(K.mkT[:, :, m * P:(m + 1) * P], pt[:, 0:2 * P].rearrange("p (c t) -> p c t", t=P),
                                       ACT.Copy).then_inc(s_te, 1)

                act.wait_ge(s_init, 1)
                row_norm(0)
                for j in range(NJOB):
                    r = rows[j]
                    if j + 1 < NJOB:
                        row_norm(j + 1)
                    act.wait_ge(s_rstd, j + 1)
                    act.wait_ge(s_mm, j + 1)
                    if j >= 2:
                        act.wait_ge(s_zn, j - 1)
                        if j < NT:
                            act.wait_ge(s_u[j % 2], 16 * (j // 2))
                    if j == NT - 1:
                        for dst, lo, hi in ((u[:r, j % 2, :], 0, UW), (z[:r, j % 2, :], UW, UW + 640), (K.v[:r, j, :], UW + 640, UW + ZW)):
                            for q in range(4):
                                a, b = max(lo, q * QC), min(hi, (q + 1) * QC)
                                if a < b:
                                    ins = act.activation(dst[:, a - lo:b - lo], pz[j % 2][q * r:(q + 1) * r, a - q * QC:b - q * QC],
                                                         ACT.Copy, scale=rstd[:r, j:j + 1])
                        ins.then_inc(s_z, 1)
                    elif j < NT:
                        act.activation(u[:r, j % 2, :], pz[j % 2][:r, 0:UW], ACT.Copy, scale=rstd[:r, j:j + 1])
                        act.activation(K.v[:r, j, :], pz[j % 2][:r, UW + 640:UW + ZW], ACT.Copy, scale=rstd[:r, j:j + 1])
                        act.activation(z[:r, j % 2, 0:640], pz[j % 2][:r, UW:UW + 640], ACT.Copy,
                                       scale=rstd[:r, j:j + 1]).then_inc(s_z, 1)
                    else:
                        act.activation(K.mv[:, j - NT, :], pz[j % 2][:, 256:512], ACT.Copy, scale=rstd[:, j:j + 1])
                        act.activation(z[:, j % 2, 0:256], pz[j % 2][:, 0:256], ACT.Copy,
                                       scale=rstd[:, j:j + 1]).then_inc(s_z, 1)
                    nh = ROWK if j < NT else 4
                    act.wait_ge(s_hs, j + 1)
                    act.activation(hr[:r, :nh], hs[:r, :nh], ACT.Sqrt, bias=K.eps[:r, 0:1], scale=1.0 / HD).then_inc(s_hq, 1)
                    if j >= 1:
                        out_of_transposes(j - 1)
                out_of_transposes(NJOB - 1)

            @block.vector
            def _(dve):
                step = Chain(dve, s_v)
                tt = dve.tensor_tensor
                dve.memset(L[:, 0, 0, :], 1.0)
                dve.memset(L[:, 1:3, 0, :], 0.0)
                dve.memset(K.eps[:, :], EPS).then_inc(s_init, 1)
                dve.wait_ge(s_small, 16)
                for k in range(KD):
                    dve.wait_ge(s_k[k], 32)
                    dve.tensor_scalar(xT[:, k, :], xT[:, k, :], g1[:, 0, k:k + 1], None, ALU.mult).then_inc(s_gain, 1)
                dve.wait_ge(s_par, 64)
                dve.wait_ge(s_ta, 1)
                tt(w[:, 1, :], par[:, 1, :], w[:, 0, :], ALU.mult).then_inc(s_tv, 1)
                step(tt(w[:, 2, :], par[:, 2, :], w[:, 0, :], ALU.mult))
                a, b, c = two_pi_parts()
                for n, quarter in enumerate((0.0, 0.25)):
                    k = w[:, 8 + n, :]
                    step(dve.tensor_scalar(k, w[:, 2, :], float(1 / (2 * np.pi)), quarter, ALU.mult, ALU.add))
                    step(dve.tensor_scalar(k, k, 12582912.0, None, ALU.add))
                    step(dve.tensor_scalar(k, k, -12582912.0, None, ALU.add))
                    r = w[:, 4 + n, :]
                    step(dve.scalar_tensor_tensor(r, k, -a, w[:, 2, :], ALU.mult, ALU.add))
                    step(dve.scalar_tensor_tensor(r, k, -b, r, ALU.mult, ALU.add))
                    step(dve.scalar_tensor_tensor(r, k, -c, r, ALU.mult, ALU.add))
                    if n:
                        step(dve.tensor_scalar(r, r, float(np.pi / 2), None, ALU.add))
                    ins = dve.tensor_scalar(r, r, 3.1415925, -3.1415925, ALU.min, ALU.max)
                    if n:
                        ins.then_inc(s_tv, 1)
                    else:
                        step(ins)
                dve.wait_ge(s_std, 1)
                dve.reciprocal(rstd[:, 0:1], rstd[:, 0:1]).then_inc(s_rstd, 1)
                dve.wait_ge(s_ta, 3)
                tt(L[:, 0, 1, :], w[:, 3, :], w[:, 7, :], ALU.mult)
                step(tt(L[:, 1, 1, :], w[:, 3, :], w[:, 6, :], ALU.mult))
                ar, ai = par[:, 1, :], par[:, 2, :]
                step(dve.tensor_scalar(w[:, 10, :], L[:, 0, 1, :], 1.0, None, ALU.subtract))
                lm, li = w[:, 10, :], L[:, 1, 1, :]
                tt(w[:, 11, :], ar, ar, ALU.mult)
                tt(w[:, 12, :], ai, ai, ALU.mult)
                tt(w[:, 13, :], lm, ar, ALU.mult)
                tt(w[:, 14, :], li, ai, ALU.mult)
                tt(w[:, 15, :], li, ar, ALU.mult)
                step(tt(w[:, 16, :], lm, ai, ALU.mult))
                tt(w[:, 11, :], w[:, 11, :], w[:, 12, :], ALU.add)
                tt(w[:, 13, :], w[:, 13, :], w[:, 14, :], ALU.add)
                step(tt(w[:, 15, :], w[:, 15, :], w[:, 16, :], ALU.subtract))
                step(dve.reciprocal(w[:, 11, :], w[:, 11, :]))
                tt(w[:, 17, :], w[:, 13, :], w[:, 11, :], ALU.mult)
                step(tt(w[:, 18, :], w[:, 15, :], w[:, 11, :], ALU.mult))
                zr, zi = widen(w[:, 17, :], 2, C), widen(w[:, 18, :], 2, C)
                t4 = [tmp[:, :, n, :] for n in range(4)]
                br, bi = bc[:, 0, :, :], bc[:, 1, :, :]
                tt(t4[0], zr, br, ALU.mult)
                tt(t4[1], zi, bi, ALU.mult)
                tt(t4[2], zr, bi, ALU.mult)
                step(tt(t4[3], zi, br, ALU.mult))
                tt(bb[:, 0, :, :], t4[0], t4[1], ALU.subtract)
                step(tt(bb[:, 1, :, :], t4[2], t4[3], ALU.add))
                for m in (1, 2, 4):
                    lo, hi = slice(1, m + 1), slice(m + 1, 2 * m + 1)
                    mr, mi = widen(L[:, 0, m, :], 1, m), widen(L[:, 1, m, :], 1, m)
                    q = [tmp[:, 4 * n:4 * n + m, 0, :] for n in range(4)]
                    tt(q[0], L[:, 0, lo, :], mr, ALU.mult)
                    tt(q[1], L[:, 1, lo, :], mi, ALU.mult)
                    tt(q[2], L[:, 0, lo, :], mi, ALU.mult)
                    step(tt(q[3], L[:, 1, lo, :], mr, ALU.mult))
                    tt(L[:, 0, hi, :], q[0], q[1], ALU.subtract)
                    step(tt(L[:, 1, hi, :], q[2], q[3], ALU.add))
                dve.tensor_scalar(L[:, 2, 1:, :], L[:, 1, 1:, :], -1.0, None, ALU.mult)
                for t in range(CH):
                    ins = dve.tensor_copy(Lrev[:, :, t, :], L[:, 0:2, CH - 1 - t, :])
                step(ins)
                for o in range(2):
                    dve.tensor_copy(A8[:, o, o, :], L[:, 0, CH, :])
                dve.tensor_copy(A8[:, 0, 1, :], L[:, 2, CH, :])
                dve.tensor_copy(A8[:, 1, 0, :], L[:, 1, CH, :]).then_inc(s_pw, 1)
                dve.wait_ge(s_small, 48)
                dve.wait_ge(s_m[0], 16)
                for k in range(KD):
                    dve.tensor_scalar(memT[:, k, :], memT[:, k, :], g1[:, 1, k:k + 1], None, ALU.mult).then_inc(s_gain, 1)

                def rstd_of(j):
                    dve.wait_ge(s_std, j + 1)
                    dve.reciprocal(rstd[:rows[j], j:j + 1], rstd[:rows[j], j:j + 1]).then_inc(s_rstd, 1)

                for j in range(NJOB):
                    r = rows[j]
                    nh = ROWK if j < NT else 4
                    g0 = 0 if j < NT else ROWK
                    zj = z[:r, j % 2, 0:nh * HD].rearrange("p (h c) -> p h c", c=HD)
                    if j + 1 < NJOB:
                        rstd_of(j + 1)
                    if j >= 4:
                        dve.wait_ge(s_t, j - 3)
                    out = zn[:r, j % 4, 0:nh * HD].rearrange("p (h c) -> p h c", c=HD)
                    dve.wait_ge(s_z, j + 1)
                    step(dve.tensor_tensor(sq[:r, :nh, :], zj, zj, ALU.mult))
                    dve.tensor_reduce(hs[:r, :nh], sq[:r, :nh, :], AX.X, ALU.add).then_inc(s_hs, 1)
                    dve.wait_ge(s_hq, j + 1)
                    step(dve.reciprocal(hr[:r, :nh], hr[:r, :nh]))
                    step(dve.tensor_tensor(out, zj, widen(hr[:r, :nh], 2, HD), ALU.mult))
                    last = dve.tensor_tensor(out, out, gains[:r, g0:g0 + nh, :], ALU.mult)
                    if j < NT:
                        step(last)
                        rot = out[:, 0:ROWH, :]
                        dve.tensor_tensor(rc[:r, :, :], rot, widen(rope[:r, j, 0, :], 1, ROWH), ALU.mult)
                        step(dve.tensor_tensor(rs[:r, :, :], rot, widen(rope[:r, j, 1, :], 1, ROWH), ALU.mult))
                        h = HD // 2
                        dve.tensor_tensor(rot[:, :, 0:h], rc[:r, :, 0:h], rs[:r, :, h:HD], ALU.subtract)
                        last = dve.tensor_tensor(rot[:, :, h:HD], rc[:r, :, h:HD], rs[:r, :, 0:h], ALU.add)
                    last.then_inc(s_zn, 1)

            @block.tensor
            def _(pe):
                def transposes(j):
                    r = rows[j]
                    pe.wait_ge(s_zn, j + 1)
                    if j >= 1:
                        pe.wait_ge(s_te, j)
                    for c in range(5 if j < NT else 2):
                        mm = pe.transpose(pt[:, c * P:c * P + r], zn[:r, j % 4, c * P:(c + 1) * P], K.ident[:r, :r])
                    mm.then_inc(s_t, 1)

                pe.wait_ge(s_id, 16)
                for j in range(NJOB):
                    r = rows[j]
                    if j >= 2:
                        pe.wait_ge(s_z, j - 1)
                    if j >= NT:
                        pe.wait_ge(s_m[1], 16)
                        pe.wait_ge(s_gain, 2 * KD)
                    for k in range(KD):
                        if j == 0:
                            pe.wait_ge(s_k[k], 32)
                            pe.wait_ge(s_gain, k + 1)
                        if j == NT - 1:
                            for q in range(4):
                                mm = pe.matmul(pz[j % 2][q * NSMP:(q + 1) * NSMP, 0:QC], xT[:, k, j * P:j * P + r],
                                               w_in[:, k, q * QC:(q + 1) * QC], start=(k == 0), stop=(k == KD - 1))
                        elif j < NT:
                            for c in range(0, UW + ZW, 512):
                                w = min(512, UW + ZW - c)
                                mm = pe.matmul(pz[j % 2][:r, c:c + w], xT[:, k, j * P:j * P + r], w_in[:, k, c:c + w],
                                               start=(k == 0), stop=(k == KD - 1))
                        else:
                            m = j - NT
                            mm = pe.matmul(pz[j % 2][:, 0:512], memT[:, k, m * P:(m + 1) * P], w_mem[:, k, :],
                                           start=(k == 0), stop=(k == KD - 1))
                    mm.then_inc(s_mm, 1)
                    if j >= 1:
                        transposes(j - 1)
                transposes(NJOB - 1)


def blend(nc, d, K):
    NC = NJ + 2 * NSEQ
    L, bb, Q, W, A8, s0 = K.L, K.bb, K.Q, K.W, K.A8, K.s0
    with Stage(nc, "blend") as S:
        room = K.wq[:, :, :].rearrange("p k c -> p (k c)")
        uch = room[:, 0:CH * UW].rearrange("p (t c) -> p t c", t=CH)
        WT = room[:, 4096:8192].rearrange("p (r g x) -> p r g x", r=2, g=GP)
        ZK = room[:, 8192:8192 + G * ((CH - 1) * C + P)].rearrange("p (g x) -> p g x", g=G)
        dI = S.sb("dI", [C, G, C])
        MT = S.sb("MT", [P, G, P])
        U = S.sb("U", [P, G, NC])
        V = K.wg[:, :, :].rearrange("p a b -> p (a b)")[:, 0:2 * GP * NC].rearrange("p (r g j) -> p r g j", r=2, g=GP)
        prod = S.sb("prod", [P, 2, 2, GP])
        part = S.sb("part", [P, 2, GP])
        fin = S.sb("fin", [P, 2, GP])
        sfin = S.sb("sfin", [P, 2, GP, NSEQ])
        st = S.sb("st", [P, 2, GP, NSEQ])
        mask = S.sb("mask", [P, 256])
        bmask = S.sb("bmask", [P, NSEQ])
        sinks = S.sb("sinks", [P, 5])
        flat = lambda t, spec: t.rearrange("p " + spec + " -> p (" + spec + ")")
        SPv = flat(W[:, :, :, :, :], "a g t c")[:, 0:2 * GP * COLS].rearrange("p (r g j) -> p r g j", r=2, g=GP)
        mcT = room[:, 0:4096].rearrange("p (a b m) -> p a b m", a=2, b=NSEQ)
        mcv = room[:, 4096:8192].rearrange("p (a b m) -> p a b m", a=2, b=NSEQ)
        soft = room[:, 8192:]
        sm, pr, prT = (soft[:, 2048 * n:2048 * (n + 1)].rearrange("p (a x) -> p a x", a=2) for n in range(3))
        smask = soft[:, 6144:6144 + NSEQ * WIN + NSMP]
        yroom = flat(K.y[:, :, :], "t c")
        ug = yroom[0:NC, :].rearrange("p (g x) -> p g x", g=G)
        big = yroom[:, 0:2048]
        kcT = yroom[:, 2048:3072].rearrange("p (b w) -> p b w", b=NSEQ)
        vc = yroom[:, 3072:4096].rearrange("p (b w) -> p b w", b=NSEQ)
        mx = S.sb("mx", [P, 2, 4])
        nm = S.sb("nm", [P, 2, 4])
        den = S.sb("den", [P, 2, 4])
        es = S.sb("es", [P, 2, 4])
        pp = S.ps("pp", [P, 8, 512])
        banks = pp[:, :, :].rearrange("p b x -> p (b x)")
        sc, tp = banks[:, 0:2048], banks[:, 2048:3072]
        ov = pp[:, 6:8, :]

        s_mask = S.sem("masks_landed")
        s_cache = S.sem("caches_landed")
        s_sc = S.sem("scores")
        s_sm = S.sem("scores_read")
        s_mx = S.sem("maxima")
        s_ex = S.sem("exps")
        s_pr = S.sem("probs")
        s_tp = S.sem("probs_turned")
        s_te = S.sem("turned_out")
        s_ov = S.sem("values")
        s_oe = S.sem("values_out")

        s_smask = S.sem("sample_mask_landed")
        s_ug = S.sem("chunks_grouped")
        s_uch = S.sem("chunks_landed")
        s_mt = S.sem("toeplitz_landed")
        s_v = S.sem("dve_chain")
        s_g = S.sem("pool_chain")
        s_uz = S.sem("uch_zeroed")
        s_ut = S.sem("u_turned")
        s_ue = S.sem("u_out")
        s_wt = S.sem("w_turned")
        s_we = S.sem("w_out")
        s_kt = S.sem("kernels")
        s_ke = S.sem("kernels_out")
        s_z = S.sem("kernels_ready")
        s_vm = S.sem("inputs_summed")
        s_ve = S.sem("inputs_out")
        s_scan = S.sem("scanned")
        s_ym = S.sem("y_summed")
        s_ye = S.sem("y_out")
        s_sf = S.sem("sample_state")
        s_out = S.sem("stored")


        units = [("win", 0), ("win", 1), ("win", 2), ("swin", 4), ("win", 3), ("mem", 0), ("smem", 4), ("mem", 1), ("mem", 2), ("mem", 3)]
        NU = len(units)

        def shape(kind, i):
            if kind == "win":
                return 4, 256, (128 if i == 0 else 0)
            if kind == "mem":
                return 4, 256, 0
            if kind == "swin":
                return 1, WIN + NSMP, 0
            return 1, 256, 0

        def probs(buf, kind, i, n):
            h, w, lo = shape(kind, i)
            if h == 4:
                return buf[:, n % 2, :].rearrange("p (h k) -> p h k", h=4)[:, :, lo:]
            return buf[:, n % 2, 0:w].unsqueeze(1)

        UB, VB = 6, 3
        ub = [range(i, min(i + UB, G)) for i in range(0, G, UB)]
        vb = [range(i, min(i + VB, GP)) for i in range(0, GP, VB)]

        with S.block() as block:
            @block.sync
            def _(sp):
                us = d["u_scratch"]
                smp = us[SEQ:T, :].rearrange("(b t) c -> b t c", t=DSEQ)
                sp.dma_start(uch[0:NJ, :, :], us[0:SEQ, :].rearrange("(j t) c -> j t c", t=CH)).then_inc(s_uch, 16)
                sp.wait_ge(s_uz, 1)
                sp.dma_start(uch[NJ:NJ + NSEQ, 0:DSEQ, :], smp).then_inc(s_uch, 16)
                sp.dma_start(uch[NJ + NSEQ:NC, DSEQ:CH, :], smp).then_inc(s_uch, 16)
                sp.dma_start(mask[:, :], d["mask"]).then_inc(s_mask, 16)
                sp.dma_start(sinks[:, :], d["sinks"]).then_inc(s_mask, 16)
                sp.dma_start(bmask[:, :], d["bmask"]).then_inc(s_mask, 16)
                sp.wait_ge(s_z, 1)
                for t in range(CH):
                    o = (CH - 1 - t) * C
                    sp.dma_start(MT[t * C:(t + 1) * C, :, :], ZK[0:C, :, o:o + P]).then_inc(s_mt, 16)
                sp.wait_ge(s_ug, 1)
                sp.dma_start(mcT, d["mcT"]).then_inc(s_cache, 16)
                sp.wait_ge(s_ut, len(ub))
                sp.dma_start(kcT, d["kcT"]).then_inc(s_cache, 16)
                sp.dma_start(vc, d["vc"]).then_inc(s_cache, 16)
                sp.wait_ge(s_mt, 16 * CH)
                sp.dma_start(smask, d["smask"]).then_inc(s_smask, 16)
                sp.wait_ge(s_vm, len(vb))
                sp.dma_start(mcv, d["mcv"]).then_inc(s_cache, 16)
                sp.wait_ge(s_scan, 1)
                sp.dma_start(d["p_ssm"], fin[:, :, :]).then_inc(s_out, 16)
                sp.wait_ge(s_sf, 1)
                sp.dma_start(d["s_ssm"], sfin[:, :, :, :]).then_inc(s_out, 16)
                sp.dma_start(K.wg[:, 0:4, :], d["w_glu"]).then_inc(K.s_wg, 16)
                sp.wait_ge(s_oe, NU)
                sp.dma_start(K.wq[:, :, :], d["wq"]).then_inc(K.s_wq, 16)
                sp.wait_ge(s_out, 32)

            @block.gpsimd
            def _(pool):
                n = 0
                pool.memset(uch[NJ:NC, :, :], 0.0).then_inc(s_uz, 1)
                pool.wait_ge(s_uz, 1)
                pool.wait_ge(s_wt, 8)
                pool.tensor_copy(SPv[:, :, :, NJ:COLS], s0[:, :, :, :])
                pool.memset(SPv[:, :, :, 0:1], 0.0).then_inc(s_g, 1)
                n += 1
                pool.wait_ge(s_ve, len(vb))
                for j in range(NJ):
                    pool.wait_ge(s_g, n)
                    pool.tensor_tensor(prod[:, :, :, :], A8[:, :, :, :], widen(SPv[:, :, :, j], 1, 2), ALU.mult).then_inc(s_g, 1)
                    n += 1
                    pool.wait_ge(s_g, n)
                    pool.tensor_tensor(part[:, :, :], prod[:, :, 0, :], prod[:, :, 1, :], ALU.add).then_inc(s_g, 1)
                    n += 1
                    pool.wait_ge(s_g, n)
                    dst = SPv[:, :, :, j + 1] if j + 1 < NJ else fin[:, :, :]
                    pool.tensor_tensor(dst, part[:, :, :], V[:, :, :, j], ALU.add).then_inc(s_g, 1)
                    n += 1
                pool.wait_ge(s_g, n)
                pool.engine_nop().then_inc(s_scan, 1)

            @block.tensor
            def _(pe):
                def scores(n):
                    kind, i = units[n]
                    at = (n % 2) * 1024
                    if n >= 2:
                        pe.wait_ge(s_sm, n - 1)
                    big = ("swin", "smem")
                    if kind in big or n and units[n - 1][0] in big:
                        pe.wait_ge(s_sm, n)
                    if kind in big:
                        pe.wait_ge(s_cache, 64)
                    tok = slice(i * P, i * P + ROWS[i])
                    for h in range(4):
                        lo, hi = (h % 2) * HD, (h % 2) * HD + HD
                        slot = (h % 2) * 2 + h // 2
                        if kind == "win":
                            a = 128 if i == 0 else 0
                            mm = pe.matmul(sc[:, at + slot * 256 + a:at + slot * 256 + 256], K.qkT[lo:hi, h // 2, tok],
                                           K.qkT[lo:hi, 2, (i - 1) * P + a:(i + 1) * P], start=True, stop=True)
                        elif kind == "mem":
                            mm = pe.matmul(sc[:, at + slot * 256:at + slot * 256 + 256], K.qkT[lo:hi, 3 + h // 2, tok],
                                           K.mkT[lo:hi, h // 2, :], start=True, stop=True)
                        elif kind == "swin":
                            for c in range(2):
                                pe.matmul(sc[h * 32:h * 32 + 32, c * 512:(c + 1) * 512], K.qkT[lo:hi, h // 2, tok],
                                          kcT[lo:hi, c * 4:(c + 1) * 4, :], start=True, stop=True)
                            mm = pe.matmul(sc[h * 32:h * 32 + 32, 1024:1024 + NSMP], K.qkT[lo:hi, h // 2, tok],
                                           K.qkT[lo:hi, 2, SEQ:T], start=True, stop=True)
                        else:
                            for c in range(4):
                                mm = pe.matmul(sc[h * 32:h * 32 + 32, c * 512:(c + 1) * 512], K.qkT[lo:hi, 3 + h // 2, tok],
                                               mcT[lo:hi, h // 2, c * 2:(c + 1) * 2, :], start=True, stop=True)
                    mm.then_inc(s_sc, 1)

                def turn(n):
                    kind, i = units[n]
                    h, w, lo = shape(kind, i)
                    pe.wait_ge(s_pr, n + 1)
                    if n >= 1:
                        pe.wait_ge(s_te, n)
                    if h == 4:
                        for x in range(4):
                            for m in range(lo // 128, 2):
                                mm = pe.transpose(tp[:, (2 * x + m) * P:(2 * x + m + 1) * P],
                                                  pr[:, n % 2, x * 256 + m * P:x * 256 + (m + 1) * P], K.ident[:, :])
                    else:
                        pe.transpose(tp[:, 0:P], pr[:, n % 2, 0:P], K.ident[:, :])
                        mm = pe.transpose(tp[0:w - P, P:2 * P], pr[:, n % 2, P:w], K.ident[:, :])
                    mm.then_inc(s_tp, 1)

                def values(n):
                    kind, i = units[n]
                    pe.wait_ge(s_te, n + 1)
                    if n >= 2:
                        pe.wait_ge(s_oe, n - 1)
                    o = ov[:, n % 2, 0:256].rearrange("p (c q) -> p c q", c=2)
                    pT = prT[:, n % 2, :]
                    for c in range(2):
                        for m in range(2):
                            for e in range(2):
                                out = o[e * HD:e * HD + HD, c, :]
                                if kind == "win" and (i or m):
                                    h = 2 * c + e
                                    mm = pe.matmul(out, K.v[:, i - 1 + m, c * HD:c * HD + HD],
                                                   pT[:, (2 * h + m) * P:(2 * h + m + 1) * P], start=(m == 0 or i == 0), stop=(m == 1))
                                elif kind == "mem":
                                    h, x = 2 * e + c, 2 * c + e
                                    mm = pe.matmul(out, K.mv[:, m, x * HD:x * HD + HD],
                                                   pT[:, (2 * h + m) * P:(2 * h + m + 1) * P], start=(m == 0), stop=(m == 1))
                                elif kind == "swin" and m == 0:
                                    h = 2 * e + c
                                    pe.matmul(out[:, 0:NSMP], K.v[0:NSMP, 4, c * HD:c * HD + HD],
                                              pT[0:NSMP, P + h * 32:P + h * 32 + 32], start=True, stop=False)
                        if kind == "swin":
                            for b in range(NSEQ):
                                for e in range(2):
                                    q = slice(b * DSEQ, (b + 1) * DSEQ)
                                    h = 2 * e + c
                                    mm = pe.matmul(o[e * HD:e * HD + HD, c, q], vc[:, b, c * HD:c * HD + HD],
                                                   pT[:, h * 32 + b * DSEQ:h * 32 + (b + 1) * DSEQ],
                                                   start=False, stop=(b == NSEQ - 1))
                        elif kind == "smem":
                            for b in range(NSEQ):
                                q = slice(b * DSEQ, (b + 1) * DSEQ)
                                for m in range(2):
                                    for e in range(2):
                                        h = 2 * c + e
                                        mm = pe.matmul(o[e * HD:e * HD + HD, c, q], mcv[:, m, b, h * HD:h * HD + HD],
                                                       pT[:, m * P + h * 32 + b * DSEQ:m * P + h * 32 + (b + 1) * DSEQ],
                                                       start=(m == 0), stop=(m == 1))
                    mm.then_inc(s_ov, 1)

                for n in range(8):
                    for m in range(4):
                        mm = pe.transpose(pp[:, n, m * P:(m + 1) * P],
                                          W[:, n // 4, (n % 4) * 4 + m, :, :].rearrange("p t c -> p (t c)"), K.ident[:, :])
                    mm.then_inc(s_wt, 1)
                for n in range(0, 8, 2):
                    pe.wait_ge(s_we, n + 2)
                    for m in range(4):
                        for ri in range(2):
                            for e in range(2):
                                h = slice(e * N, e * N + N)
                                gp = n * 2 + m
                                mm = pe.matmul(pp[0:C, n + e, m * P:(m + 1) * P], bb[h, ri, gp, :], Q[h, ri, gp, 0:CH, :],
                                               start=(ri == 0), stop=(ri == 1))
                                if m == 3 and ri == 1:
                                    mm.then_inc(s_kt, 1)
                pe.wait_ge(s_ug, 1)
                for n, gs in enumerate(ub):
                    pe.wait_ge(s_ke, n + 1)
                    for m, g in enumerate(gs):
                        mm = pe.transpose(pp[:, n, m * NC:(m + 1) * NC], ug[:, g, :], K.ident[:NC, :NC])
                    mm.then_inc(s_ut, 1)
                for n, gs in enumerate(vb):
                    pe.wait_ge(s_ue, min(n + 1, len(ub)))
                    for m, gp in enumerate(gs):
                        for ri in range(2):
                            for e in range(2):
                                h = slice(e * N, e * N + N)
                                mm = pe.matmul(pp[h, n, (m * 2 + ri) * NC:(m * 2 + ri + 1) * NC], WT[:, ri, gp, h],
                                               U[:, gp * 2 + e, :], start=True, stop=True)
                    mm.then_inc(s_vm, 1)
                pe.wait_ge(s_ke, 8)
                pe.wait_ge(s_ve, len(vb))
                scores(0)
                scores(1)
                turn(0)
                for n in range(NU):
                    if n + 2 < NU:
                        scores(n + 2)
                    if n + 1 < NU:
                        turn(n + 1)
                    values(n)
                pe.wait_ge(s_oe, NU)
                pe.wait_ge(s_mt, 16 * CH)
                pe.wait_ge(s_scan, 1)
                for n in range(0, 8, 2):
                    for m in range(4):
                        gp = n * 2 + m
                        o = [pp[0:COLS, n + e, m * P:(m + 1) * P] for e in range(2)]
                        for e in range(2):
                            pe.matmul(o[e], U[:, 2 * gp + e, 0:COLS], MT[:, 2 * gp + e, :], start=True, stop=False)
                        for ri in range(2):
                            for e in range(2):
                                h = slice(e * N, e * N + N)
                                mm = pe.matmul(o[e], SPv[h, ri, gp, :], Q[h, ri, gp, 1:CH + 1, :], start=False, stop=(ri == 1))
                                if m == 3 and ri == 1:
                                    mm.then_inc(s_ym, 1)

            @block.vector
            def _(dve):
                step = Chain(dve, s_v)
                tt = dve.tensor_tensor
                SCALE = float(HD) ** -0.5

                def maxima(n):
                    kind, i = units[n]
                    h, w, lo = shape(kind, i)
                    at = (n % 2) * 1024
                    if n >= 2:
                        dve.wait_ge(s_ex, n - 1)
                    dve.wait_ge(s_sc, n + 1)
                    dst = probs(sm, kind, i, n)
                    if kind == "win":
                        src = sc[:, at:at + 1024].rearrange("p (h k) -> p h k", h=4)[:, :, lo:]
                        ins = dve.scalar_tensor_tensor(dst, src, SCALE, widen(mask[:, lo:], 1, 4), ALU.mult, ALU.add)
                    elif kind == "mem":
                        ins = dve.tensor_scalar(sm[:, n % 2, :], sc[:, at:at + 1024], SCALE, None, ALU.mult)
                    elif kind == "swin":
                        W = NSEQ * WIN
                        dve.wait_ge(s_smask, 16)
                        ins = dve.scalar_tensor_tensor(big[:, 0:W + NSMP], sc[:, 0:W + NSMP], SCALE, smask, ALU.mult, ALU.add)
                    else:
                        ins = dve.scalar_tensor_tensor(big[:, :].rearrange("p (b k) -> p b k", b=NSEQ),
                                                       sc[:, :].rearrange("p (b k) -> p b k", b=NSEQ), SCALE,
                                                       widen(bmask[:, :], 2, MEM), ALU.mult, ALU.add)
                    ins.then_inc(s_sm, 1)
                    dve.wait_ge(s_sm, n + 1)
                    if h == 1:
                        k = WIN if kind == "swin" else MEM
                        ins = dve.tensor_reduce(sm[:, n % 2, 0:k], big[:, 0:NSEQ * k].rearrange("p (b k) -> p k b", b=NSEQ), AX.X, ALU.max)
                        if kind == "swin":
                            ins = dve.tensor_copy(sm[:, n % 2, k:k + NSMP], big[:, NSEQ * k:NSEQ * k + NSMP])
                        step(ins)
                    step(dve.tensor_reduce(mx[:, n % 2, 0:h], dst, AX.X, ALU.max))
                    if kind in ("win", "swin"):
                        snk = sinks[:, 0:4] if h == 4 else sinks[:, 4:5]
                        step(dve.tensor_tensor(mx[:, n % 2, 0:h], mx[:, n % 2, 0:h], snk, ALU.max))
                        dve.tensor_tensor(es[:, n % 2, 0:h], snk, mx[:, n % 2, 0:h], ALU.subtract)
                    dve.tensor_scalar(nm[:, n % 2, 0:h], mx[:, n % 2, 0:h], -1.0, None, ALU.mult).then_inc(s_mx, 1)

                def normalise(n):
                    kind, i = units[n]
                    h, w, lo = shape(kind, i)
                    dve.wait_ge(s_ex, n + 1)
                    if kind in ("win", "swin"):
                        step(dve.tensor_tensor(den[:, n % 2, 0:h], den[:, n % 2, 0:h], es[:, n % 2, 0:h], ALU.add))
                    step(dve.reciprocal(den[:, n % 2, 0:h], den[:, n % 2, 0:h]))
                    p = probs(pr, kind, i, n)
                    dve.tensor_tensor(p, p, widen(den[:, n % 2, 0:h], 2, w - lo), ALU.mult).then_inc(s_pr, 1)

                dve.memset(ZK[0:C, :, 0:(CH - 1) * C], 0.0)
                step(tt(dI[:, :, :], widen(K.ident[0:C, 0:C], 1, G), widen(K.dsk[:, :], 2, C), ALU.mult))
                dve.wait_ge(s_uch, 48)
                dve.tensor_copy(ug.rearrange("p g (t c) -> p g t c", c=C), uch[0:NC, :, :].rearrange("p t (g c) -> p g t c", c=C))\
                    .then_inc(s_ug, 1)
                dve.wait_ge(s_ke, 8)
                k0 = ZK[0:C, :, (CH - 1) * C:CH * C]
                tt(k0, k0, dI[:, :, :], ALU.add).then_inc(s_z, 1)
                dve.wait_ge(s_ve, len(vb))
                l4r, l4i = widen(L[:, 0, DSEQ, :], 2, NSEQ), widen(L[:, 1, DSEQ, :], 2, NSEQ)
                x0, x1 = s0[:, 0, :, :], s0[:, 1, :, :]
                for n, (x, y, op) in enumerate(((x0, x1, ALU.subtract), (x1, x0, ALU.add))):
                    tt(st[:, 0, :, :], l4r, x, ALU.mult)
                    step(tt(st[:, 1, :, :], l4i, y, ALU.mult))
                    step(tt(sfin[:, n, :, :], st[:, 0, :, :], st[:, 1, :, :], op))
                tt(sfin[:, :, :, :], sfin[:, :, :, :], V[:, :, :, NJ + NSEQ:NC], ALU.add).then_inc(s_sf, 1)
                dve.wait_ge(s_mask, 48)
                dve.wait_ge(s_mt, 16 * CH)
                maxima(0)
                maxima(1)
                normalise(0)
                for n in range(NU):
                    if n + 1 < NU:
                        normalise(n + 1)
                    if n + 2 < NU:
                        maxima(n + 2)

            @block.scalar
            def _(act):
                def exps(n):
                    kind, i = units[n]
                    h, w, lo = shape(kind, i)
                    act.wait_ge(s_mx, n + 1)
                    if n >= 2:
                        act.wait_ge(s_tp, n - 1)
                    src, dst = probs(sm, kind, i, n), probs(pr, kind, i, n)
                    if kind in ("win", "swin"):
                        act.activation(es[:, n % 2, 0:h], es[:, n % 2, 0:h], ACT.Exp)
                    for x in range(h):
                        ins = act.activation(dst[:, x, :], src[:, x, :], ACT.Exp, bias=nm[:, n % 2, x:x + 1],
                                             accum_out=den[:, n % 2, x:x + 1])
                    ins.then_inc(s_ex, 1)

                def turned(n):
                    kind, i = units[n]
                    h, w, lo = shape(kind, i)
                    act.wait_ge(s_tp, n + 1)
                    if n >= 2:
                        act.wait_ge(s_ov, n - 1)
                    if h == 4:
                        v = lambda t: t.rearrange("p (h m q) -> p h m q", h=4, m=2)[:, :, lo // 128:, :]
                        ins = act.activation(v(prT[:, n % 2, :]), v(tp[:, :]), ACT.Copy)
                    elif kind == "swin":
                        act.activation(prT[:, n % 2, 0:P], tp[:, 0:P], ACT.Copy)
                        ins = act.activation(prT[0:NSMP, n % 2, P:2 * P], tp[0:NSMP, P:2 * P], ACT.Copy)
                    else:
                        ins = act.activation(prT[:, n % 2, 0:2 * P], tp[:, 0:2 * P], ACT.Copy)
                    ins.then_inc(s_te, 1)

                def values_out(n):
                    kind, i = units[n]
                    act.wait_ge(s_ov, n + 1)
                    base = 6 if "mem" in kind else 4
                    r = ROWS[i]
                    o = ov[:, n % 2, 0:256].rearrange("p (c q) -> p c q", c=2)
                    act.activation(K.mixed[:, i, base:base + 2, 0:r], o[:, :, 0:r], ACT.Copy).then_inc(s_oe, 1)

                for n in range(8):
                    act.wait_ge(s_wt, n + 1)
                    act.activation(WT[:, n // 4, (n % 4) * 4:(n % 4) * 4 + 4, :],
                                   pp[:, n, :].rearrange("p (g j) -> p g j", j=P), ACT.Copy).then_inc(s_we, 1)
                for n in range(8):
                    act.wait_ge(s_kt, n + 1)
                    act.activation(ZK[0:C, :, (CH - 1) * C:].rearrange("p (a m e) x -> p a e m x", m=4, e=2)[:, n // 2, n % 2, :, :],
                                   pp[0:C, n, :].rearrange("p (g j) -> p g j", j=P), ACT.Copy).then_inc(s_ke, 1)
                for n, gs in enumerate(ub):
                    act.wait_ge(s_ut, n + 1)
                    k = len(gs)
                    act.activation(U[:, gs[0]:gs[0] + k, :], pp[:, n, 0:k * NC].rearrange("p (g j) -> p g j", j=NC),
                                   ACT.Copy).then_inc(s_ue, 1)
                for n, gs in enumerate(vb):
                    act.wait_ge(s_vm, n + 1)
                    k = len(gs)
                    act.activation(V[:, :, gs[0]:gs[0] + k, :].rearrange("p r g j -> p g r j"),
                                   pp[:, n, 0:k * 2 * NC].rearrange("p (g r j) -> p g r j", r=2, j=NC),
                                   ACT.Copy).then_inc(s_ve, 1)
                exps(0)
                exps(1)
                turned(0)
                for n in range(NU):
                    if n + 1 < NU:
                        turned(n + 1)
                    values_out(n)
                    if n + 2 < NU:
                        exps(n + 2)
                for n in range(8):
                    act.wait_ge(s_ym, n + 1)
                    act.activation(K.y[0:COLS, :, :].rearrange("p t (a m e c) -> p a e m t c", m=4, e=2, c=C)[:, n // 2, n % 2, :, :, :],
                                   pp[0:COLS, n, :].rearrange("p (g t c) -> p g t c", t=CH, c=C), ACT.Gelu).then_inc(s_ye, 1)


def gate(nc, d, K):
    with Stage(nc, "gate") as S:
        wg = K.wg
        bg = S.sb("bg", [P, 4])
        yT = S.sb("yT", [P, 4, CH, COLS])
        sg = S.sb("sg", [P, 2, 4, COLS])
        pq = S.ps("pq", [P, 4, 512])

        s_in = S.sem("glu_landed")
        s_yt = S.sem("y_turned")
        s_ye = S.sem("y_out")
        s_gm = S.sem("glu_summed")
        s_sg = S.sem("sigmoids")
        s_gl = S.sem("glu_done")

        with S.block() as block:
            @block.sync
            def _(sp):
                sp.dma_start(bg[:, :], d["b_glu"]).then_inc(s_in, 16)
                sp.dma_start(K.wo[:, :, :], d["w_out"]).then_inc(K.s_wo, 16)
                sp.dma_start(K.x[0:NSMP, 4, :], d["x_tok"][SEQ:T, :]).then_inc(K.s_small, 16)
                sp.dma_start(K.g2[:, :], d["g2"]).then_inc(K.s_small, 16)
                sp.dma_start(K.keys[:, :, :], d["keys"]).then_inc(K.s_small, 16)
                sp.dma_start(K.iota[:, :], d["iota"]).then_inc(K.s_small, 16)
                sp.dma_start(K.ident4[:, :], d["ident4"]).then_inc(K.s_small, 16)
                sp.dma_start(K.x[:, 0:4, :], d["x_tok"][0:SEQ, :].rearrange("(i p) n -> p i n", p=P)).then_inc(K.s_x, 16)

            @block.tensor
            def _(pe):
                for n in range(8):
                    kc, th = n // 2, n % 2
                    if n >= 4:
                        pe.wait_ge(s_ye, n - 3)
                    for t in range(4):
                        mm = pe.transpose(pq[:, n % 4, t * COLS:(t + 1) * COLS],
                                          K.y[0:COLS, th * 4 + t, kc * P:(kc + 1) * P], K.ident[:COLS, :COLS])
                    mm.then_inc(s_yt, 1)
                pe.wait_ge(K.s_wg, 16)
                pe.wait_ge(s_ye, 8)
                for n in range(8):
                    co, th = n // 2, n % 2
                    if n >= 4:
                        pe.wait_ge(s_sg, n - 3)
                    for kc in range(4):
                        mm = pe.matmul(pq[:, n % 4, 0:4 * COLS], wg[:, kc, co * P:(co + 1) * P],
                                       yT[:, kc, th * 4:(th + 1) * 4, :], start=(kc == 0), stop=(kc == 3))
                    mm.then_inc(s_gm, 1)

            @block.scalar
            def _(act):
                for n in range(8):
                    kc, th = n // 2, n % 2
                    act.wait_ge(s_yt, n + 1)
                    act.activation(yT[:, kc, th * 4:(th + 1) * 4, :], pq[:, n % 4, 0:4 * COLS].rearrange("p (t j) -> p t j", j=COLS),
                                   ACT.Copy).then_inc(s_ye, 1)
                act.wait_ge(s_in, 16)
                for n in range(8):
                    co = n // 2
                    act.wait_ge(s_gm, n + 1)
                    if n >= 2:
                        act.wait_ge(s_gl, n - 1)
                    act.activation(sg[:, n % 2, :, :], pq[:, n % 4, 0:4 * COLS].rearrange("p (t j) -> p t j", j=COLS),
                                   ACT.Sigmoid, bias=bg[:, co:co + 1]).then_inc(s_sg, 1)

            @block.vector
            def _(dve):
                NI = P // CH
                for n in range(8):
                    co, th = n // 2, n % 2
                    t = slice(th * 4, th * 4 + 4)
                    dve.wait_ge(s_sg, n + 1)
                    for i in range(4):
                        prompt = K.mixed[:, i, co, :].rearrange("p (j t) -> p t j", t=CH)[:, t, :]
                        j = slice(i * NI, (i + 1) * NI)
                        ins = dve.tensor_tensor(prompt, yT[:, co, t, j], sg[:, n % 2, :, j], ALU.mult)
                    if th == 0:
                        smp = K.mixed[:, 4, co, 0:NSMP].rearrange("p (b t) -> p t b", t=DSEQ)
                        ins = dve.tensor_tensor(smp, yT[:, co, 0:DSEQ, NJ:COLS], sg[:, n % 2, :, NJ:COLS], ALU.mult)
                    ins.then_inc(s_gl, 1)


def experts(nc, d, K):
    with Stage(nc, "peer") as S:
        RU, RV, RD = 7, 8, 4
        GRP = TOPK
        order = [4, 0, 1, 2, 3]
        count = [SLOTS // 4 if i == 4 else SLOTS for i in order]
        first = [sum(count[:k]) for k in range(NT + 1)]
        steps = [(k, s) for k in range(NT) for s in range(count[k])]
        NS, NG = len(steps), len(steps) // GRP
        NH2 = 2 * PH
        U = S.sb("U", [P, RU, D])
        V, wo, g2, keys, iotaf, ident4 = K.V, K.wo, K.g2, K.keys, K.iota, K.ident4
        dg = S.sb("dg", [P, RD, P])
        a = S.sb("a", [P, 2, GRP])
        ga = S.sb("ga", [P, 2, GRP])
        wt = S.sb("wt", [P, 2, GRP])
        xs = S.sb("xs", [P, D])
        es = S.sb("es", [P, SLOTS // 4], U32)
        gs = S.sb("gs", [P, SLOTS // 4])
        held = [P if i == 4 else ROWS[i] for i in order]

        QH = PH // 4
        QS = QH * TOPK

        def part(k, b):
            return b if k == 0 else 1 + 4 * (k - 1) + b

        xnT = S.sb("xnT", [P, KD, P])
        qT = S.sb("qT", [P, NH2, P])
        iota = S.sb("iota", [P, TOPK], BF16)
        ss = S.sb("ss", [P, NT])
        rowq = S.sb("rowq", [P, 2, 4 * P])
        val = S.sb("val", [P, 4, TOPK])
        idx = S.sb("idx", [P, 4, TOPK], U32)
        idxb = S.sb("idxb", [P, 4, TOPK], BF16)
        left = S.sb("left", [P, 4, PK])
        cand = S.sb("cand", [P, QH, CAND])
        top = S.sb("top", [P, QH, TOPK])
        pos = S.sb("pos", [P, QS], U32)
        t32 = S.sb("t32", [P, QS], U32)
        f = S.sb("f", [P, 4, QS])
        rcb = S.sb("rcb", [P, 2, QS], BF16)
        hot = S.sb("hot", [P, QS, TOPK], BF16)
        ex = S.sb("ex", [P, PH, TOPK])
        dn = S.sb("dn", [P, QH])
        acc = S.ps("acc", [P, 2, 512])
        pq = S.ps("pq", [P, 2, 512])
        psc = S.ps("psc", [P, 4, 512])

        s_om = S.sem("out_summed")
        s_h = S.sem("residual")
        s_sq = S.sem("squares")
        s_std = S.sem("std")
        s_xn = S.sem("normed")
        s_xs = S.sem("sample_rows_spread")
        s_xt = S.sem("rows_turned")
        s_xe = S.sem("rows_out")
        s_rm = S.sem("queries_summed")
        s_re = S.sem("query_rows_out")
        s_qm = S.sem("queries_turned")
        s_qe = S.sem("queries_out")
        s_sc = S.sem("scores")
        s_sr = S.sem("scores_read")
        s_df = S.sem("differences")
        s_ex = S.sem("exps")
        s_id = S.sem("experts_known")
        s_gt = S.sem("gates_known")
        s_u = [S.sem(f"u_landed{n}") for n in range(RU)]
        s_v = [S.sem(f"v_landed{n}") for n in range(RV)]
        s_dot = S.sem("dots")
        s_ga = S.sem("gelus")
        s_wt = S.sem("weights")
        s_dg = S.sem("diagonals")
        s_mm = S.sem("summed")
        s_y = S.sem("result")
        s_out = S.sem("stored")
        s_ch = S.sem("dve_chain")

        LAG = 34
        WEIGH = LAG - 1
        TURN_OUT = 2
        ROWS_OUT, QTURN, QUERY_OUT, SCORE, EXPS, ROUTE, GATES = 3, 4, 7, 8, 22, 50, 62
        query = {(1, b): 8 * (b - 1) for b in range(1, 4)}
        query.update({(k, b): first[k - 1] + 6 + 8 * b for k in range(2, NT) for b in range(4)})
        ROUTE0, GATES0 = 16, 24
        RESIDUAL, LAST_NORM = (26, 30, 34), 3
        RESULT = LAG + 2

        def due(n, behind):
            return [kb for kb, at in query.items() if at + behind == n]

        out_banks = [acc[:, :, :], acc[:, :, :], acc[:, :, :], psc[:, 2:4, :], psc[:, 0:2, :]]

        with S.block() as block:
            @block.sync
            def _(sp):
                sp.wait_ge(s_xn, 1)
                for q in range(4):
                    sp.dma_start(xs[q * NSMP:(q + 1) * NSMP, :], K.xn[0:NSMP, 4, :]).then_inc(s_xs, 16)
                for k, i in enumerate(order):
                    sp.wait_ge(s_y, k + 1)
                    dst = d["y_s"] if i == 4 else d["y_p"][i * P:(i + 1) * P, :]
                    sp.dma_start(dst, K.x[:ROWS[i], i, :]).then_inc(s_out, 16)
                sp.wait_ge(s_out, 16 * NT)

            @block.gpsimd
            def _(pool):

                def rows(n):
                    k, s = steps[n]
                    return K.expert[:, order[k], s:s + 1] if k else es[:, s:s + 1]

                for n in range(NS + LAG):
                    if n < NS:
                        k, s = steps[n]
                        if s % QS == 0:
                            pool.wait_ge(s_id, part(k, s // QS) + 1)
                        if n >= RU:
                            pool.wait_ge(s_dot, n - RU + 1)
                        pool.indirect_dma_start(U[:, n % RU, :], None, d["peer_u"],
                                                bass.IndirectOffsetOnAxis(ap=rows(n), axis=0)).then_inc(s_u[n % RU], 16)
                    m = n - LAG
                    if m >= 0:
                        if m == 0:
                            pool.wait_ge(s_om, NT)
                        if m >= RV:
                            pool.wait_ge(s_mm, m - RV + 1)
                        pool.indirect_dma_start(V[:, m % RV, :], None, d["peer_v"],
                                                bass.IndirectOffsetOnAxis(ap=rows(m), axis=0)).then_inc(s_v[m % RV], 16)

            @block.vector
            def _(dve):
                step = Chain(dve, s_ch)
                tt, ts = dve.tensor_tensor, dve.tensor_scalar

                def residual(k):
                    i = order[k]
                    r = ROWS[i]
                    dve.wait_ge(s_om, k + 1)
                    dve.wait_ge(K.s_x if k else K.s_small, 16 if k else 80)
                    if k:
                        ins = tt(K.x[:r, i, :], K.x[:r, i, :], out_banks[k].rearrange("p a b -> p (a b)"), ALU.add)
                    else:
                        for q in range(4):
                            c = K.x[0:NSMP, 4, q * D // 4:(q + 1) * D // 4]
                            ins = tt(c, c, acc[q * NSMP:(q + 1) * NSMP, 0, 0:D // 4], ALU.add)
                    ins.then_inc(s_h, 1)
                    dve.wait_ge(s_std, k + 1)
                    step(dve.reciprocal(ss[:r, i:i + 1], ss[:r, i:i + 1]))
                    dve.scalar_tensor_tensor(K.xn[:r, i, :], K.x[:r, i, :], ss[:r, i:i + 1], g2[:r, :], ALU.mult,
                                             ALU.mult).then_inc(s_xn, 1)

                def best(k, b):
                    r = held[k]
                    n = part(k, b)
                    dve.wait_ge(s_sc, n + 1)
                    sc = [psc[:r, b, m * P:(m + 1) * P] for m in range(4)]
                    for m in range(4):
                        ins = dve.max(val[:r, m, 0:8], sc[m])
                    step(ins)
                    for m in range(4):
                        dve.max_index(idx[:r, m, 0:8], val[:r, m, 0:8], sc[m])
                        ins = dve.match_replace(left[:r, m, :], val[:r, m, 0:8], sc[m], -BIG)
                    ins.then_inc(s_sr, 1)
                    dve.wait_ge(s_sr, n + 1)
                    for m in range(4):
                        ins = dve.max(val[:r, m, 8:16], left[:r, m, :])
                    step(ins)
                    for m in range(4):
                        ins = dve.max_index(idx[:r, m, 8:16], val[:r, m, 8:16], left[:r, m, :])
                    step(ins)

                def sums(k, b):
                    r, H = held[k], QH
                    v = val[:r, 0:2 * H, :].rearrange("p (h e) k -> p h e k", e=2)
                    v1, v2 = v[:, :, 0, :], v[:, :, 1, :]
                    tt(cand[:r, 0:H, 0:16], v2, v1[:, :, 0:1].broadcast_to([r, H, 16]), ALU.add)
                    tt(cand[:r, 0:H, 16:72].rearrange("p h (a b) -> p h a b", b=8), widen(v1[:, :, 1:8], 3, 8),
                       widen(v2[:, :, 0:8], 2, 7), ALU.add)
                    tt(cand[:r, 0:H, 72:80], v1[:, :, 8:16], v2[:, :, 0:1].broadcast_to([r, H, 8]), ALU.add)
                    step(dve.tensor_copy(idxb[:r, 0:2 * H, :], idx[:r, 0:2 * H, :]))
                    p8 = pos[:r, :].rearrange("p (h k) -> p h k", k=TOPK)
                    for h in range(H):
                        ins = dve.max(top[:r, h, 0:8], cand[:r, h, :])
                    step(ins)
                    for h in range(H):
                        dve.max_index(p8[:, h, 0:8], top[:r, h, 0:8], cand[:r, h, :])
                        ins = dve.match_replace(left[:r, h, 0:CAND], top[:r, h, 0:8], cand[:r, h, :], -BIG)
                    step(ins)
                    for h in range(H):
                        ins = dve.max(top[:r, h, 8:16], left[:r, h, 0:CAND])
                    step(ins)
                    for h in range(H):
                        ins = dve.max_index(p8[:, h, 8:16], top[:r, h, 8:16], left[:r, h, 0:CAND])
                    step(ins)
                    tt(ex[:r, b * H:(b + 1) * H, :], top[:r, 0:H, :], top[:r, 0:H, 0:1].broadcast_to([r, H, TOPK]), ALU.subtract).then_inc(s_df, 1)

                def numbers(k, b):
                    r, H, n = held[k], QH, QS
                    F = [f[:r, m, 0:n] for m in range(4)]
                    dve.tensor_copy(F[0], pos[:r, 0:n])
                    step(ts(t32[:r, 0:n], pos[:r, 0:n], 56.0, None, ALU.add))
                    step(ts(t32[:r, 0:n], t32[:r, 0:n], 3, None, ALU.logical_shift_right))
                    step(dve.tensor_copy(F[1], t32[:r, 0:n]))
                    step(ts(F[1], F[1], -8.0, 0.0, ALU.add, ALU.max))
                    step(dve.scalar_tensor_tensor(F[1], F[0], -64.0, F[1], ALU.add, ALU.max))
                    ts(F[2], F[1], 1.0, 8.0, ALU.min, ALU.mult)
                    step(dve.scalar_tensor_tensor(F[3], F[1], -8.0, F[0], ALU.mult, ALU.add))
                    step(tt(F[3], F[3], F[2], ALU.subtract))
                    dve.tensor_copy(rcb[:r, 0, 0:n], F[1])
                    step(ts(rcb[:r, 1, 0:n], F[3], 0.0, None, ALU.max))
                    ib = idxb[:r, 0:2 * H, :].rearrange("p (h e) k -> p h e k", e=2)
                    for e in range(2):
                        step(tt(hot[:r, 0:n, :], widen(rcb[:r, e, 0:n], 2, TOPK), widen(iota[:r, :], 1, n), ALU.is_equal))
                        h4 = hot[:r, 0:n, :].rearrange("p (h k) j -> p h k j", k=TOPK)
                        step(tt(h4, h4, widen(ib[:, :, e, :], 2, TOPK), ALU.mult))
                        step(dve.tensor_reduce(F[e], hot[:r, 0:n, :], AX.X, ALU.add))
                    dve.scalar_tensor_tensor(K.expert[:r, order[k], b * n:(b + 1) * n] if k else es[:, :], F[0], float(PK), F[1], ALU.mult, ALU.add).then_inc(s_id, 1)

                def gates(k, b):
                    r, H = held[k], QH
                    e = ex[:r, b * H:(b + 1) * H, :]
                    gate = K.gate[:r, order[k], b * QS:(b + 1) * QS] if k else gs[:, :]
                    dve.wait_ge(s_ex, part(k, b) + 1)
                    step(dve.tensor_reduce(dn[:r, 0:H], e, AX.X, ALU.add))
                    step(dve.reciprocal(dn[:r, 0:H], dn[:r, 0:H]))
                    tt(gate.rearrange("p (h k) -> p h k", k=TOPK), e, widen(dn[:r, 0:H], 2, TOPK),
                       ALU.mult).then_inc(s_gt, 1)

                def route(k, b):
                    best(k, b)
                    sums(k, b)
                    numbers(k, b)

                def weights(g):
                    k, s = steps[g * GRP]
                    dve.wait_ge(s_gt, part(k, s // QS) + 1)
                    gate = K.gate[:, order[k], s:s + GRP] if k else gs[:, s:s + GRP]
                    dve.wait_ge(s_ga, g + 1)
                    if g >= 2:
                        dve.wait_ge(s_dg, GRP * (g - 1))
                    tt(wt[:, g % 2, :], ga[:, g % 2, :], gate, ALU.mult).then_inc(s_wt, 1)

                def result(k):
                    i = order[k]
                    r = ROWS[i]
                    dve.wait_ge(s_mm, first[k + 1])
                    tt(K.x[:r, i, :], K.x[:r, i, :], acc[:r, :, :].rearrange("p a b -> p (a b)"), ALU.add).then_inc(s_y, 1)

                residual(0)
                step(dve.tensor_copy(iota[:, :], iotaf[:, :]))
                route(0, 0)
                gates(0, 0)
                residual(1)
                dve.wait_ge(s_xs, 64)
                for n in range(NS):
                    k, s = steps[n]
                    g = n // GRP
                    if n % GRP == 0 and g >= 2:
                        dve.wait_ge(s_ga, g - 1)
                    if n >= WEIGH and (n - WEIGH) % GRP == 0:
                        weights((n - WEIGH) // GRP)
                    if n in RESIDUAL:
                        residual(2 + RESIDUAL.index(n))
                    if n == GATES0:
                        gates(1, 0)
                    for kb in due(n, GATES):
                        gates(*kb)
                    if k and s == RESULT:
                        result(k - 1)
                    if n == ROUTE0:
                        route(1, 0)
                    for kb in due(n, ROUTE):
                        route(*kb)
                    dve.wait_ge(s_u[n % RU], 16 * (n // RU + 1))
                    x = K.xn[:, order[k], :] if k else xs[:, :]
                    dve.tensor_tensor_reduce(U[:, n % RU, :], U[:, n % RU, :], x, 1.0, 0.0, ALU.mult, ALU.add,
                                             a[:, g % 2, n % GRP:n % GRP + 1]).then_inc(s_dot, 1)
                for g in range((NS - 1 - WEIGH) // GRP + 1, NG):
                    weights(g)
                result(NT - 1)

            @block.scalar
            def _(act):
                def norm(k):
                    i = order[k]
                    r = ROWS[i]
                    act.wait_ge(s_h, k + 1)
                    act.activation(K.xn[:r, i, :], K.x[:r, i, :], ACT.Square, accum_out=ss[:r, i:i + 1]).then_inc(s_sq, 1)
                    act.wait_ge(s_sq, k + 1)
                    act.activation(ss[:r, i:i + 1], ss[:r, i:i + 1], ACT.Sqrt, bias=K.eps[:r, 0:1], scale=1.0 / D).then_inc(s_std, 1)

                def rows_out(k, b):
                    r = held[k]
                    n = part(k, b)
                    act.wait_ge(s_rm, n + 1)
                    if n >= 2:
                        act.wait_ge(s_qm, n - 1)
                    act.activation(rowq[:r, n % 2, :], pq[:r, 0, :], ACT.Copy).then_inc(s_re, 1)

                def turned_out(k):
                    r = ROWS[order[k]]
                    act.wait_ge(s_xt, k + 1)
                    act.activation(xnT[:, :, 0:r], pq[:, :, :].rearrange("p a (b t) -> p (a b) t", t=P)[:, :, 0:r],
                                   ACT.Copy).then_inc(s_xe, 1)

                def queries_out(k, b):
                    r = held[k]
                    act.wait_ge(s_qm, part(k, b) + 1)
                    act.activation(qT[:, 4 * b:4 * b + 4, 0:r], pq[:, 1, :].rearrange("p (m t) -> p m t", t=P)[:, :, 0:r],
                                   ACT.Copy).then_inc(s_qe, 1)

                def exps(k, b):
                    e = ex[:held[k], b * QH:(b + 1) * QH, :]
                    act.wait_ge(s_df, part(k, b) + 1)
                    act.activation(e, e, ACT.Exp).then_inc(s_ex, 1)

                norm(0)
                turned_out(0)
                rows_out(0, 0)
                queries_out(0, 0)
                exps(0, 0)
                norm(1)
                turned_out(1)
                rows_out(1, 0)
                queries_out(1, 0)
                exps(1, 0)
                norm(2)
                norm(3)
                for n in range(NS):
                    k, s = steps[n]
                    g = n // GRP
                    if n == LAST_NORM:
                        norm(4)
                    if k and k + 1 < NT and s == TURN_OUT:
                        turned_out(k + 1)
                    for kb in due(n, ROWS_OUT):
                        rows_out(*kb)
                    for kb in due(n, QUERY_OUT):
                        queries_out(*kb)
                    for kb in due(n, EXPS):
                        exps(*kb)
                    if n % GRP == 0:
                        act.wait_ge(s_dot, GRP * (g + 1))
                        if g >= 2:
                            act.wait_ge(s_wt, g - 1)
                        act.activation(ga[:, g % 2, :], a[:, g % 2, :], ACT.Gelu).then_inc(s_ga, 1)
                        act.wait_ge(s_wt, g + 1)
                    if n >= RD:
                        act.wait_ge(s_mm, n - RD + 1)
                    dst, src = (dg[:, n % RD, :], K.ident[:, :]) if k else (dg[:, n % RD, 0:NSMP], ident4[:, :])
                    act.activation(dst, src, ACT.Copy, scale=wt[:, g % 2, n % GRP:n % GRP + 1]).then_inc(s_dg, 1)

            @block.tensor
            def _(pe):
                def turn(k):
                    i = order[k]
                    r = ROWS[i]
                    pe.wait_ge(s_xn, k + 1)
                    if k:
                        pe.wait_ge(s_qe, part(k, 0))
                    for c in range(KD):
                        mm = pe.transpose(pq[:, c // 4, (c % 4) * P:(c % 4) * P + r], K.xn[:r, i, c * P:(c + 1) * P], K.ident[:r, :r])
                    mm.then_inc(s_xt, 1)

                def sample_scores():
                    quarter = [slice(q * NSMP, (q + 1) * NSMP) for q in range(4)]
                    pe.wait_ge(s_xe, 1)
                    pe.wait_ge(K.s_wq, 16)
                    for c in range(KD):
                        for q in range(4):
                            mm = pe.matmul(pq[quarter[q], 0, :], xnT[:, c, 0:NSMP], K.wq[:, c, 4 * q * P:4 * (q + 1) * P],
                                           start=(c == 0), stop=(c == KD - 1))
                    mm.then_inc(s_rm, 1)
                    pe.wait_ge(s_re, 1)
                    for m in range(4):
                        mm = pe.transpose(pq[:, 1, m * P:(m + 1) * P], rowq[:, 0, m * P:(m + 1) * P], K.ident[:, :])
                    mm.then_inc(s_qm, 1)
                    pe.wait_ge(s_qe, 1)
                    for m in range(4):
                        for q in range(4):
                            mm = pe.matmul(psc[quarter[q], 0, m * P:(m + 1) * P], qT[:, m, quarter[q]], keys[:, m % 2, :],
                                           start=True, stop=True)
                    mm.then_inc(s_sc, 1)

                def queries(k, b):
                    r = ROWS[order[k]]
                    n = part(k, b)
                    pe.wait_ge(s_xe, k + 1)
                    pe.wait_ge(s_re, n)
                    for c in range(KD):
                        mm = pe.matmul(pq[:r, 0, :], xnT[:, c, 0:r], K.wq[:, c, 4 * b * P:4 * (b + 1) * P],
                                       start=(c == 0), stop=(c == KD - 1))
                    mm.then_inc(s_rm, 1)

                def turn_queries(k, b):
                    r = ROWS[order[k]]
                    n = part(k, b)
                    pe.wait_ge(s_re, n + 1)
                    pe.wait_ge(s_qe, n)
                    for m in range(4):
                        mm = pe.transpose(pq[:, 1, m * P:m * P + r], rowq[:r, n % 2, m * P:(m + 1) * P], K.ident[:r, :r])
                    mm.then_inc(s_qm, 1)

                def project(k):
                    i = order[k]
                    r = ROWS[i]
                    if k in (1, 2):
                        pe.wait_ge(s_h, k)
                    if k == 4:
                        pe.wait_ge(s_sr, part(1, 0) + 1)
                    for c in range(KD):
                        for e in range(2):
                            mm = pe.matmul(out_banks[k][:r, e, :], K.mixed[:, i, c, 0:r], wo[:, c, e * 512:(e + 1) * 512],
                                           start=(c == 0), stop=(c == KD - 1))
                    mm.then_inc(s_om, 1)

                def scores(k, b):
                    r = ROWS[order[k]]
                    pe.wait_ge(s_qe, part(k, b) + 1)
                    if k == 1:
                        pe.wait_ge(s_h, NT if b == 1 else NT - 1 if b else 1)
                    else:
                        pe.wait_ge(s_sr, part(k - 1, b) + 1)
                    for m in range(4):
                        hh = b * 4 + m
                        mm = pe.matmul(psc[:r, b, m * P:(m + 1) * P], qT[:, hh, 0:r], keys[:, hh % 2, :], start=True, stop=True)
                    mm.then_inc(s_sc, 1)

                pe.wait_ge(K.s_wo, 16)
                for c in range(KD):
                    for q in range(4):
                        mm = pe.matmul(acc[q * NSMP:(q + 1) * NSMP, 0, 0:D // 4], K.mixed[:, 4, c, 0:NSMP],
                                       wo[:, c, q * D // 4:(q + 1) * D // 4], start=(c == 0), stop=(c == KD - 1))
                mm.then_inc(s_om, 1)
                turn(0)
                sample_scores()
                project(1)
                turn(1)
                queries(1, 0)
                turn_queries(1, 0)
                scores(1, 0)
                for j in range(2, NT):
                    project(j)
                pe.wait_ge(s_h, 3)
                for n in range(NS):
                    k, s = steps[n]
                    r = ROWS[order[k]]
                    if k and k + 1 < NT and s == 0:
                        turn(k + 1)
                    for kb in due(n, 0):
                        queries(*kb)
                    for kb in due(n, QTURN):
                        turn_queries(*kb)
                    for kb in due(n, SCORE):
                        scores(*kb)
                    pe.wait_ge(s_dg, n + 1)
                    pe.wait_ge(s_v[n % RV], 16 * (n // RV + 1))
                    if k and s == 0:
                        pe.wait_ge(s_y, k)
                    for c in range(2):
                        mm = pe.matmul(acc[:r, c, :], dg[:, n % RD, 0:r], V[:, n % RV, c * 512:(c + 1) * 512],
                                       start=(s == 0), stop=(s == count[k] - 1))
                    mm.then_inc(s_mm, 1)


class Kept:
    pass


def build(nc, d):
    K = Kept()
    with Stage(nc, "kept") as S, Stage(nc, "rows", "right") as X:
        K.ident = S.sb("ident", [P, P])
        K.eps = S.sb("eps", [P, 1])
        K.s_wo, K.s_wq, K.s_x, K.s_small = (S.sem(n) for n in ("wout_landed", "wq_landed", "x_landed", "small_landed"))
        with Stage(nc, "tables") as B:
            K.par = B.sb("par", [P, 3, GP])
            K.bc = B.sb("bc", [P, 4, GP, C])
            K.dsk = B.sb("dsk", [C, G])
            K.s0 = B.sb("s0", [P, 2, GP, NSEQ])
            K.w = B.sb("w", [P, 24, GP])
            K.L = B.sb("L", [P, 3, CH + 1, GP])
            K.Lrev = B.sb("Lrev", [P, 2, CH, GP])
            K.bb = B.sb("bb", [P, 2, GP, C])
            K.Q = B.sb("Q", [P, 2, GP, CH + 1, C])
            K.W = B.sb("W", [P, 2, GP, CH, C])
            K.A8 = B.sb("A8", [P, 2, 2, GP])
            with Stage(nc, "heads") as H:
                K.qkT = H.sb("qkT", [P, 5, T])
                K.v = H.sb("v", [P, NT, 128])
                K.mkT = H.sb("mkT", [P, 2, MEM])
                K.mv = H.sb("mv", [P, 2, 256])
                project(nc, d, K)
                K.xn = X.sb("xn", [P, NT, D])
                K.mixed = K.xn[:, :, :].rearrange("p i (k t) -> p i k t", t=P)
                K.wq = X.sb("wq", [P, KD, PH * 256])
                Y = Stage(nc, "y", "right")
                Y.__enter__()
                K.y = Y.sb("y", [P, CH, UW])
                K.wg = Y.sb("wg", [P, 5, 512])
                K.s_wg = S.sem("wglu_landed")
                blend(nc, d, K)
        K.x = S.sb("x", [P, NT, D])
        K.expert = S.sb("expert", [P, NT - 1, SLOTS], U32)
        K.gate = S.sb("gate", [P, NT - 1, SLOTS])
        K.V = S.sb("V", [P, 8, D])
        K.wo = K.V
        K.g2 = S.sb("g2", [P, D])
        K.keys = S.sb("keys", [P, 2, PK])
        K.iota = S.sb("iota", [P, TOPK])
        K.ident4 = S.sb("ident4", [P, NSMP])
        gate(nc, d, K)
        Y.__exit__(None, None, None)
        experts(nc, d, K)


def constants():
    half = HD // 2
    inv = (10000.0 ** (-np.arange(half, dtype=np.float32) / half)).astype(np.float32)
    pos = np.concatenate([np.arange(SEQ), np.tile(2048 + np.arange(DSEQ), NSEQ)]).astype(np.float32)
    ang = pos[:, None] * inv[None, :]
    rope = np.zeros((P, NT, 2, HD), np.float32)
    for i in range(NT):
        a = ang[i * P:i * P + ROWS[i]]
        rope[:ROWS[i], i, 0] = np.concatenate([np.cos(a), np.cos(a)], 1)
        rope[:ROWS[i], i, 1] = np.concatenate([np.sin(a), np.sin(a)], 1)
    q, k = np.arange(P)[:, None], np.arange(256)[None, :] - 128
    mask = np.where((q - k >= 0) & (q - k < WIN), 0.0, -BIG).astype(np.float32)
    row = np.arange(P) % NSMP
    rb, rq = (row // DSEQ)[:, None], (row % DSEQ)[:, None]
    kb, kw = np.arange(NSEQ * WIN)[None, :] // WIN, np.arange(NSEQ * WIN)[None, :] % WIN
    old = np.where((rb == kb) & (kw > rq), 0.0, -BIG)
    nb, ns = np.arange(NSMP)[None, :] // DSEQ, np.arange(NSMP)[None, :] % DSEQ
    new = np.where((rb == nb) & (ns <= rq), 0.0, -BIG)
    return {
        "rope": rope,
        "mask": mask,
        "smask": np.concatenate([old, new], 1).astype(np.float32),
        "bmask": np.where(rb == np.arange(NSEQ)[None, :], 0.0, -BIG).astype(np.float32),
        "iota": np.tile(np.arange(TOPK, dtype=np.float32), (P, 1)),
        "ident": np.eye(P, dtype=np.float32),
        "ident4": np.tile(np.eye(NSMP, dtype=np.float32), (4, 1)),
    }


def layouts(i):
    A = {k: np.asarray(v) for k, v in i.items()}

    def chunked(w):
        return w.reshape(w.shape[0] // P, P, -1).transpose(1, 0, 2)

    x = np.concatenate([A["x_prompt"].reshape(SEQ, D), A["x_sample"].reshape(NSMP, D)])
    mem = A["mem_prompt"].reshape(MEM, D)
    w = A["w_in"][0]
    q = w[:, 512:768].reshape(D, 2, 2, HD).transpose(0, 2, 1, 3).reshape(D, 256)
    w = np.concatenate([w[:, :512], q, w[:, 768:896], w[:, 1024:1280], w[:, 896:1024]], 1)
    pair = lambda a: a.reshape(GP, 2, N).transpose(1, 2, 0).reshape(P, GP)
    pairc = lambda a: a.reshape(GP, 2, N, C).transpose(1, 2, 0, 3).reshape(P, GP, C)
    pairs = lambda a: a.reshape(NSEQ, GP, 2, N).transpose(2, 3, 1, 0).reshape(P, GP, NSEQ)
    cT = lambda a: a[0].transpose(0, 2, 1)
    sink = A["swa_sinks"][0].reshape(2, 2).T.reshape(4)
    ck, cv = A["cache_win_k"][0], A["cache_win_v"][0]
    mk, mv = A["cache_mem_k"][0], A["cache_mem_v"][0]
    gains = np.concatenate([np.tile(A["swa_q_norm"], (4, 1)), np.tile(A["swa_k_norm"], (2, 1)),
                            np.tile(A["mem_q_norm"], (4, 1)), np.tile(A["mem_k_norm"], (4, 1))])
    out = {
        "x_tok": x,
        "xT": chunked(x.T),
        "memT": chunked(mem.T),
        "mem_tok": mem.reshape(2, P, D).transpose(1, 0, 2),
        "w_in": chunked(w),
        "w_mem": chunked(A["w_mem_kv"][0]),
        "g1T": np.stack([A["norm1_g"][0].reshape(KD, P).T, A["mem_norm_g"][0].reshape(KD, P).T], 1),
        "gains": np.broadcast_to(gains, (P,) + gains.shape),
        "sinks": np.concatenate([np.broadcast_to(A["swa_sinks"][0], (P, 4)), np.repeat(sink, NSMP)[:, None]], 1),
        "cache_k": ck.reshape(NSEQ, WIN, 128),
        "cache_v": cv.reshape(NSEQ, WIN, 128),
        "kcT": ck.transpose(2, 3, 0, 1).reshape(P, NSEQ, WIN),
        "vc": cv.transpose(1, 0, 2, 3).reshape(P, NSEQ, 128),
        "mcT": mk.reshape(NSEQ, MEM, 2, 2, HD).transpose(3, 4, 2, 0, 1).reshape(P, 2, NSEQ, MEM),
        "mcv": mv.reshape(NSEQ, 2, P, 256).transpose(2, 1, 0, 3),
        "ssm_par": np.stack([pair(A["ssm_log_dt"][0]), pair(A["ssm_a_re"][0]), pair(A["ssm_a_im"][0])], 1),
        "ssm_bc": np.stack([pairc(A["ssm_b_re"][0]), pairc(A["ssm_b_im"][0]), pairc(cT(A["ssm_c_re"])),
                            pairc(cT(A["ssm_c_im"]))], 1),
        "ssm_d": A["ssm_d"][0].T,
        "ssm_s0": np.stack([pairs(A["state_ssm_re"][0]), pairs(A["state_ssm_im"][0])], 1),
        "w_glu": chunked(A["w_glu"][0]),
        "b_glu": A["b_glu"][0].reshape(4, P).T,
        "w_out": chunked(A["w_out"][0]),
        "g2": np.broadcast_to(A["norm2_g"][0], (P, D)),
        "wq": chunked(A["peer_wq"][0]),
        "keys": np.stack([A["peer_k1"][0].T, A["peer_k2"][0].T], 1),
        "peer_u": A["peer_u"][0],
        "peer_v": A["peer_v"][0],
    }
    out.update(constants())
    return {k: np.ascontiguousarray(v) for k, v in out.items()}


OUTS = {
    "y_p": (SEQ, D), "y_s": (NSMP, D), "p_ssm": (P, 2, GP), "s_ssm": (P, 2, GP, NSEQ),
    "p_win_k": (WIN, 128), "p_win_v": (WIN, 128), "p_mem_k": (MEM, 256), "p_mem_v": (MEM, 256),
    "s_win_k": (NSEQ, WIN, 128), "s_win_v": (NSEQ, WIN, 128),
}


def program(nc, arrays):
    d = {k: nc.dram_tensor(k, v.shape, mybir.dt.from_np(v.dtype), kind="ExternalInput").ap() for k, v in arrays.items()}
    for k, shape in OUTS.items():
        d[k] = nc.dram_tensor("out_" + k, shape, F32, kind="ExternalOutput").ap()
    d["u_scratch"] = nc.dram_tensor("u_scratch", (T, UW), F32, kind="Internal").ap()
    build(nc, d)


def returned(r):
    ps, ss = r["p_ssm"], r["s_ssm"]
    back = lambda a: a.reshape(2, N, GP).transpose(2, 0, 1).reshape(1, 1, G, N)
    backs = lambda a: a.reshape(2, N, GP, NSEQ).transpose(3, 2, 0, 1).reshape(1, NSEQ, G, N)
    return (r["y_p"].reshape(1, SEQ, D), r["y_s"].reshape(NSEQ, DSEQ, D),
            back(ps[:, 0]), back(ps[:, 1]),
            r["p_win_k"].reshape(1, 1, WIN, 2, HD), r["p_win_v"].reshape(1, 1, WIN, 2, HD),
            r["p_mem_k"].reshape(1, 1, MEM, 4, HD), r["p_mem_v"].reshape(1, 1, MEM, 4, HD),
            backs(ss[:, 0]), backs(ss[:, 1]),
            r["s_win_k"].reshape(1, NSEQ, WIN, 2, HD), r["s_win_v"].reshape(1, NSEQ, WIN, 2, HD))


def kernel(**inputs):
    import concourse.bacc as bacc
    from concourse.bass_utils import run_bass_kernel_spmd

    nc = bacc.Bacc("TRN2", target_bir_lowering=False, num_devices=1)
    arrays = layouts(inputs)
    program(nc, arrays)
    r = run_bass_kernel_spmd(nc, [arrays], core_ids=[0]).results[0]
    return returned({k: np.asarray(r["out_" + k]) for k in OUTS})
```
